# Optimizing a Trainium2 kernel written in Bass

```python
import jax, jax.numpy as jnp
from jax import lax
import numpy as np

D_MODEL = 1024
BATCH = 1
SEQ = 512
DEPTH = 1

MEM_LEN = 256
HG_HEADS = 4
HG_KEY_DIM = 128
HG_VAL_DIM = 128
HG_KW = HG_HEADS * HG_KEY_DIM
HG_VW = HG_HEADS * HG_VAL_DIM
HG_CHUNK = 64
ATT_Q_HEADS = 8
ATT_KV_HEADS = 2
ATT_GROUP = ATT_Q_HEADS // ATT_KV_HEADS
ATT_HEAD_DIM = 64
ATT_QW = ATT_Q_HEADS * ATT_HEAD_DIM
ATT_KVW = ATT_KV_HEADS * ATT_HEAD_DIM
WINDOW = 128
ATT_BLOCK = 128
ROPE_THETA = 500000.0
ROT_DIM = ATT_HEAD_DIM // 4
MEM_HEADS = 4
MEM_HEAD_DIM = D_MODEL // MEM_HEADS
D_FF = 2816
CONV_WIDTH = 3
NORM_EPS = 1e-6
IN_SPLITS = (HG_KW, HG_KW, HG_KW, HG_VW, HG_VW, ATT_QW, ATT_KVW, ATT_KVW, D_MODEL, D_MODEL)
IN_COLS = sum(IN_SPLITS)
SPLIT_IDX = [int(c) for c in np.cumsum(IN_SPLITS)[:-1]]


def rms_norm(x, g):
    xf = x.astype(jnp.float32)
    y = xf * lax.rsqrt(jnp.mean(xf * xf, axis=-1, keepdims=True) + NORM_EPS) * g.astype(jnp.float32)
    return y.astype(x.dtype)

def partial_rotary(t, positions):
    half = ROT_DIM // 2
    inv_freq = 1.0 / (ROPE_THETA ** (jnp.arange(0, ROT_DIM, 2, dtype=jnp.float32) / ROT_DIM))
    ang = positions.astype(jnp.float32)[..., None] * inv_freq
    cos, sin = jnp.cos(ang)[:, :, None, :], jnp.sin(ang)[:, :, None, :]
    tf = t.astype(jnp.float32)
    t1, t2 = tf[..., :half], tf[..., half:ROT_DIM]
    out = jnp.concatenate([t1 * cos - t2 * sin, t2 * cos + t1 * sin, tf[..., ROT_DIM:]], axis=-1)
    return out.astype(t.dtype)

def gla_chunkwise(q, k, log_f, v):
    B, S, H, K = q.shape
    V = v.shape[-1]
    n_chunks = S // HG_CHUNK

    def chunks(t):
        return t.reshape(B, n_chunks, HG_CHUNK, H, t.shape[-1]).transpose(1, 0, 3, 2, 4)

    incl = jnp.tril(jnp.ones((HG_CHUNK, HG_CHUNK), dtype=bool))[:, :, None]

    def step(state, inp):
        qc, kc, gc, vc = inp
        b = jnp.cumsum(gc, axis=2)
        o_inter = jnp.einsum('bhtk,bhkv->bhtv', qc * jnp.exp(b), state)
        decay = jnp.exp(jnp.where(incl, b[:, :, :, None, :] - b[:, :, None, :, :], -jnp.inf))
        scores = jnp.einsum('bhtk,bhtsk->bhts', qc, decay * kc[:, :, None, :, :])
        o_intra = jnp.einsum('bhts,bhsv->bhtv', scores, vc)
        b_end = b[:, :, -1, :]
        new_state = (jnp.exp(b_end)[..., None] * state
                     + jnp.einsum('bhsk,bhsv->bhkv', kc * jnp.exp(b_end[:, :, None, :] - b), vc))
        return new_state, o_inter + o_intra

    state0 = jnp.zeros((B, H, K, V), jnp.float32)
    _, o = lax.scan(step, state0, (chunks(q), chunks(k), chunks(log_f), chunks(v)))
    return o.transpose(1, 0, 3, 2, 4).reshape(B, S, H, V)

def window_gqa_sink(q, k, v, sink):
    B, S = q.shape[0], q.shape[1]
    nb = S // ATT_BLOCK
    qb = q.reshape(B, nb, ATT_BLOCK, ATT_KV_HEADS, ATT_GROUP, ATT_HEAD_DIM)

    def band(t):
        tp = jnp.pad(t.reshape(B, nb, ATT_BLOCK, ATT_KV_HEADS, ATT_HEAD_DIM),
                     ((0, 0), (1, 1), (0, 0), (0, 0), (0, 0)))
        return jnp.concatenate([tp[:, :-2], tp[:, 1:-1], tp[:, 2:]], axis=2)

    kb, vb = band(k), band(v)
    s = jnp.einsum('bnqhgd,bnkhd->bnhgqk', qb, kb).astype(jnp.float32) * (ATT_HEAD_DIM ** -0.5)
    blk = jnp.arange(nb)[:, None, None]
    qi = blk * ATT_BLOCK + jnp.arange(ATT_BLOCK)[None, :, None]
    kj = (blk - 1) * ATT_BLOCK + jnp.arange(3 * ATT_BLOCK)[None, None, :]
    valid = (jnp.abs(qi - kj) <= WINDOW) & (kj >= 0) & (kj < S)
    s = jnp.where(valid[None, :, None, None], s, -jnp.inf)
    sk = sink.astype(jnp.float32).reshape(ATT_KV_HEADS, ATT_GROUP)[None, None, :, :, None, None]
    m = jnp.maximum(jnp.max(s, axis=-1, keepdims=True), sk)
    p = jnp.exp(s - m)
    p = p / (jnp.sum(p, axis=-1, keepdims=True) + jnp.exp(sk - m))
    o = jnp.einsum('bnhgqk,bnkhd->bnqhgd', p.astype(v.dtype), vb)
    return o.reshape(B, S, ATT_QW)

def token_mixers(n, positions, w_in, lb_fwd, lb_bwd, hg_norm, sink, w_br_rec, w_br_att, w_out):
    B, S, _ = n.shape
    f32 = jnp.float32
    proj = n @ w_in
    q_r, fz_f, fz_b, i_r, g_r, q_a, k_a, v_a, gate_r, gate_a = jnp.split(proj, SPLIT_IDX, axis=-1)

    qh = jax.nn.silu(q_r.astype(f32)).reshape(B, S, HG_HEADS, HG_KEY_DIM) * (HG_KEY_DIM ** -0.5)
    vh = i_r.astype(f32).reshape(B, S, HG_HEADS, HG_VAL_DIM)

    def forget(z, lb):
        f = lb + (1.0 - lb) * jax.nn.sigmoid(z.astype(f32))
        return ((1.0 - f).reshape(B, S, HG_HEADS, HG_KEY_DIM),
                jnp.log(f).reshape(B, S, HG_HEADS, HG_KEY_DIM))

    k_f, lf_f = forget(fz_f, lb_fwd)
    k_b, lf_b = forget(fz_b, lb_bwd)
    o_f = gla_chunkwise(qh, k_f, lf_f, vh)
    o_b = gla_chunkwise(qh[:, ::-1], k_b[:, ::-1], lf_b[:, ::-1], vh[:, ::-1])[:, ::-1]
    o = o_f + o_b
    o = (o * lax.rsqrt(jnp.mean(o * o, axis=-1, keepdims=True) + NORM_EPS)
         * hg_norm.astype(f32).reshape(HG_HEADS, HG_VAL_DIM))
    o = o.reshape(B, S, HG_VW) * jax.nn.silu(g_r.astype(f32))
    y_rec = o.astype(n.dtype) @ w_br_rec

    qa = partial_rotary(q_a.reshape(B, S, ATT_Q_HEADS, ATT_HEAD_DIM), positions)
    ka = partial_rotary(k_a.reshape(B, S, ATT_KV_HEADS, ATT_HEAD_DIM), positions)
    va = v_a.reshape(B, S, ATT_KV_HEADS, ATT_HEAD_DIM)
    y_att = window_gqa_sink(qa, ka, va, sink) @ w_br_att

    merged = jax.nn.sigmoid(gate_r) * y_rec + jax.nn.sigmoid(gate_a) * y_att
    return merged @ w_out

def memory_cross_attention(n, mem_n, w_q, w_kv, w_o):
    B, S, _ = n.shape
    M = mem_n.shape[1]
    q = (n @ w_q).reshape(B, S, MEM_HEADS, MEM_HEAD_DIM)
    k, v = jnp.split(mem_n @ w_kv, 2, axis=-1)
    k = k.reshape(B, M, MEM_HEADS, MEM_HEAD_DIM)
    v = v.reshape(B, M, MEM_HEADS, MEM_HEAD_DIM)
    s = jnp.einsum('bshd,bmhd->bhsm', q, k).astype(jnp.float32) * (MEM_HEAD_DIM ** -0.5)
    p = jax.nn.softmax(s, axis=-1).astype(v.dtype)
    o = jnp.einsum('bhsm,bmhd->bshd', p, v).reshape(B, S, D_MODEL)
    return o @ w_o

def conv_ffn(n, w_up, conv_w, conv_b, w_down):
    S = n.shape[1]
    u, g = jnp.split(n @ w_up, 2, axis=-1)
    pad = CONV_WIDTH // 2
    gp = jnp.pad(g, ((0, 0), (pad, pad), (0, 0)))
    gc = sum(gp[:, j:j + S] * conv_w[j] for j in range(CONV_WIDTH)) + conv_b
    return (jax.nn.silu(gc) * u) @ w_down

def first_inputs(seed: int = 0) -> dict:
    key = jax.random.key(seed)
    ks = jax.random.split(key, 24)

    def nrm(k, shape, scale):
        return jax.random.normal(k, shape, jnp.float32) * scale

    def gain(k, shape):
        return 1.0 + 0.02 * jax.random.normal(k, shape, jnp.float32)

    L, D = DEPTH, D_MODEL
    return {
        'x': nrm(ks[0], (BATCH, SEQ, D), 1.0),
        'mem': nrm(ks[1], (BATCH, MEM_LEN, D), 1.0),
        'positions': jnp.broadcast_to(jnp.arange(SEQ, dtype=jnp.int32), (BATCH, SEQ)),
        'norm_mix': gain(ks[2], (L, D)),
        'w_in': nrm(ks[3], (L, D, IN_COLS), D ** -0.5),
        'lower_bounds': nrm(ks[4], (2, L + 1, HG_KW), 0.5),
        'hg_norm': gain(ks[5], (L, HG_VW)),
        'attn_sink': nrm(ks[6], (L, ATT_Q_HEADS), 0.5),
        'w_br_rec': nrm(ks[7], (L, HG_VW, D), HG_VW ** -0.5),
        'w_br_att': nrm(ks[8], (L, ATT_QW, D), ATT_QW ** -0.5),
        'w_mix_out': nrm(ks[9], (L, D, D), D ** -0.5),
        'norm_mem': gain(ks[10], (L, D)),
        'norm_mem_kv': gain(ks[11], (L, D)),
        'w_mem_q': nrm(ks[12], (L, D, D), D ** -0.5),
        'w_mem_kv': nrm(ks[13], (L, D, 2 * D), D ** -0.5),
        'w_mem_o': nrm(ks[14], (L, D, D), D ** -0.5),
        'norm_ffn': gain(ks[15], (L, D)),
        'w_up': nrm(ks[16], (L, D, 2 * D_FF), D ** -0.5),
        'conv_w': nrm(ks[17], (L, CONV_WIDTH, D_FF), CONV_WIDTH ** -0.5),
        'conv_b': nrm(ks[18], (L, D_FF), 0.01),
        'w_down': nrm(ks[19], (L, D_FF, D), D_FF ** -0.5),
        'final_norm': gain(ks[20], (D,)),
    }

def first_block(x, mem, positions, norm_mix, w_in, lower_bounds, hg_norm, attn_sink, w_br_rec,
              w_br_att, w_mix_out, norm_mem, norm_mem_kv, w_mem_q, w_mem_kv, w_mem_o, norm_ffn,
              w_up, conv_w, conv_b, w_down, final_norm):
    lb_table = jnp.cumsum(jax.nn.softmax(lower_bounds.astype(jnp.float32), axis=1), axis=1)
    h = x
    for l in range(DEPTH):
        n = rms_norm(h, norm_mix[l])
        h = h + token_mixers(n, positions, w_in[l], lb_table[0, l], lb_table[1, l], hg_norm[l],
                             attn_sink[l], w_br_rec[l], w_br_att[l], w_mix_out[l])
        n = rms_norm(h, norm_mem[l])
        mem_n = rms_norm(mem, norm_mem_kv[l])
        h = h + memory_cross_attention(n, mem_n, w_mem_q[l], w_mem_kv[l], w_mem_o[l])
        n = rms_norm(h, norm_ffn[l])
        h = h + conv_ffn(n, w_up[l], conv_w[l], conv_b[l], w_down[l])
    return rms_norm(h, final_norm)


DEPTH_2 = 2

N_EVEN = (DEPTH_2 + 1) // 2
N_ODD = DEPTH_2 // 2

POOL_WINDOWS = (2, 4, 8, 16)
POOL_GROUPS = len(POOL_WINDOWS)
POOL_DIM = D_MODEL // 2
POOL_GROUP_DIM = POOL_DIM // POOL_GROUPS

MLA_HEADS = 8
QK_NOPE_DIM = D_MODEL // 16
QK_ROPE_DIM = D_MODEL // 32
QK_HEAD_DIM = QK_NOPE_DIM + QK_ROPE_DIM
V_HEAD_DIM = D_MODEL // 16
Q_LORA_RANK = 3 * D_MODEL // 8
KV_LORA_RANK = D_MODEL // 4
ROPE_THETA_2 = 10000.0
Q_BLOCK = 128

MIX_IN_EVEN = POOL_DIM + Q_LORA_RANK + KV_LORA_RANK + QK_ROPE_DIM
MIX_OUT_EVEN = POOL_DIM + MLA_HEADS * V_HEAD_DIM

CONV_DIM = D_MODEL


def rms_norm_2(x, g):
    xf = x.astype(jnp.float32)
    y = xf * lax.rsqrt(jnp.mean(xf * xf, axis=-1, keepdims=True) + NORM_EPS)
    return (y * g.astype(jnp.float32)).astype(x.dtype)

def swiglu(x, w_gate, w_up, w_down):
    return (jax.nn.silu(x @ w_gate) * (x @ w_up)) @ w_down

def rotary(x, cos, sin):
    x1, x2 = jnp.split(x, 2, axis=-1)
    c = cos[None, :, None, :]
    s = sin[None, :, None, :]
    return jnp.concatenate([x1 * c - x2 * s, x2 * c + x1 * s], axis=-1)

def causal_multiscale_pool(u):
    s = u.shape[1]
    uf = u.astype(jnp.float32)
    cs = jnp.pad(jnp.cumsum(uf, axis=1), ((0, 0), (1, 0), (0, 0), (0, 0)))
    t = jnp.arange(1, s + 1)
    means = []
    for g, w in enumerate(POOL_WINDOWS):
        lo = jnp.maximum(t - w, 0)
        wsum = cs[:, 1:, g] - cs[:, lo, g]
        cnt = jnp.minimum(t, w).astype(jnp.float32)[None, :, None]
        means.append(wsum / cnt)
    mean = jnp.stack(means, axis=2)
    return (mean - uf).astype(u.dtype)

def causal_attention(q, k, v):
    b, s, h, dqk = q.shape
    dv = v.shape[-1]
    scale = dqk ** -0.5
    kpos = jnp.arange(s)

    def block(i):
        start = i * Q_BLOCK
        qb = lax.dynamic_slice_in_dim(q, start, Q_BLOCK, axis=1)
        sc = jnp.einsum('bqhd,bkhd->bhqk', qb, k,
                        preferred_element_type=jnp.float32) * scale
        qpos = start + jnp.arange(Q_BLOCK)
        sc = jnp.where(kpos[None, :] <= qpos[:, None], sc, -jnp.inf)
        p = jax.nn.softmax(sc, axis=-1)
        return jnp.einsum('bhqk,bkhd->bqhd', p.astype(v.dtype), v)

    out = lax.map(block, jnp.arange(s // Q_BLOCK))
    return jnp.moveaxis(out, 0, 1).reshape(b, s, h, dv)

def pool_mla_mixer(hn, cos, sin, w_in, q_a_norm, w_q_up, kv_a_norm, w_kv_up,
                   q_head_norm, k_head_norm, w_pool, pool_scale, w_out):
    b, s, _ = hn.shape
    z = hn @ w_in
    c1 = POOL_DIM
    c2 = c1 + Q_LORA_RANK
    c3 = c2 + KV_LORA_RANK
    u, q_lat, kv_lat, k_rope = jnp.split(z, [c1, c2, c3], axis=-1)

    u = u.reshape(b, s, POOL_GROUPS, POOL_GROUP_DIM)
    pooled = causal_multiscale_pool(u)
    pool_out = jnp.einsum('bsgc,gcd->bsgd', pooled, w_pool).reshape(b, s, POOL_DIM) * pool_scale

    q = (rms_norm_2(q_lat, q_a_norm) @ w_q_up).reshape(b, s, MLA_HEADS, QK_HEAD_DIM)
    kv = (rms_norm_2(kv_lat, kv_a_norm) @ w_kv_up).reshape(b, s, MLA_HEADS, QK_NOPE_DIM + V_HEAD_DIM)
    k_nope, v = jnp.split(kv, [QK_NOPE_DIM], axis=-1)
    k_rope_h = jnp.broadcast_to(k_rope[:, :, None, :], (b, s, MLA_HEADS, QK_ROPE_DIM))
    k = jnp.concatenate([k_nope, k_rope_h], axis=-1)
    q = rms_norm_2(q, q_head_norm)
    k = rms_norm_2(k, k_head_norm)
    q = jnp.concatenate([q[..., :QK_NOPE_DIM], rotary(q[..., QK_NOPE_DIM:], cos, sin)], axis=-1)
    k = jnp.concatenate([k[..., :QK_NOPE_DIM], rotary(k[..., QK_NOPE_DIM:], cos, sin)], axis=-1)
    attn = causal_attention(q, k, v).reshape(b, s, MLA_HEADS * V_HEAD_DIM)

    return jnp.concatenate([pool_out, attn], axis=-1) @ w_out

def gated_conv_mixer(hn, w_in, conv_w, w_out):
    gb, gc, hh = jnp.split(hn @ w_in, 3, axis=-1)
    u = gc * hh
    s = u.shape[1]
    up = jnp.pad(u, ((0, 0), (CONV_WIDTH - 1, 0), (0, 0)))
    y = conv_w[0] * up[:, 0:s]
    for j in range(1, CONV_WIDTH):
        y = y + conv_w[j] * up[:, j:j + s]
    return (gb * y) @ w_out

def second_inputs(seed: int = 0) -> dict:
    key = jax.random.key(seed)
    ks = iter(jax.random.split(key, 32))

    def dense(shape, fan_in):
        return jax.random.normal(next(ks), shape, jnp.float32) * (fan_in ** -0.5)

    def gain(shape):
        return 1.0 + 0.05 * jax.random.normal(next(ks), shape, jnp.float32)

    return {
        "x": jax.random.normal(next(ks), (BATCH, SEQ, D_MODEL), jnp.float32),
        "ffn1_norm": gain((DEPTH_2, D_MODEL)),
        "ffn1_w_gate": dense((DEPTH_2, D_MODEL, D_FF), D_MODEL),
        "ffn1_w_up": dense((DEPTH_2, D_MODEL, D_FF), D_MODEL),
        "ffn1_w_down": dense((DEPTH_2, D_FF, D_MODEL), D_FF),
        "mix_norm": gain((DEPTH_2, D_MODEL)),
        "ffn2_norm": gain((DEPTH_2, D_MODEL)),
        "ffn2_w_gate": dense((DEPTH_2, D_MODEL, D_FF), D_MODEL),
        "ffn2_w_up": dense((DEPTH_2, D_MODEL, D_FF), D_MODEL),
        "ffn2_w_down": dense((DEPTH_2, D_FF, D_MODEL), D_FF),
        "a_w_in": dense((N_EVEN, D_MODEL, MIX_IN_EVEN), D_MODEL),
        "a_q_a_norm": gain((N_EVEN, Q_LORA_RANK)),
        "a_w_q_up": dense((N_EVEN, Q_LORA_RANK, MLA_HEADS * QK_HEAD_DIM), Q_LORA_RANK),
        "a_kv_a_norm": gain((N_EVEN, KV_LORA_RANK)),
        "a_w_kv_up": dense((N_EVEN, KV_LORA_RANK, MLA_HEADS * (QK_NOPE_DIM + V_HEAD_DIM)), KV_LORA_RANK),
        "a_q_head_norm": gain((N_EVEN, QK_HEAD_DIM)),
        "a_k_head_norm": gain((N_EVEN, QK_HEAD_DIM)),
        "a_w_pool": dense((N_EVEN, POOL_GROUPS, POOL_GROUP_DIM, POOL_GROUP_DIM), POOL_GROUP_DIM),
        "a_pool_scale": gain((N_EVEN, POOL_DIM)),
        "a_w_out": dense((N_EVEN, MIX_OUT_EVEN, D_MODEL), MIX_OUT_EVEN),
        "c_w_in": dense((N_ODD, D_MODEL, 3 * CONV_DIM), D_MODEL),
        "c_conv_w": dense((N_ODD, CONV_WIDTH, CONV_DIM), CONV_WIDTH),
        "c_w_out": dense((N_ODD, CONV_DIM, D_MODEL), CONV_DIM),
    }

def second_block(x, ffn1_norm, ffn1_w_gate, ffn1_w_up, ffn1_w_down, mix_norm,
              ffn2_norm, ffn2_w_gate, ffn2_w_up, ffn2_w_down,
              a_w_in, a_q_a_norm, a_w_q_up, a_kv_a_norm, a_w_kv_up,
              a_q_head_norm, a_k_head_norm, a_w_pool, a_pool_scale, a_w_out,
              c_w_in, c_conv_w, c_w_out):
    s = x.shape[1]
    pos = jnp.arange(s, dtype=jnp.float32)
    inv_freq = ROPE_THETA_2 ** (-jnp.arange(0, QK_ROPE_DIM, 2, dtype=jnp.float32) / QK_ROPE_DIM)
    ang = pos[:, None] * inv_freq[None, :]
    cos = jnp.cos(ang).astype(x.dtype)
    sin = jnp.sin(ang).astype(x.dtype)

    for layer in range(DEPTH_2):
        x = x + 0.5 * swiglu(rms_norm_2(x, ffn1_norm[layer]),
                             ffn1_w_gate[layer], ffn1_w_up[layer], ffn1_w_down[layer])
        hn = rms_norm_2(x, mix_norm[layer])
        i = layer // 2
        if layer % 2 == 0:
            x = x + pool_mla_mixer(hn, cos, sin, a_w_in[i], a_q_a_norm[i], a_w_q_up[i],
                                   a_kv_a_norm[i], a_w_kv_up[i], a_q_head_norm[i],
                                   a_k_head_norm[i], a_w_pool[i], a_pool_scale[i], a_w_out[i])
        else:
            x = x + gated_conv_mixer(hn, c_w_in[i], c_conv_w[i], c_w_out[i])
        x = x + 0.5 * swiglu(rms_norm_2(x, ffn2_norm[layer]),
                             ffn2_w_gate[layer], ffn2_w_up[layer], ffn2_w_down[layer])
    return x


def setup_inputs(seed=0):
    out = dict(first_inputs(seed))
    for name, value in second_inputs(seed + 1).items():
        if name != "x":
            out[name + "_2"] = value
    return out


def reference(
    x, mem, positions, norm_mix, w_in, lower_bounds, hg_norm, attn_sink, w_br_rec, w_br_att,
    w_mix_out, norm_mem, norm_mem_kv, w_mem_q, w_mem_kv, w_mem_o, norm_ffn, w_up, conv_w,
    conv_b, w_down, final_norm, ffn1_norm_2, ffn1_w_gate_2, ffn1_w_up_2, ffn1_w_down_2,
    mix_norm_2, ffn2_norm_2, ffn2_w_gate_2, ffn2_w_up_2, ffn2_w_down_2, a_w_in_2, a_q_a_norm_2,
    a_w_q_up_2, a_kv_a_norm_2, a_w_kv_up_2, a_q_head_norm_2, a_k_head_norm_2, a_w_pool_2,
    a_pool_scale_2, a_w_out_2, c_w_in_2, c_conv_w_2, c_w_out_2,
):
    x = first_block(
        x, mem, positions, norm_mix, w_in, lower_bounds, hg_norm, attn_sink, w_br_rec, w_br_att,
        w_mix_out, norm_mem, norm_mem_kv, w_mem_q, w_mem_kv, w_mem_o, norm_ffn, w_up, conv_w,
        conv_b, w_down, final_norm,
    )
    return second_block(
        x, ffn1_norm_2, ffn1_w_gate_2, ffn1_w_up_2, ffn1_w_down_2, mix_norm_2, ffn2_norm_2,
        ffn2_w_gate_2, ffn2_w_up_2, ffn2_w_down_2, a_w_in_2, a_q_a_norm_2, a_w_q_up_2,
        a_kv_a_norm_2, a_w_kv_up_2, a_q_head_norm_2, a_k_head_norm_2, a_w_pool_2,
        a_pool_scale_2, a_w_out_2, c_w_in_2, c_conv_w_2, c_w_out_2,
    )


_drawn_inputs = setup_inputs


def setup_inputs(seed=0):
    import zlib

    import numpy as np

    out = dict(_drawn_inputs(seed))
    spreads = {}
    factors = {'norm_mix': 3.517,
     'hg_norm': 5.359,
     'attn_sink': 64.0,
     'norm_mem': 8.0,
     'norm_mem_kv': 8.0,
     'norm_ffn': 2.682,
     'conv_b': 7.71,
     'a_q_a_norm_2': 8.0,
     'a_kv_a_norm_2': 5.766,
     'a_q_head_norm_2': 8.0,
     'a_k_head_norm_2': 8.0,
     'ffn2_norm_2': 7.688,
     'a_pool_scale_2': 7.448}
    for name, (base, spread) in spreads.items():
        noise = np.random.default_rng([zlib.crc32(name.encode()), seed]).standard_normal(out[name].shape)
        drawn = base * np.exp(spread * noise) if base else spread * noise
        out[name] = __import__('jax').numpy.asarray(drawn.astype(out[name].dtype))
    for name, factor in factors.items():
        out[name] = (out[name] * factor).astype(out[name].dtype)
    return out
```

```python
from contextlib import ExitStack

import numpy as np

import concourse.bass as bass
from concourse import mybir

F32 = mybir.dt.float32
F32R = mybir.dt.float32r
U8 = mybir.dt.uint8
I32 = mybir.dt.int32
ALU = mybir.AluOpType
ACT = mybir.ActivationFunctionType
AX = mybir.AxisListType

P = 128
S = 512
D = 1024
KT = D // P
MEM = 256
FF = 2816
FT = FF // P
HEADS = 4
HK = 128
BLK = S // P
WIN_HEADS, WIN_KV, WIN_D = 8, 2, 64
WIN_TILES = WIN_HEADS // 2
MEM_HEADS, MEM_D = 4, 256
MLA_HEADS, MLA_NOPE, MLA_ROPE, MLA_V = 8, 64, 32, 64
MLA_QK = MLA_NOPE + MLA_ROPE
Q_LORA, KV_LORA, POOL = 384, 256, 512
EPS = 1e-6
NEG = -1e30
CW = 2048
PAIR = 256

PHASES = [
    ("qf", 6, 12), ("v", 2, 4), ("g", 2, 4), ("kv_a", 1, 2), ("q_a", 2, 4), ("merge", 12, 32), ("mix_out", 4, 8),
    ("mem_k", 4, 8), ("mem_v", 4, 8), ("mem_q", 4, 8), ("mem_o", 4, 8),
    ("up0", 22, 44), ("down0", 12, 8),
    ("up1", 22, 44), ("down1", 12, 8),
    ("a_in", 5, 10), ("mla", 3, 24), ("a_out", 4, 8),
    ("up2", 22, 44), ("down2", 12, 8),
    ("up3", 22, 44), ("down3", 12, 8),
    ("c_in", 12, 24), ("c_out", 4, 8),
    ("up4", 22, 44), ("down4", 12, 8),
]
C0, T0 = {}, {}
_c = _t = 0
for _name, _n, _m in PHASES:
    C0[_name], T0[_name] = _c, _t
    _c, _t = _c + _n, _t + _m
CHUNKS = _c
RESIDUALS = ["mix_out", "mem_o", "down0", "renorm", "down1", "a_out", "down2", "down3", "c_out", "down4"]
R0 = {name: KT * i for i, name in enumerate(RESIDUALS)}
N0 = {name: i for i, name in enumerate(RESIDUALS)}

COL = {}
_at = 0
for _name, _n in [("norm_mix", 8), ("norm_mem", 8), ("norm_mem_kv", 8), ("norm_ffn", 8), ("final_norm", 8),
                  ("ffn1_0", 8), ("ffn1_1", 8), ("mix_0", 8), ("mix_1", 8), ("ffn2_0", 8), ("ffn2_1", 8),
                  ("hg_norm", 4), ("conv_b", 22), ("conv_w0", 22), ("conv_w1", 22), ("conv_w2", 22),
                  ("q_a_norm", 3), ("kv_a_norm", 2), ("q_head", 1), ("k_head", 1), ("pool_scale", 4),
                  ("cc_w0", 8), ("cc_w1", 8), ("cc_w2", 8), ("sink", 8), ("lb0", 8), ("lb1", 8),
                  ("inv_freq", 1), ("rot_sign", 1), ("eps", 1)]:
    COL[_name] = _at
    _at += _n
NPAR = _at

CCOL = {}
_at = 0
for _name, _n in [("ident", P), ("ones", P), ("band", BLK * 384), ("perm1", P), ("perm2", P), ("causal", P), ("sel", 32),
                  ("rope_c", S), ("rope_s", S), ("count", 4 * S), ("levels", 7 * P)]:
    CCOL[_name] = _at
    _at += _n
NCONST = _at


def row(tensor, i):
    if isinstance(i, int):
        return tensor[:, i, :]
    return tensor[:, bass.ds(i, 1), :].rearrange("p a n -> p (a n)")


def rows(tensor, i, n):
    return tensor[:, bass.ds(i, n), :]


def past(n):
    return n + 1


def free(ap, offset, dims):
    return bass.AP(tensor=ap.tensor, offset=ap.offset + offset, ap=[ap.ap[0]] + dims)


def build(nc, stream, x_in, mem_in, pos_in, par_in, const_in, out):
    ctx = ExitStack()
    with ctx:
        TILE = 4 * S
        at = [16512]

        def take(nbytes):
            nbytes = -(-nbytes // 32) * 32
            at[0] += nbytes
            return at[0] - nbytes

        def place(name, offset, shape, dt=F32):
            return nc.alloc_sbuf_tensor_at(name, shape, dt, offset=offset)

        H_AT, XH_AT, XL_AT = take(KT * TILE), take(KT * TILE), take(KT * TILE)
        W_AT = [take(4 * CW) for _ in range(6)]
        HID = take(2 * FT * TILE)
        TMP = take(2 * 4 * (S + 8) + 2 * TILE)

        def hid(tile):
            return HID + TILE * tile

        h = place("h", H_AT, [P, KT, S])
        x_hi = place("x_hi", XH_AT, [P, KT, S], F32R)
        x_lo = place("x_lo", XL_AT, [P, KT, S], F32R)
        stage = [place(f"stage{i}", W_AT[i], [P, CW]) for i in range(2)]
        w_hi = [place(f"w_hi{i}", W_AT[2 + i], [P, CW], F32R) for i in range(2)]
        w_lo = [place(f"w_lo{i}", W_AT[4 + i], [P, CW], F32R) for i in range(2)]
        gate_b = place("gate_b", TMP, [P, 2, S + 8])
        up_b = place("up_b", TMP + 2 * 4 * (S + 8), [P, 2, S])
        rstd = place("rstd", take(TILE), [P, S])
        ssum = place("ssum", take(TILE), [P, S])
        sq = place("sq", take(TILE), [P, S])
        par = place("par", take(4 * NPAR), [P, NPAR])
        const2 = place("const2", take(4 * 2 * P), [P, 2 * P])
        ident, ones = const2[:, 0:P], const2[:, P:2 * P]
        small = place("small", take(4 * 64), [P, 64])
        ls_mask = place("ls_mask", take(7 * P), [P, 7, P], U8)
        rope_c = place("rope_c", take(TILE), [P, S])
        rope_s = place("rope_s", take(TILE), [P, S])
        assert at[0] <= 229344

        f_hi = place("f_hi", HID, [P, FT, S], F32R)
        f_lo = place("f_lo", hid(FT), [P, FT, S], F32R)
        qf = place("qf", hid(0), [P, 12, S])
        v_nat = place("v_nat", hid(12), [P, BLK, HEADS * HK])
        g_silu = place("g_silu", hid(16), [P, HEADS, S])
        rec_hi = place("rec_hi", hid(26), [P, HEADS, S], F32R)
        rec_lo = place("rec_lo", hid(30), [P, HEADS, S], F32R)
        att_hi = place("att_hi", hid(34), [P, WIN_TILES, S], F32R)
        att_lo = place("att_lo", hid(38), [P, WIN_TILES, S], F32R)
        mrg_hi = place("mrg_hi", hid(0), [P, KT, S], F32R)
        mrg_lo = place("mrg_lo", hid(8), [P, KT, S], F32R)
        QQ = [place(f"QQ{e}", hid(20 if e == 0 else 34), [P, 2, S]) for e in range(2)]
        KK = [place(f"KK{e}", hid(22 if e == 0 else 36), [P, 2, S]) for e in range(2)]
        TA = [place(f"TA{e}", hid(24 if e == 0 else 38), [P, 2, S // 2]) for e in range(2)]
        TB = [place(f"TB{e}", hid(25 if e == 0 else 39), [P, 2, S // 4]) for e in range(2)]
        KC = [sq, rstd]
        A = [place(f"A{e}", hid(40) if e == 0 else TMP, [P, BLK, S]) for e in range(2)]
        qa = place("qa", hid(20), [P, WIN_TILES, S])
        va = place("va", hid(24), [P, BLK, P])
        k_pad = place("k_pad", hid(0), [P, P + S + P])
        q_st = [place(f"q_st{e}", hid(2 + e), [P, S]) for e in range(2)]
        w_s = [place(f"w_s{e}", hid(4 + 3 * e), [P, BLK, 384]) for e in range(2)]
        w_pT = [place(f"w_pT{e}", hid(10 + 3 * e), [P, 3 * BLK * P]) for e in range(2)]
        band = place("band", TMP, [P, BLK, 384])
        perm1 = place("perm1", hid(25), [P, P])
        pos_i = place("pos_i", hid(34), [P, S], I32)
        ang = place("ang", hid(35), [P, S])
        turns = place("turns", hid(36), [P, S])
        mask_f = place("mask_f", hid(38), [P, 7, P])
        sq8 = place("sq8", hid(0), [P, KT, S])
        xn = place("xn", hid(8), [P, 2, S])
        mem_hi = place("mem_hi", hid(16), [P, KT, MEM], F32R)
        mem_lo = place("mem_lo", hid(20), [P, KT, MEM], F32R)
        mem_raw = place("mem_raw", hid(0), [P, KT, MEM])
        mem_sq = place("mem_sq", hid(4), [P, KT, MEM])
        mem_r = place("mem_r", hid(8), [P, MEM])
        mem_t = place("mem_t", hid(9), [P, 2, MEM])
        km = place("km", hid(0), [P, KT, MEM])
        vm = place("vm", hid(4), [P, 2, D])
        qm = [place(f"qm{e}", hid(8 + 2 * e), [P, 2, S]) for e in range(2)]
        m_p = [place(f"m_p{e}", hid(12 + 2 * e), [P, BLK, MEM]) for e in range(2)]
        m_pT = [place(f"m_pT{e}", hid(16 + 2 * e), [P, 2, S]) for e in range(2)]
        v_st = [place(f"v_st{e}", hid(20 + e), [P, 2, MEM_D]) for e in range(2)]
        mo_hi = place("mo_hi", hid(28), [P, KT, S], F32R)
        mo_lo = place("mo_lo", hid(36), [P, KT, S], F32R)
        PAD = 8
        u_p = place("u_p", hid(0), [P, 4, PAD + S])
        lat = place("lat", hid(5), [P, 6, S])
        lat_hi = place("lat_hi", hid(11), [P, 5, S], F32R)
        lat_lo = place("lat_lo", hid(16), [P, 5, S], F32R)
        lat_q2 = place("lat_q2", hid(21), [P, 5, S])
        lat_r = place("lat_r", hid(29), [P, 2, S])
        pl_hi = place("pl_hi", hid(21), [P, 4, S], F32R)
        pl_lo = place("pl_lo", hid(25), [P, 4, S], F32R)
        win_a = place("win_a", hid(36), [P, 4, PAD + S])
        win_b = place("win_b", XH_AT, [P, 4, PAD + S])
        cnt = place("cnt", TMP, [P, 4, S])
        v_mla = place("v_mla", hid(29), [P, BLK, MLA_HEADS * MLA_V])
        pc2 = place("pc2", hid(33), [P, 2 * P + 32])
        perm2, causal, sel16 = pc2[:, 0:P], pc2[:, P:2 * P], pc2[:, 2 * P:2 * P + 32]
        cat_hi = [place("cat_hi0", hid(36), [P, 4, S], F32R), place("cat_hi1", hid(0), [P, 4, S], F32R)]
        cat_lo = [place("cat_lo0", hid(40), [P, 4, S], F32R), place("cat_lo1", hid(4), [P, 4, S], F32R)]
        q_h = place("q_h", XH_AT, [P, MLA_HEADS, S])
        k_h = place("k_h", XL_AT, [P, MLA_HEADS, S])
        qh_sq = place("qh_sq", hid(8), [P, MLA_HEADS, S])
        kh_sq = place("kh_sq", hid(16), [P, MLA_HEADS, S])
        qk_st = [place(f"qk_st{e}", hid(8 + 4 * e), [P, 2, S]) for e in range(2)]
        qk_t = [place(f"qk_t{e}", hid(10 + 4 * e), [P, 2, S]) for e in range(2)]
        l_p = place("l_p", hid(16), [P, BLK, S])
        l_pT = place("l_pT", hid(20), [P, BLK, S])
        vl_st = [place(f"vl_st{e}", hid(24 + e), [P, BLK, MLA_V]) for e in range(2)]
        sel_st = [place(f"sel_st{e}", hid(26 + e), [P, 2, MLA_QK]) for e in range(2)]
        cc_hi = place("cc_hi", hid(0), [P, KT, S], F32R)
        cc_lo = place("cc_lo", hid(8), [P, KT, S], F32R)
        cg = place("cg", hid(16), [P, 2, S])
        cu = place("cu", hid(18), [P, 2, S + 2])
        cv = place("cv", hid(21), [P, 2, S])
        ch = place("ch", hid(23), [P, 2, S])

        ps = nc.alloc_psum_tensor("ps", [P, 8, S], F32)

        def sem(name):
            return ctx.enter_context(nc.semaphore(name))

        landed = [sem("landed0"), sem("landed1")]
        hi_ready, lo_ready = sem("hi_ready"), sem("lo_ready")
        chunk_done = sem("chunk_done")
        acc_evac = sem("acc_evac")
        x_landed, par_landed, pos_landed, mask_landed = sem("x_landed"), sem("par_landed"), sem("pos_landed"), sem("mask_landed")
        x_sq, trig, rope1_ready, xn_ready = sem("x_sq"), sem("trig"), sem("rope1_ready"), sem("xn_ready")
        lb_step, lb_exp = sem("lb_step"), sem("lb_exp")
        stat_done, std_ready, rstd_ready = sem("stat_done"), sem("std_ready"), sem("rstd_ready")
        sq_ready, ss_ready = sem("sq_ready"), sem("ss_ready")
        x_hi_ready, x_ready = sem("x_hi_ready"), sem("x_ready")
        renorm_ready = sem("renorm_ready")
        conv_step, silu_ready, prod_ready = sem("conv_step"), sem("silu_ready"), sem("prod_ready")
        f_hi_ready, f_ready = sem("f_hi_ready"), sem("f_ready")
        qf_act, f_ready1, g_ready = sem("qf_act"), sem("f_ready1"), sem("g_ready")
        ls_q, ls_init, ls_ops, ls_scores, ls_diag, ls_cross, ls_v, ls_kc = (sem("ls_q"), sem("ls_init"), sem("ls_ops"), sem("ls_scores"),
                                                                    sem("ls_diag"), sem("ls_cross"), sem("ls_v"), sem("ls_kc"))
        ls_o, ls_sq, ls_ss, ls_std, ls_norm, ls_hi, rec_ready = (sem("ls_o"), sem("ls_sq"), sem("ls_ss"), sem("ls_std"),
                                                                 sem("ls_norm"), sem("ls_hi"), sem("rec_ready"))
        const_landed, pad_ready, perm_done, rot_step = sem("const_landed"), sem("pad_ready"), sem("perm_done"), sem("rot_step")
        wa_q, wa_scores, wa_s, wa_max, wa_exp, wa_den, wa_p, wa_turned, wa_pT, wa_o, wa_hi, att_ready = (
            sem("wa_q"), sem("wa_scores"), sem("wa_s"), sem("wa_max"), sem("wa_exp"), sem("wa_den"), sem("wa_p"),
            sem("wa_turned"), sem("wa_pT"), sem("wa_o"), sem("wa_hi"), sem("att_ready"))
        gate_sig, mrg_t, mrg_prod, mrg_sum, mrg_hi_ready, mrg_ready = (sem("gate_sig"), sem("mrg_t"), sem("mrg_prod"), sem("mrg_sum"),
                                                             sem("mrg_hi_ready"), sem("mrg_ready"))
        mem_landed, mem_sq_ready, mem_stat, mem_std, mem_n, mem_hi_ready, mem_ready = (
            sem("mem_landed"), sem("mem_sq_ready"), sem("mem_stat"), sem("mem_std"), sem("mem_n"), sem("mem_hi_ready"), sem("mem_ready"))
        ma_scores, ma_max, ma_exp, ma_den, ma_p, ma_turned, ma_pT, ma_v, ma_o, ma_hi, mo_ready = (
            sem("ma_scores"), sem("ma_max"), sem("ma_exp"), sem("ma_den"), sem("ma_p"), sem("ma_turned"), sem("ma_pT"),
            sem("ma_v"), sem("ma_o"), sem("ma_hi"), sem("mo_ready"))
        rope2_landed, lat_sq, lat_stat, lat_std, lat_n, lat_hi_ready, lat_ready = (
            sem("rope2_landed"), sem("lat_sq"), sem("lat_stat"), sem("lat_std"), sem("lat_n"), sem("lat_hi_ready"), sem("lat_ready"))
        u_pad, pool_step, pl_hi_ready, pl_ready, mla_tile, cat0_hi, cat0_ready = (
            sem("u_pad"), sem("pool_step"), sem("pl_hi_ready"), sem("pl_ready"), sem("mla_tile"), sem("cat0_hi"), sem("cat0_ready"))
        kr_copied, hd_sq, hd_stat, hd_std, hd_rstd = sem("kr_copied"), sem("hd_sq"), sem("hd_stat"), sem("hd_std"), sem("hd_rstd")
        la_sel, la_spread, la_norm, la_swap, la_sin, la_cos, la_rot = (
            sem("la_sel"), sem("la_spread"), sem("la_norm"), sem("la_swap"), sem("la_sin"), sem("la_cos"), sem("la_rot"))
        la_scores, la_mask, la_max, la_exp, la_den, la_p, la_turned, la_pT, la_v, la_o, la_hi, cat1_ready = (
            sem("la_scores"), sem("la_mask"), sem("la_max"), sem("la_exp"), sem("la_den"), sem("la_p"), sem("la_turned"),
            sem("la_pT"), sem("la_v"), sem("la_o"), sem("la_hi"), sem("cat1_ready"))
        cu_pad, cu_ready, cv_step, cz_ready, cc_hi_ready, cc_ready = (
            sem("cu_pad"), sem("cu_ready"), sem("cv_step"), sem("cz_ready"), sem("cc_hi_ready"), sem("cc_ready"))
        out_done = sem("out_done")

        def pc(name, i, n=1):
            k = COL[name] + i
            return par[:, k:k + n] if isinstance(k, int) else par[:, bass.ds(k, n)]

        def cc(name, n):
            return const_in[:, CCOL[name]:CCOL[name] + n]

        UPS = {f"up{i}": i for i in range(5)}
        FOLLOWED = {
            "mix_out": "norm_mem", "mem_o": "norm_ffn", "down0": None, "renorm": "ffn1_0", "down1": "mix_0",
            "a_out": "ffn2_0", "down2": "ffn1_1", "down3": "mix_1", "c_out": "ffn2_1", "down4": None}
        SCALE = {"mix_out": 1.0, "mem_o": 1.0, "down0": 1.0, "down1": 0.5, "a_out": 1.0, "down2": 0.5, "down3": 0.5,
                 "c_out": 1.0, "down4": 0.5}
        XR0, _n = {}, 0
        for name in RESIDUALS:
            XR0[name] = KT + _n
            _n += KT if FOLLOWED[name] else 0
        NS0 = {name: 1 + i for i, name in enumerate(n for n in RESIDUALS if n != "down4")}

        MLA_LAST = [6, 15, 23]
        LEVELS = 10

        def walk(engine, n, body, first=0):
            with engine.Fori(first, n) as it:
                body(it)

        block = ctx.enter_context(nc.Block())

        @block.sync
        def _(sp):
            for i in range(4):
                sp.dma_start(h[:, 2 * i:2 * i + 2, :], x_in[:, 2 * i:2 * i + 2, :]).then_inc(x_landed, 16)

            def load(c, slot):
                src = stream[c] if isinstance(c, int) else stream[bass.ds(c, 1)].rearrange("a p n -> p (a n)")
                sp.dma_start(stage[slot][:, :], src).then_inc(landed[slot], 16)

            load(0, 0)
            load(1, 1)

            def two(i):
                for s in range(2):
                    sp.wait_ge(lo_ready, i * 2 + s - 1)
                    load(i * 2 + s, s)

            walk(sp, CHUNKS // 2, two, 1)
            if CHUNKS % 2:
                sp.wait_ge(lo_ready, CHUNKS - 2)
                load(CHUNKS - 1, (CHUNKS - 1) % 2)

            for m in range(KT):
                sp.wait_ge(acc_evac, T0["down4"] + m + 1)
                sp.dma_start(out[:, m, :], h[:, m, :]).then_inc(out_done, 16)
            sp.wait_ge(out_done, 16 * KT)

        @block.scalar
        def _(act):
            def split_hi(c):
                n, reg = c
                if isinstance(reg, int) and n + reg >= CHUNKS:
                    return
                slot = n % 2
                act.wait_ge(landed[slot], reg * 8 + 16 * (n // 2 + 1))
                if n >= 2:
                    act.wait_ge(chunk_done, reg + (n - 1))
                act.activation(w_hi[slot][:, :], stage[slot][:, :], ACT.Copy).then_inc(hi_ready, 1)

            def stat(n, bias_scale=1.0 / D):
                act.wait_ge(stat_done, n + 1)
                act.activation(ssum[:, :], ps[:, 4, :], ACT.Sqrt, bias=pc("eps", 0), scale=bias_scale).then_inc(std_ready, 1)

            def residual(name):
                r0, t0, c0 = XR0[name], T0[name], C0[name]
                gain = FOLLOWED[name]
                per = 6 if name.startswith("down") else 2

                def step(it):
                    for pair in range(2):
                        for k in range(per // 2):
                            split_hi((c0 + 2 + pair * (per // 2) + k, it * per))
                        for e in range(2):
                            m = 2 * pair + e
                            if gain:
                                act.wait_ge(acc_evac, it * 4 + t0 + m + 1)
                                act.activation(row(x_hi, it * 4 + m), row(h, it * 4 + m), ACT.Copy,
                                               scale=pc(gain, it * 4 + m)).then_inc(x_hi_ready, 1)

                if name == "down4":
                    step(0)
                    step(1)
                else:
                    walk(act, 2, step)

            def up(name):
                c0, t0, f0, conv = C0[name], T0[name], FT * UPS[name], name == "up0"

                def step(it):
                    split_hi((c0 + 2, it * 2))
                    for e in range(2):
                        if conv:
                            act.wait_ge(conv_step, it * 6 + 3 * e + 3)
                            act.activation(gate_b[:, e, 1:1 + S], up_b[:, e, :], ACT.Silu).then_inc(silu_ready, 1)
                        else:
                            act.wait_ge(acc_evac, it * 4 + t0 + e + 1)
                            act.activation(gate_b[:, e, 1:1 + S], gate_b[:, e, 1:1 + S], ACT.Silu).then_inc(silu_ready, 1)
                    split_hi((c0 + 3, it * 2))
                    for e in range(2):
                        act.wait_ge(prod_ready, it * 2 + f0 + e + 1)
                        act.activation(row(f_hi, it * 2 + e), up_b[:, e, :], ACT.Copy).then_inc(f_hi_ready, 1)

                walk(act, FT // 2, step)

            act.dma_start(par[:, :], par_in).then_inc(par_landed, 16)
            act.dma_start(const2[:, :], const_in[:, 0:2 * P]).then_inc(par_landed, 16)
            act.dma_start(pos_i[:, :], pos_in).then_inc(pos_landed, 16)
            act.dma_start(mask_f[:, :, :], cc("levels", 7 * P).rearrange("p (a n) -> p a n", a=7)).then_inc(mask_landed, 16)
            for k in range(KT):
                if k % 2 == 0:
                    act.wait_ge(x_landed, 16 * (KT // 2))
                act.activation(sq8[:, k, :], h[:, k, :], ACT.Square).then_inc(x_sq, 1)
            split_hi((0, 0))
            split_hi((1, 0))
            act.wait_ge(par_landed, 32)
            act.wait_ge(lb_step, 3)
            act.activation(small[:, 32:40], small[:, 32:40], ACT.Exp).then_inc(lb_exp, 1)
            act.activation(small[:, 40:48], small[:, 40:48], ACT.Exp).then_inc(lb_exp, 1)
            stat(0)
            for k in range(KT):
                act.wait_ge(xn_ready, k + 1)
                act.activation(x_hi[:, k, :], xn[:, k % 2, :], ACT.Copy).then_inc(x_hi_ready, 1)

            c0 = C0["qf"]

            def qf_step(it):
                split_hi((c0 + 2, it * 2))
                split_hi((c0 + 3, it * 2))

            act.wait_ge(trig, 2)
            act.activation(rope_s[:, :], ang[:, :], ACT.Sin).then_inc(rope1_ready, 1)
            act.activation(rope_c[:, :], turns[:, :], ACT.Sin).then_inc(rope1_ready, 1)
            walk(act, 3, qf_step)
            act.wait_ge(acc_evac, T0["qf"] + 4)
            act.activation(qf[:, 0:4, :], qf[:, 0:4, :], ACT.Silu).then_inc(qf_act, 1)
            act.wait_ge(acc_evac, T0["qf"] + 12)
            act.activation(qf[:, 4:12, :], qf[:, 4:12, :], ACT.Sigmoid).then_inc(qf_act, 1)
            for c in range(C0["v"], C0["kv_a"]):
                split_hi((c + 2, 0))
            act.wait_ge(acc_evac, T0["g"] + 4)
            act.activation(g_silu[:, :, :], g_silu[:, :, :], ACT.Silu).then_inc(g_ready, 1)

            def ls_tail(it):
                for level in range(1, 8):
                    w = 1 << (level - 1)
                    for e in range(2):
                        act.wait_ge(ls_ops, it * 18 + (max(2 * (level - 1), 0) + e + 1))
                        if level > 1:
                            act.wait_ge(ls_scores, it * 2 * LEVELS + (2 * (level - 1) + e + 1))
                        else:
                            act.wait_ge(ls_o, past(it * 2))
                        for half in range(2):
                            act.activation(free(KC[e][:, :], half * w, [[2 * w, S // (2 * w)], [1, w]]),
                                           free(KK[e][:, :, :], half * w + (1 - half) * S, [[2 * w, S // (2 * w)], [1, w]]),
                                           ACT.Copy).then_inc(ls_kc, 1)
                for e in range(2):
                    head = it * 2 + e
                    a = A[e][:, :, :]
                    act.wait_ge(ls_scores, it * 2 * LEVELS + 2 * 8 + e + 1)
                    act.activation(free(a, P, [[1280, 2], [384, 2], [1, P]]),
                                   ps[:, 4 + 2 * e, :].rearrange("p (a b n) -> p a b n", a=2, b=2), ACT.Copy).then_inc(ls_cross, 1)
                for e in range(2):
                    act.wait_ge(ls_scores, it * 2 * LEVELS + 2 * 9 + e + 1)
                    act.activation(A[e][:, 0:2, 256:512], ps[:, 5 + 2 * e, :].rearrange("p (a n) -> p a n", a=2),
                                   ACT.Copy).then_inc(ls_cross, 1)
                    act.activation(A[e][:, 2:4, 0:256], ps[:, e, :].rearrange("p (a n) -> p a n", a=2),
                                   ACT.Copy).then_inc(ls_cross, 1)
                for e in range(2):
                    act.wait_ge(ls_o, past(it * 2 + e + 1))
                    act.activation(KK[e][:, 0, :], ps[:, 2 + e, :], ACT.Square).then_inc(ls_sq, 1)
                for e in range(2):
                    act.wait_ge(ls_ss, it * 2 + e + 1)
                    act.activation(KK[e][:, 1, :], ps[:, 4 + 2 * e, :], ACT.Sqrt, bias=pc("eps", 0), scale=1.0 / HK).then_inc(ls_std, 1)
                for e in range(2):
                    act.wait_ge(ls_norm, it * 8 + 4 * e + 4)
                    act.activation(row(rec_hi, it * 2 + e), TA[e][:, :, :].rearrange("p a n -> p (a n)"), ACT.Copy).then_inc(ls_hi, 1)

            walk(act, 2, ls_tail)

            act.wait_ge(rec_ready, past(HEADS))
            act.dma_start(band[:, :, :], cc("band", 4 * 384).rearrange("p (a n) -> p a n", a=4)).then_inc(const_landed, 16)
            act.dma_start(perm1[:, :], cc("perm1", P)).then_inc(const_landed, 16)
            for c in range(C0["kv_a"], C0["merge"]):
                split_hi((c + 2, 0))
            def wa_exps(it):
                def exps(e, p):
                    u = it * 4 + 2 * e + p
                    act.wait_ge(wa_max, u * 2 + 2)
                    for n in range(BLK):
                        act.activation(w_s[p][:, n, :], w_s[p][:, n, :], ACT.Exp, bias=small[:, 4 * p + n:4 * p + n + 1],
                                       accum_out=small[:, 8 + 4 * p + n:9 + 4 * p + n])
                    act.activation(small[:, 16 + 4 * p:20 + 4 * p], small[:, 4 * p:4 * p + 4], ACT.Exp,
                                   bias=pc("sink", it * 2 + e + 4 * p)).then_inc(wa_exp, 1)
                    act.wait_ge(wa_den, u * 2 + 2)
                    act.wait_ge(wa_exp, u + 1)
                    for n in range(BLK):
                        ins = act.activation(w_s[p][:, n, :], w_s[p][:, n, :], ACT.Copy, scale=small[:, 24 + 4 * p + n:25 + 4 * p + n])
                    ins.then_inc(wa_p, 1)

                for e in range(2):
                    exps(e, 0)
                    exps(e, 1)
                    act.wait_ge(wa_o, it * 4 + 2 * e + 2)
                    act.activation(row(att_hi, it * 2 + e), ps[:, 7, :], ACT.Copy).then_inc(wa_hi, 1)

            walk(act, 2, wa_exps)

            act.wait_ge(att_ready, past(WIN_TILES))
            act.dma_start(mem_raw[:, :, :], mem_in).then_inc(mem_landed, 16)
            act.wait_ge(mem_landed, 16)
            for k in range(KT):
                act.activation(mem_sq[:, k, :], mem_raw[:, k, :], ACT.Square).then_inc(mem_sq_ready, 1)
            act.wait_ge(mem_stat, 1)
            act.activation(mem_r[:, :], ps[:, 5, 0:MEM], ACT.Sqrt, bias=pc("eps", 0), scale=1.0 / D).then_inc(mem_std, 1)
            for k in range(KT):
                act.wait_ge(mem_n, k + 1)
                act.activation(mem_hi[:, k, :], mem_t[:, k % 2, :], ACT.Copy).then_inc(mem_hi_ready, 1)

            c0, t0 = C0["merge"], T0["merge"]

            def merge(it):
                for j in range(2):
                    t = it * 16 + (t0 + 8 * j)
                    n = it * 4 + 2 * j
                    split_hi((c0 + 2 + 3 * j, it * 6))
                    for e in range(2):
                        act.wait_ge(acc_evac, t + e + 1)
                        act.activation(gate_b[:, e, 0:S], gate_b[:, e, 0:S], ACT.Sigmoid).then_inc(gate_sig, 1)
                    split_hi((c0 + 3 + 3 * j, it * 6))
                    for e in range(2):
                        act.wait_ge(acc_evac, t + e + 3)
                        act.activation(up_b[:, e, :], up_b[:, e, :], ACT.Sigmoid).then_inc(gate_sig, 1)
                    split_hi((c0 + 4 + 3 * j, it * 6))
                    for e in range(2):
                        act.wait_ge(mrg_sum, n + e + 1)
                        act.activation(row(mrg_hi, n + e), up_b[:, e, :], ACT.Copy).then_inc(mrg_hi_ready, 1)

            walk(act, 2, merge)

            residual("mix_out")

            def two_chunks(name, n):
                c0 = C0[name]

                def step(it):
                    split_hi((c0 + 2, it * 2))
                    split_hi((c0 + 3, it * 2))

                walk(act, n // 2, step)

            two_chunks("mem_k", 4)
            two_chunks("mem_v", 4)

            stat(NS0["mix_out"])
            c0, t0 = C0["mem_q"], T0["mem_q"]

            def mem_heads(it):
                for e in range(2):
                    u = it * 2 + e
                    split_hi((c0 + 2 + e, it * 2))
                    act.wait_ge(ma_max, u * 2 + 2)
                    for n in range(BLK):
                        ins = act.activation(m_p[e][:, n, :], ps[:, 4 + n // 2, (n % 2) * MEM:(n % 2 + 1) * MEM], ACT.Exp,
                                             bias=small[:, 4 * e + n:4 * e + n + 1], scale=MEM_D ** -0.5,
                                             accum_out=small[:, 8 + 4 * e + n:9 + 4 * e + n])
                    ins.then_inc(ma_exp, 1)
                    act.wait_ge(ma_den, u + 1)
                    act.wait_ge(ma_exp, u + 1)
                    for n in range(BLK):
                        ins = act.activation(m_p[e][:, n, :], m_p[e][:, n, :], ACT.Copy, scale=small[:, 24 + 4 * e + n:25 + 4 * e + n])
                    ins.then_inc(ma_p, 1)
                    for d in range(2):
                        act.wait_ge(ma_o, past(u + 1))
                        act.activation(row(mo_hi, it * 4 + 2 * e + d), ps[:, 4 + d, :], ACT.Copy).then_inc(ma_hi, 1)

            walk(act, 2, mem_heads)
            residual("mem_o")
            stat(NS0["mem_o"])
            up("up0")
            residual("down0")
            stat(NS0["down0"])
            for m in range(KT):
                act.wait_ge(renorm_ready, m + 1)
                act.activation(x_hi[:, m, :], h[:, m, :], ACT.Copy, scale=pc("ffn1_0", m)).then_inc(x_hi_ready, 1)
            stat(NS0["renorm"])
            up("up1")
            residual("down1")

            act.wait_ge(chunk_done, C0["a_in"])
            act.dma_start(rope_c[:, :], cc("rope_c", S)).then_inc(rope2_landed, 16)
            act.dma_start(rope_s[:, :], cc("rope_s", S)).then_inc(rope2_landed, 16)
            act.dma_start(pc2[:, :], const_in[:, CCOL["perm2"]:CCOL["perm2"] + 2 * P + 32]).then_inc(rope2_landed, 16)
            act.dma_start(cnt[:, :, :], cc("count", 4 * S).rearrange("p (a n) -> p a n", a=4)).then_inc(rope2_landed, 16)
            stat(NS0["down1"])
            for c in range(C0["a_in"], C0["mla"]):
                split_hi((c + 2, 0))
            for i in range(5):
                act.wait_ge(acc_evac, T0["a_in"] + 4 + i + 1)
                act.activation(lat_q2[:, i, :], lat[:, i, :], ACT.Square).then_inc(lat_sq, 1)
            for i in range(2):
                act.wait_ge(lat_stat, i + 1)
                act.activation(lat_r[:, i, :], ps[:, 5 + i, :], ACT.Sqrt, bias=pc("eps", 0),
                               scale=1.0 / (Q_LORA if i == 0 else KV_LORA)).then_inc(lat_std, 1)
            for i in range(5):
                act.wait_ge(lat_n, i + 1)
                act.activation(lat_hi[:, i, :], lat[:, i, :], ACT.Copy).then_inc(lat_hi_ready, 1)
            for g in range(4):
                act.wait_ge(pool_step, 8 + g + 1)
                act.activation(pl_hi[:, g, :], u_p[:, g, PAD:PAD + S], ACT.Copy).then_inc(pl_hi_ready, 1)
            for c in range(C0["mla"], C0["a_out"]):
                split_hi((c + 2, 0))
            for g in range(4):
                act.wait_ge(acc_evac, T0["mla"] + 8 + g + 1)
                act.activation(cat_hi[0][:, g, :], u_p[:, g, PAD:PAD + S], ACT.Copy).then_inc(cat0_hi, 1)
            act.wait_ge(acc_evac, T0["a_out"])
            act.wait_ge(kr_copied, 1)
            act.activation(qh_sq[0:MLA_QK, :, :], q_h[0:MLA_QK, :, :], ACT.Square).then_inc(hd_sq, 1)
            act.activation(kh_sq[0:MLA_QK, :, :], k_h[0:MLA_QK, :, :], ACT.Square).then_inc(hd_sq, 1)
            act.wait_ge(hd_stat, 1)
            act.activation(sq[0:16, :], ps[0:16, 4, :], ACT.Sqrt, bias=par[0:16, COL["eps"]:COL["eps"] + 1],
                           scale=1.0 / MLA_QK).then_inc(hd_std, 1)

            def mla_heads(it):
                for e in range(2):
                    u = it * 2 + e
                    act.wait_ge(la_max, u * 2 + 2)
                    for n in range(BLK):
                        w = (n + 1) * P
                        ins = act.activation(l_p[:, n, 0:w], ps[:, n, 0:w], ACT.Exp, bias=small[:, 4 * e + n:4 * e + n + 1],
                                             scale=MLA_QK ** -0.5, accum_out=small[:, 8 + 4 * e + n:9 + 4 * e + n])
                    ins.then_inc(la_exp, 1)
                    act.wait_ge(la_den, u + 1)
                    act.wait_ge(la_exp, u + 1)
                    for n in range(BLK):
                        w = (n + 1) * P
                        ins = act.activation(l_p[:, n, 0:w], l_p[:, n, 0:w], ACT.Copy, scale=small[:, 24 + 4 * e + n:25 + 4 * e + n])
                    ins.then_inc(la_p, 1)
                act.wait_ge(la_o, past(it * 2 + 2))
                act.activation(row(cat_hi[1], it), ps[:, 7, :], ACT.Copy).then_inc(la_hi, 1)

            walk(act, MLA_HEADS // 2, mla_heads)
            residual("a_out")
            stat(NS0["a_out"])
            up("up2")
            residual("down2")
            stat(NS0["down2"])
            up("up3")
            residual("down3")

            stat(NS0["down3"])
            c0 = C0["c_in"]

            def conv_mix(it):
                for j in range(2):
                    for k in range(3):
                        split_hi((c0 + 2 + 3 * j + k, it * 6))
                    for e in range(2):
                        act.wait_ge(cz_ready, it * 4 + 2 * j + e + 1)
                        act.activation(row(cc_hi, it * 4 + 2 * j + e), cv[:, e, :], ACT.Copy).then_inc(cc_hi_ready, 1)

            walk(act, 2, conv_mix)
            residual("c_out")
            stat(NS0["c_out"])
            up("up4")
            residual("down4")

        @block.vector
        def _(dve):
            for at_start in (rec_ready, wa_s, wa_pT, att_ready, ma_pT, mo_ready, la_sin, la_pT, cat1_ready, mrg_ready, f_ready):
                dve.sem_inc(at_start, 1)

            def split_lo(c):
                n, reg = c
                if isinstance(reg, int) and n + reg >= CHUNKS:
                    return
                slot = n % 2
                dve.wait_ge(hi_ready, reg + (n + 1))
                dve.tensor_tensor(w_lo[slot][:, :], stage[slot][:, :], w_hi[slot][:, :].bitcast(F32),
                                  ALU.subtract).then_inc(lo_ready, 1)

            def norm_rstd(n):
                dve.wait_ge(std_ready, n + 1)
                dve.reciprocal(rstd[:, :], ssum[:, :]).then_inc(rstd_ready, 1)
                dve.wait_ge(rstd_ready, n + 1)

            def residual(name):
                r0, t0, c0, n0 = XR0[name], T0[name], C0[name], N0[name]
                gain, scale = FOLLOWED[name], SCALE[name]
                per = 6 if name.startswith("down") else 2

                def step(it):
                    for pair in range(2):
                        last = c0 + (pair + 1) * (per // 2) - 1
                        for k in range(per // 2 - 1):
                            dve.wait_ge(chunk_done, it * per + (c0 + pair * (per // 2) + k + 1))
                            split_lo((c0 + 2 + pair * (per // 2) + k, it * per))
                        dve.wait_ge(chunk_done, it * per + (last + 1))
                        for e in range(2):
                            m = 2 * pair + e
                            hm = row(h, it * 4 + m)
                            dve.scalar_tensor_tensor(hm, ps[:, (t0 + m) % 4, :], scale, hm, ALU.mult, ALU.add).then_inc(acc_evac, 1)
                        split_lo((last + 2, it * per))
                        for e in range(2):
                            m = 2 * pair + e
                            if gain:
                                dve.wait_ge(x_hi_ready, it * 4 + (r0 + m + 1))
                                dve.scalar_tensor_tensor(row(x_lo, it * 4 + m), row(h, it * 4 + m), pc(gain, it * 4 + m),
                                                         row(x_hi, it * 4 + m).bitcast(F32), ALU.mult, ALU.subtract).then_inc(x_ready, 1)

                if name == "down4":
                    step(0)
                    step(1)
                else:
                    walk(dve, 2, step)

            def up(name):
                c0, t0, f0, conv = C0[name], T0[name], FT * UPS[name], name == "up0"

                def step(it):
                    dve.wait_ge(chunk_done, it * 2 + (c0 + 1))
                    for e in range(2):
                        dve.tensor_tensor(gate_b[:, e, 1:1 + S], ps[:, (t0 + e) % 4, :], rstd[:, :], ALU.mult).then_inc(acc_evac, 1)
                    split_lo((c0 + 2, it * 2))
                    dve.wait_ge(f_ready, past(it * 2 + f0))
                    if conv:
                        for e in range(2):
                            f = it * 2 + e
                            g = gate_b[:, e, :]
                            dve.wait_ge(acc_evac, it * 4 + (t0 + e + 1))
                            dve.tensor_scalar(up_b[:, e, :], g[:, 1:1 + S], pc("conv_w1", f), pc("conv_b", f), ALU.mult, ALU.add).then_inc(conv_step, 1)
                            dve.wait_ge(conv_step, it * 6 + 3 * e + 1)
                            dve.scalar_tensor_tensor(up_b[:, e, :], g[:, 0:S], pc("conv_w0", f), up_b[:, e, :], ALU.mult, ALU.add).then_inc(conv_step, 1)
                            dve.wait_ge(conv_step, it * 6 + 3 * e + 2)
                            dve.scalar_tensor_tensor(up_b[:, e, :], g[:, 2:2 + S], pc("conv_w2", f), up_b[:, e, :], ALU.mult, ALU.add).then_inc(conv_step, 1)
                    dve.wait_ge(chunk_done, it * 2 + (c0 + 2))
                    for e in range(2):
                        if conv:
                            dve.wait_ge(silu_ready, it * 2 + (f0 + e + 1))
                        dve.tensor_tensor(up_b[:, e, :], ps[:, (t0 + 2 + e) % 4, :], rstd[:, :], ALU.mult).then_inc(acc_evac, 1)
                    split_lo((c0 + 3, it * 2))
                    for e in range(2):
                        dve.wait_ge(f_hi_ready, it * 2 + (f0 + e + 1))
                        dve.tensor_tensor(row(f_lo, it * 2 + e), up_b[:, e, :], row(f_hi, it * 2 + e).bitcast(F32), ALU.subtract).then_inc(f_ready, 1)

                walk(dve, FT // 2, step)

            dve.wait_ge(par_landed, 32)
            lb, om, t8 = small[:, 32:40], small[:, 40:48], small[:, 48:56]
            a0, a1 = pc("lb0", 0, 8), pc("lb1", 0, 8)
            step = [0]

            def link(ins, s):
                step[0] += 1
                ins.then_inc(s, 1)
                dve.wait_ge(s, step[0])

            link(dve.tensor_tensor(t8, a0, a1, ALU.max), lb_step)
            link(dve.tensor_tensor(lb, a0, t8, ALU.subtract), lb_step)
            dve.tensor_tensor(om, a1, t8, ALU.subtract).then_inc(lb_step, 1)
            step[0] += 1
            dve.wait_ge(lb_exp, 2)
            link(dve.tensor_tensor(t8, lb, om, ALU.add), lb_step)
            link(dve.reciprocal(t8, t8), lb_step)
            link(dve.tensor_tensor(lb, lb, t8, ALU.mult), lb_step)
            link(dve.tensor_scalar(om, lb, -1.0, 1.0, ALU.mult, ALU.add), lb_step)
            two_pi = 2.0 * np.pi
            p1 = 6.28125
            p2 = float(np.float32(np.round((two_pi - p1) * 2.0 ** 22) / 2.0 ** 22))
            p3 = float(np.float32(two_pi - p1 - p2))
            big = 1.5 * 2.0 ** 23
            top = 3.1415925
            dve.wait_ge(mask_landed, 16)
            link(dve.tensor_copy(ls_mask[:, :, :], mask_f[:, :, :]), lb_step)
            dve.wait_ge(pos_landed, 16)
            link(dve.tensor_copy(ang[:, :], pos_i[:, :]), lb_step)
            link(dve.tensor_scalar(ang[:, :], ang[:, :], pc("inv_freq", 0), None, ALU.mult), lb_step)
            link(dve.tensor_scalar(turns[:, :], ang[:, :], 1.0 / two_pi, None, ALU.mult), lb_step)
            link(dve.tensor_scalar(turns[:, :], turns[:, :], big, None, ALU.add), lb_step)
            link(dve.tensor_scalar(turns[:, :], turns[:, :], -big, None, ALU.add), lb_step)
            for part in (p1, p2, p3):
                link(dve.scalar_tensor_tensor(ang[:, :], turns[:, :], -part, ang[:, :], ALU.mult, ALU.add), lb_step)
            link(dve.tensor_scalar(turns[:, :], ang[:, :], float(np.pi / 2), -two_pi, ALU.is_gt, ALU.mult), lb_step)
            link(dve.scalar_tensor_tensor(turns[:, :], ang[:, :], float(np.pi / 2), turns[:, :], ALU.add, ALU.add), lb_step)
            dve.tensor_scalar(ang[:, :], ang[:, :], top, -top, ALU.min, ALU.max).then_inc(trig, 1)
            dve.tensor_scalar(turns[:, :], turns[:, :], top, -top, ALU.min, ALU.max).then_inc(trig, 1)

            split_lo((0, 0))
            split_lo((1, 0))
            norm_rstd(0)
            for k in range(KT):
                if k >= 2:
                    dve.wait_ge(x_ready, k - 1)
                dve.scalar_tensor_tensor(xn[:, k % 2, :], h[:, k, :], pc("norm_mix", k), rstd[:, :], ALU.mult, ALU.mult).then_inc(xn_ready, 1)
                if k >= 1:
                    dve.wait_ge(x_hi_ready, k)
                    dve.tensor_tensor(x_lo[:, k - 1, :], xn[:, (k - 1) % 2, :], x_hi[:, k - 1, :].bitcast(F32), ALU.subtract).then_inc(x_ready, 1)
            dve.wait_ge(x_hi_ready, KT)
            dve.tensor_tensor(x_lo[:, KT - 1, :], xn[:, (KT - 1) % 2, :], x_hi[:, KT - 1, :].bitcast(F32), ALU.subtract).then_inc(x_ready, 1)
            dve.wait_ge(rope1_ready, 2)
            dve.tensor_scalar(rope_s[:, :], rope_s[:, :], pc("rot_sign", 0), None, ALU.mult).then_inc(rope1_ready, 1)

            c0, t0 = C0["qf"], T0["qf"]

            def qf_step(it):
                for j in range(2):
                    dve.wait_ge(chunk_done, it * 2 + (c0 + j + 1))
                    for e in range(2):
                        dve.tensor_copy(row(qf, it * 4 + 2 * j + e), ps[:, (t0 + 2 * j + e) % 4, :]).then_inc(acc_evac, 1)
                    split_lo((c0 + j + 2, it * 2))

            walk(dve, 3, qf_step)
            for j in range(2):
                dve.wait_ge(chunk_done, C0["v"] + j + 1)
                for e in range(2):
                    dve.tensor_scalar(v_nat[:, 2 * e:2 * e + 2, j * PAIR:(j + 1) * PAIR],
                                      ps[:, (T0["v"] + 2 * j + e) % 4, :].rearrange("p (a n) -> p a n", a=2),
                                      HK ** -0.5, None, ALU.mult).then_inc(acc_evac, 1)
                split_lo((C0["v"] + j + 2, 0))
            dve.wait_ge(qf_act, 2)
            for i in range(8):
                dve.tensor_scalar(qf[:, 4 + i, :], qf[:, 4 + i, :], om[:, i:i + 1], lb[:, i:i + 1], ALU.mult, ALU.add).then_inc(f_ready1, 1)
            for j in range(2):
                dve.wait_ge(chunk_done, C0["g"] + j + 1)
                for e in range(2):
                    dve.tensor_copy(g_silu[:, 2 * j + e, :], ps[:, (T0["g"] + 2 * j + e) % 4, :]).then_inc(acc_evac, 1)
                split_lo((C0["g"] + j + 2, 0))
            dve.wait_ge(f_ready1, 8)

            def ls_heads(it):
                def init(e):
                    f = 2 * e + 4
                    dve.wait_ge(ls_o, past(it * 2))
                    fb, ff = row(qf, it * 4 + f), row(qf, it * 4 + f + 1)
                    q = row(qf, it * 2 + e)
                    dve.tensor_tensor(QQ[e][:, 0, :], q, fb, ALU.mult)
                    dve.tensor_tensor(QQ[e][:, 1, :], q, ff, ALU.mult)
                    dve.tensor_scalar(KK[e][:, 1, :], ff, -1.0, 1.0, ALU.mult, ALU.add).then_inc(ls_init, 1)
                    dve.tensor_scalar(KK[e][:, 0, :], fb, -1.0, 1.0, ALU.mult, ALU.add).then_inc(ls_init, 1)
                    dve.wait_ge(ls_init, it * 4 + 2 * e + 2)
                    dve.tensor_tensor(A[e][:, 3, :], KK[e][:, 0, :], KK[e][:, 1, :], ALU.add).then_inc(ls_ops, 1)

                def update(level, e):
                    w = 1 << (level - 1)
                    nb = S // (2 * w)
                    if w == 1:
                        base = rows(qf, it * 4 + (2 * e + 4), 2)
                        pitch = S
                    else:
                        t = TA[e] if level % 2 == 0 else TB[e]
                        base, pitch = t[:, :, :], (S // 2 if level % 2 == 0 else S // 4)
                    new, npitch = (TB[e], S // 4) if level % 2 == 0 else (TA[e], S // 2)
                    q4 = free(QQ[e][:, :, :], 0, [[2 * w, nb], [S + w, 2], [1, w]])
                    k4 = free(KK[e][:, :, :], w, [[2 * w, nb], [S - w, 2], [1, w]])
                    tq = free(base, 1, [[2, nb], [pitch - 1, 2], [0, w]])
                    tk = free(base, 0, [[2, nb], [pitch + 1, 2], [0, w]])
                    dve.wait_ge(ls_scores, it * 2 * LEVELS + (2 * level + e + 1))
                    dve.wait_ge(ls_diag, it * 16 + (min(2 * (level - 1), 14) + e + 1))
                    dve.tensor_tensor(q4, q4, tq, ALU.mult)
                    ins = dve.tensor_tensor(k4, k4, tk, ALU.mult)
                    if w < S // 4:
                        a = free(base, 0, [[pitch, 2], [2, nb]])
                        b = free(base, 1, [[pitch, 2], [2, nb]])
                        ins = dve.tensor_tensor(free(new[:, :, :], 0, [[npitch, 2], [1, nb]]), a, b, ALU.mult)
                    ins.then_inc(ls_ops, 1)

                for e in range(2):
                    init(e)
                for level in range(9):
                    for e in range(2):
                        a_diag = free(A[e][:, :, :], 0, [[S + P, BLK], [1, P]])
                        bank = 4 + 2 * e + level % 2
                        s4 = ps[:, bank, :].rearrange("p (a n) -> p a n", a=BLK)
                        if level == 0:
                            dve.wait_ge(ls_scores, it * 2 * LEVELS + (e + 1))
                            dve.tensor_tensor(a_diag, s4, free(ident, 0, [[0, BLK], [1, P]]), ALU.mult).then_inc(ls_diag, 1)
                            continue
                        update(level, e)
                        if level < 8:
                            dve.copy_predicated(a_diag, free(ls_mask[:, level - 1, :], 0, [[0, BLK], [1, P]]), s4).then_inc(ls_diag, 1)
                for e in range(2):
                    o = TA[e][:, :, :].rearrange("p a n -> p (a n)")
                    r = KK[e][:, 1, :]
                    dve.wait_ge(ls_std, it * 2 + e + 1)
                    dve.reciprocal(r, r).then_inc(ls_norm, 1)
                    dve.wait_ge(ls_norm, it * 8 + 4 * e + 1)
                    dve.tensor_tensor(o, ps[:, 2 + e, :], r, ALU.mult).then_inc(ls_norm, 1)
                    dve.wait_ge(ls_norm, it * 8 + 4 * e + 2)
                    dve.tensor_scalar(o, o, pc("hg_norm", it * 2 + e), None, ALU.mult).then_inc(ls_norm, 1)
                    dve.wait_ge(ls_norm, it * 8 + 4 * e + 3)
                    dve.tensor_tensor(o, o, row(g_silu, it * 2 + e), ALU.mult).then_inc(ls_norm, 1)
                for e in range(2):
                    dve.wait_ge(ls_hi, it * 2 + e + 1)
                    dve.tensor_tensor(row(rec_lo, it * 2 + e), TA[e][:, :, :].rearrange("p a n -> p (a n)"),
                                      row(rec_hi, it * 2 + e).bitcast(F32), ALU.subtract).then_inc(rec_ready, 1)

            dve.wait_ge(g_ready, 1)
            walk(dve, 2, ls_heads)

            rot = [0]

            def rotate(t, target):
                i = rot[0]
                rot[0] += 1
                dve.wait_ge(perm_done, i + 1)
                dve.wait_ge(rope1_ready, 3)
                dve.tensor_tensor(w_s[0][:, 0:2, 0:PAIR], ps[:, 4 + i % 2, :].rearrange("p (a n) -> p a n", a=2),
                                  rope_s[:, :].rearrange("p (a n) -> p a n", a=2), ALU.mult).then_inc(rot_step, 1)
                dve.tensor_tensor(target, target, rope_c[:, :], ALU.mult).then_inc(rot_step, 1)
                dve.wait_ge(rot_step, 3 * i + 2)
                dve.tensor_tensor(target.rearrange("p (a n) -> p a n", a=2), target.rearrange("p (a n) -> p a n", a=2),
                                  w_s[0][:, 0:2, 0:PAIR], ALU.add).then_inc(rot_step, 1)

            t0 = T0["kv_a"]
            dve.wait_ge(chunk_done, C0["kv_a"] + 1)
            dve.wait_ge(pad_ready, 1)
            dve.tensor_copy(k_pad[:, P:P + S], ps[:, t0 % 4, :]).then_inc(acc_evac, 1)
            dve.tensor_copy(va[:, :, :], ps[:, (t0 + 1) % 4, :].rearrange("p (a n) -> p a n", a=BLK)).then_inc(acc_evac, 1)
            split_lo((C0["kv_a"] + 2, 0))
            rotate(t0, k_pad[:, P:P + S])
            for j in range(2):
                t = T0["q_a"] + 2 * j
                dve.wait_ge(chunk_done, C0["q_a"] + j + 1)
                for e in range(2):
                    dve.tensor_copy(qa[:, 2 * j + e, :], ps[:, (t + e) % 4, :]).then_inc(acc_evac, 1)
                split_lo((C0["q_a"] + j + 2, 0))
                for e in range(2):
                    dve.wait_ge(rot_step, 3 * rot[0])
                    rotate(t + e, qa[:, 2 * j + e, :])

            dve.wait_ge(const_landed, 32)

            def wa_units(it):
                def pre(e, p):
                    u = it * 4 + 2 * e + p
                    mx, nm = small[:, 56 + 4 * p:60 + 4 * p], small[:, 4 * p:4 * p + 4]
                    dve.wait_ge(wa_scores, past(u + 1))
                    dve.scalar_tensor_tensor(w_s[p][:, :, :], ps[:, 0:4, 0:384], WIN_D ** -0.5, band[:, :, :], ALU.mult, ALU.add).then_inc(wa_s, 1)
                    dve.wait_ge(wa_s, past(u + 1))
                    dve.tensor_reduce(mx, w_s[p][:, :, :], AX.X, ALU.max).then_inc(wa_max, 1)
                    dve.wait_ge(wa_max, u * 2 + 1)
                    dve.tensor_scalar(nm, mx, pc("sink", it * 2 + e + 4 * p), -1.0, ALU.max, ALU.mult).then_inc(wa_max, 1)

                def den(e, p):
                    u = it * 4 + 2 * e + p
                    d, es, rd = small[:, 8 + 4 * p:12 + 4 * p], small[:, 16 + 4 * p:20 + 4 * p], small[:, 24 + 4 * p:28 + 4 * p]
                    dve.wait_ge(wa_exp, u + 1)
                    dve.tensor_tensor(rd, d, es, ALU.add).then_inc(wa_den, 1)
                    dve.wait_ge(wa_den, u * 2 + 1)
                    dve.reciprocal(rd, rd).then_inc(wa_den, 1)

                def turned(e, p):
                    u = it * 4 + 2 * e + p
                    dve.wait_ge(wa_turned, u + 1)
                    dve.tensor_copy(w_pT[p][:, :].rearrange("p (a n) -> p a n", a=3), ps[:, 4:7, :]).then_inc(wa_pT, 1)

                units = [(0, 0), (0, 1), (1, 0), (1, 1)]
                pre(0, 0)
                for i, (e, p) in enumerate(units):
                    den(e, p)
                    if i + 1 < 4:
                        if i >= 1:
                            dve.wait_ge(wa_turned, it * 4 + i)
                        pre(*units[i + 1])
                    turned(e, p)
                    if p == 1:
                        dve.wait_ge(wa_hi, it * 2 + e + 1)
                        dve.tensor_tensor(row(att_lo, it * 2 + e), ps[:, 7, :], row(att_hi, it * 2 + e).bitcast(F32), ALU.subtract).then_inc(att_ready, 1)

            walk(dve, 2, wa_units)

            dve.wait_ge(mem_std, 1)
            dve.reciprocal(mem_r[:, :], mem_r[:, :]).then_inc(mem_std, 1)
            dve.wait_ge(mem_std, 2)
            for k in range(KT):
                if k >= 2:
                    dve.wait_ge(mem_ready, k - 1)
                dve.scalar_tensor_tensor(mem_t[:, k % 2, :], mem_raw[:, k, :], pc("norm_mem_kv", k), mem_r[:, :], ALU.mult, ALU.mult).then_inc(mem_n, 1)
                dve.wait_ge(mem_hi_ready, k + 1)
                dve.tensor_tensor(mem_lo[:, k, :], mem_t[:, k % 2, :], mem_hi[:, k, :].bitcast(F32), ALU.subtract).then_inc(mem_ready, 1)

            c0, t0 = C0["merge"], T0["merge"]

            def merge(it):
                for j in range(2):
                    t = t0 + 8 * j
                    n = it * 4 + 2 * j
                    c = c0 + 3 * j
                    dve.wait_ge(chunk_done, it * 6 + (c + 1))
                    for e in range(2):
                        dve.tensor_copy(gate_b[:, e, 0:S], ps[:, (t + e) % 4, :]).then_inc(acc_evac, 1)
                    split_lo((c + 2, it * 6))
                    dve.wait_ge(chunk_done, it * 6 + (c + 2))
                    dve.wait_ge(mrg_ready, past(n))
                    for e in range(2):
                        dve.tensor_copy(up_b[:, e, :], ps[:, (t + 2 + e) % 4, :]).then_inc(acc_evac, 1)
                    split_lo((c + 3, it * 6))
                    dve.wait_ge(chunk_done, it * 6 + (c + 3))
                    for e in range(2):
                        dve.wait_ge(gate_sig, it * 8 + (4 * j + e + 1))
                        dve.tensor_tensor(gate_b[:, e, 0:S], gate_b[:, e, 0:S], ps[:, (t + 4 + e) % 4, :], ALU.mult).then_inc(acc_evac, 1)
                    for e in range(2):
                        dve.wait_ge(gate_sig, it * 8 + (4 * j + 2 + e + 1))
                        dve.tensor_tensor(up_b[:, e, :], up_b[:, e, :], ps[:, (t + 6 + e) % 4, :], ALU.mult).then_inc(acc_evac, 1)
                    split_lo((c + 4, it * 6))
                    for e in range(2):
                        dve.wait_ge(acc_evac, it * 16 + (t + 6 + e + 1))
                        dve.tensor_tensor(up_b[:, e, :], up_b[:, e, :], gate_b[:, e, 0:S], ALU.add).then_inc(mrg_sum, 1)
                    for e in range(2):
                        dve.wait_ge(mrg_hi_ready, n + e + 1)
                        dve.tensor_tensor(row(mrg_lo, n + e), up_b[:, e, :], row(mrg_hi, n + e).bitcast(F32), ALU.subtract).then_inc(mrg_ready, 1)

            walk(dve, 2, merge)

            residual("mix_out")

            c0, t0 = C0["mem_k"], T0["mem_k"]

            def mem_keys(it):
                for j in range(2):
                    dve.wait_ge(chunk_done, it * 2 + (c0 + j + 1))
                    for e in range(2):
                        dve.tensor_copy(row(km, it * 4 + 2 * j + e), ps[:, (t0 + 2 * j + e) % 4, 0:MEM]).then_inc(acc_evac, 1)
                    split_lo((c0 + j + 2, it * 2))

            walk(dve, 2, mem_keys)
            c1, t1 = C0["mem_v"], T0["mem_v"]

            def mem_values(it):
                for j in range(2):
                    dve.wait_ge(chunk_done, it * 2 + (c1 + j + 1))
                    for e in range(2):
                        dve.tensor_copy(vm[:, e, bass.ds(it * 2 * PAIR + j * PAIR, PAIR)], ps[:, (t1 + 2 * j + e) % 4, 0:PAIR]).then_inc(acc_evac, 1)
                    split_lo((c1 + j + 2, it * 2))

            walk(dve, 2, mem_values)

            norm_rstd(NS0["mix_out"])
            c2, t2 = C0["mem_q"], T0["mem_q"]

            def mem_heads(it):
                for e in range(2):
                    u = it * 2 + e
                    dve.wait_ge(chunk_done, it * 2 + (c2 + e + 1))
                    for d in range(2):
                        dve.tensor_tensor(qm[e][:, d, :], ps[:, (t2 + 2 * e + d) % 4, :], rstd[:, :], ALU.mult).then_inc(acc_evac, 1)
                    split_lo((c2 + e + 2, it * 2))
                    mx, nm, d4, rd = (small[:, 56 + 4 * e:60 + 4 * e], small[:, 4 * e:4 * e + 4], small[:, 8 + 4 * e:12 + 4 * e],
                                      small[:, 24 + 4 * e:28 + 4 * e])
                    dve.wait_ge(ma_scores, u + 1)
                    dve.tensor_reduce(mx, ps[:, 4:6, :].rearrange("p a (b n) -> p (a b) n", b=2), AX.X, ALU.max).then_inc(ma_max, 1)
                    dve.wait_ge(ma_max, u * 2 + 1)
                    dve.tensor_scalar(nm, mx, -(MEM_D ** -0.5), None, ALU.mult).then_inc(ma_max, 1)
                    dve.wait_ge(ma_exp, u + 1)
                    dve.reciprocal(rd, d4).then_inc(ma_den, 1)
                    dve.wait_ge(ma_turned, u + 1)
                    dve.tensor_copy(m_pT[e][:, :, :], ps[:, 6:8, :]).then_inc(ma_pT, 1)
                    for d in range(2):
                        dve.wait_ge(ma_hi, u * 2 + d + 1)
                        dve.tensor_tensor(row(mo_lo, it * 4 + 2 * e + d), ps[:, 4 + d, :], row(mo_hi, it * 4 + 2 * e + d).bitcast(F32),
                                          ALU.subtract).then_inc(mo_ready, 1)

            walk(dve, 2, mem_heads)
            residual("mem_o")
            dve.memset(gate_b[:, :, 0:1], 0.0)
            dve.memset(gate_b[:, :, S + 1:S + 2], 0.0)
            norm_rstd(NS0["mem_o"])
            up("up0")
            residual("down0")
            norm_rstd(NS0["down0"])
            for m in range(KT):
                dve.scalar_tensor_tensor(h[:, m, :], h[:, m, :], pc("final_norm", m), rstd[:, :], ALU.mult, ALU.mult).then_inc(renorm_ready, 1)
                if m >= 1:
                    dve.wait_ge(x_hi_ready, XR0["renorm"] + m)
                    dve.scalar_tensor_tensor(x_lo[:, m - 1, :], h[:, m - 1, :], pc("ffn1_0", m - 1), x_hi[:, m - 1, :].bitcast(F32),
                                             ALU.mult, ALU.subtract).then_inc(x_ready, 1)
            dve.wait_ge(x_hi_ready, XR0["renorm"] + KT)
            dve.scalar_tensor_tensor(x_lo[:, KT - 1, :], h[:, KT - 1, :], pc("ffn1_0", KT - 1), x_hi[:, KT - 1, :].bitcast(F32),
                                     ALU.mult, ALU.subtract).then_inc(x_ready, 1)
            norm_rstd(NS0["renorm"])
            up("up1")
            residual("down1")

            norm_rstd(NS0["down1"])
            c0, t0 = C0["a_in"], T0["a_in"]
            for j in range(5):
                dve.wait_ge(chunk_done, c0 + j + 1)
                for e in range(2):
                    i = 2 * j + e
                    target = u_p[:, i, PAD:PAD + S] if i < 4 else lat[:, i - 4, :]
                    dve.tensor_tensor(target, ps[:, (t0 + i) % 4, :], rstd[:, :], ALU.mult).then_inc(acc_evac, 1)
                split_lo((c0 + j + 2, 0))
            dve.wait_ge(lat_std, 2)
            dve.reciprocal(lat_r[:, :, :], lat_r[:, :, :]).then_inc(lat_std, 1)
            dve.wait_ge(lat_std, 3)
            for i in range(5):
                gain = pc("q_a_norm", i) if i < 3 else pc("kv_a_norm", i - 3)
                dve.scalar_tensor_tensor(lat[:, i, :], lat[:, i, :], gain, lat_r[:, 0 if i < 3 else 1, :], ALU.mult, ALU.mult).then_inc(lat_n, 1)
            for i in range(5):
                dve.wait_ge(lat_hi_ready, i + 1)
                dve.tensor_tensor(lat_lo[:, i, :], lat[:, i, :], lat_hi[:, i, :].bitcast(F32), ALU.subtract).then_inc(lat_ready, 1)
            for g in range(4):
                dve.wait_ge(pl_hi_ready, g + 1)
                dve.tensor_tensor(pl_lo[:, g, :], u_p[:, g, PAD:PAD + S], pl_hi[:, g, :].bitcast(F32), ALU.subtract).then_inc(pl_ready, 1)
            t0 = T0["mla"]
            done = 0
            for i in range(24):
                if i in MLA_LAST:
                    dve.wait_ge(chunk_done, C0["mla"] + MLA_LAST.index(i) + 1)
                else:
                    done += 1
                    dve.wait_ge(mla_tile, done)
                src = ps[:, (t0 + i) % 4, :]
                if i < 8:
                    ins = dve.tensor_copy(q_h[0:MLA_QK, i, :], src[0:MLA_QK])
                elif i < 12:
                    ins = dve.tensor_scalar(u_p[:, i - 8, PAD:PAD + S], src, pc("pool_scale", i - 8), None, ALU.mult)
                elif i < 16:
                    ins = dve.tensor_copy(v_mla[:, i - 12, :], src)
                else:
                    ins = dve.tensor_copy(k_h[0:MLA_NOPE, i - 16, :], src[0:MLA_NOPE])
                ins.then_inc(acc_evac, 1)
                if i in MLA_LAST:
                    split_lo((C0["mla"] + MLA_LAST.index(i) + 2, 0))
            for g in range(4):
                dve.wait_ge(cat0_hi, g + 1)
                dve.tensor_tensor(cat_lo[0][:, g, :], u_p[:, g, PAD:PAD + S], cat_hi[0][:, g, :].bitcast(F32), ALU.subtract).then_inc(cat0_ready, 1)
            dve.wait_ge(hd_std, 1)
            dve.reciprocal(sq[0:16, :], sq[0:16, :]).then_inc(hd_rstd, 1)
            dve.wait_ge(rope2_landed, 64)

            def mla_heads(it):
                def rotated(e):
                    u = it * 2 + e
                    st, t = qk_st[e][0:MLA_QK, :, :], qk_t[e][0:MLA_QK, :, :]
                    dve.wait_ge(la_spread, u + 1)
                    for i, (src, gain) in enumerate(((q_h, "q_head"), (k_h, "k_head"))):
                        dve.scalar_tensor_tensor(st[:, i, :], row(src, it * 2 + e)[0:MLA_QK], par[0:MLA_QK, COL[gain]:COL[gain] + 1],
                                                 ps[0:MLA_QK, 4 + i, :], ALU.mult, ALU.mult).then_inc(la_norm, 1)
                    dve.wait_ge(la_swap, u + 1)
                    dve.tensor_tensor(t, ps[0:MLA_QK, 4:6, :], free(rope_s[0:MLA_QK, :], 0, [[0, 2], [1, S]]), ALU.mult).then_inc(la_sin, 1)
                    dve.wait_ge(la_sin, past(u + 1))
                    dve.wait_ge(la_cos, u + 1)
                    dve.tensor_tensor(st, st, t, ALU.add).then_inc(la_rot, 1)

                rotated(0)
                for e in range(2):
                    u = it * 2 + e
                    mx, nm, d4, rd = (small[:, 56 + 4 * e:60 + 4 * e], small[:, 4 * e:4 * e + 4], small[:, 8 + 4 * e:12 + 4 * e],
                                      small[:, 24 + 4 * e:28 + 4 * e])
                    dve.wait_ge(la_scores, u + 1)
                    diag = free(ps[:, 0, :], 0, [[S + P, BLK], [1, P]])
                    dve.tensor_tensor(diag, diag, free(causal, 0, [[0, BLK], [1, P]]), ALU.add).then_inc(la_mask, 1)
                    dve.wait_ge(la_mask, u + 1)
                    for n in range(BLK):
                        ins = dve.tensor_reduce(mx[:, n:n + 1], ps[:, n, 0:(n + 1) * P], AX.X, ALU.max)
                    ins.then_inc(la_max, 1)
                    dve.wait_ge(la_max, u * 2 + 1)
                    dve.tensor_scalar(nm, mx, -(MLA_QK ** -0.5), None, ALU.mult).then_inc(la_max, 1)
                    if e == 0:
                        rotated(1)
                    dve.wait_ge(la_exp, u + 1)
                    dve.reciprocal(rd, d4).then_inc(la_den, 1)
                    dve.wait_ge(la_turned, u + 1)
                    for kb in range(BLK):
                        ins = dve.tensor_copy(l_pT[:, kb, kb * P:S], ps[:, kb, kb * P:S])
                    ins.then_inc(la_pT, 1)
                dve.wait_ge(la_hi, it + 1)
                dve.tensor_tensor(row(cat_lo[1], it), ps[:, 7, :], row(cat_hi[1], it).bitcast(F32), ALU.subtract).then_inc(cat1_ready, 1)

            walk(dve, MLA_HEADS // 2, mla_heads)
            residual("a_out")
            norm_rstd(NS0["a_out"])
            up("up2")
            residual("down2")
            norm_rstd(NS0["down2"])
            up("up3")
            residual("down3")

            norm_rstd(NS0["down3"])
            c3, t3 = C0["c_in"], T0["c_in"]
            dve.wait_ge(cu_pad, 1)

            def conv_mix(it):
                for j in range(2):
                    for k, target in enumerate((cg, cu, ch)):
                        dve.wait_ge(chunk_done, it * 6 + (c3 + 3 * j + k + 1))
                        for e in range(2):
                            o = target[:, e, 2:2 + S] if target is cu else target[:, e, :]
                            dve.tensor_tensor(o, ps[:, (t3 + 6 * j + 2 * k + e) % 4, :], rstd[:, :], ALU.mult).then_inc(acc_evac, 1)
                        split_lo((c3 + 3 * j + k + 2, it * 6))
                    for e in range(2):
                        f = it * 4 + 2 * j + e
                        dve.wait_ge(cu_ready, it * 4 + 2 * j + e + 1)
                        u, y = cu[:, e, :], cv[:, e, :]
                        dve.tensor_scalar(y, u[:, 2:2 + S], pc("cc_w2", f), None, ALU.mult).then_inc(cv_step, 1)
                        dve.wait_ge(cv_step, it * 12 + (6 * j + 3 * e + 1))
                        dve.scalar_tensor_tensor(y, u[:, 1:1 + S], pc("cc_w1", f), y, ALU.mult, ALU.add).then_inc(cv_step, 1)
                        dve.wait_ge(cv_step, it * 12 + (6 * j + 3 * e + 2))
                        dve.scalar_tensor_tensor(y, u[:, 0:S], pc("cc_w0", f), y, ALU.mult, ALU.add).then_inc(cv_step, 1)
                    for e in range(2):
                        f = it * 4 + 2 * j + e
                        dve.wait_ge(cc_hi_ready, it * 4 + 2 * j + e + 1)
                        dve.tensor_tensor(row(cc_lo, f), cv[:, e, :], row(cc_hi, f).bitcast(F32), ALU.subtract).then_inc(cc_ready, 1)

            walk(dve, 2, conv_mix)
            residual("c_out")
            norm_rstd(NS0["c_out"])
            up("up4")
            residual("down4")

        @block.gpsimd
        def _(pool):
            def sums(name):
                i = N0[name]
                base = 9 * i
                pool.wait_ge(rstd_ready, i + 1)
                pool.memset(ssum[:, :], 0.0).then_inc(ss_ready, 1)

                def step(m):
                    if name == "renorm":
                        pool.wait_ge(renorm_ready, m + 1)
                    else:
                        pool.wait_ge(acc_evac, m + (T0[name] + 1))
                    pool.wait_ge(ss_ready, m + (base + 1))
                    pool.tensor_tensor(sq[:, :], row(h, m), row(h, m), ALU.mult).then_inc(sq_ready, 1)
                    pool.wait_ge(sq_ready, m + (8 * i + 1))
                    pool.tensor_tensor(ssum[:, :], ssum[:, :], sq[:, :], ALU.add).then_inc(ss_ready, 1)

                walk(pool, KT, step)

            def up(name):
                t0, f0 = T0[name], FT * UPS[name]

                def step(it):
                    for e in range(2):
                        pool.wait_ge(silu_ready, it * 2 + (f0 + e + 1))
                        pool.wait_ge(acc_evac, it * 4 + (t0 + 2 + e + 1))
                        pool.tensor_tensor(up_b[:, e, :], up_b[:, e, :], gate_b[:, e, 1:1 + S], ALU.mult).then_inc(prod_ready, 1)

                walk(pool, FT // 2, step)

            pool.wait_ge(f_ready1, 8)

            def ls_copies(it):
                for e in range(2):
                    pool.wait_ge(ls_o, past(it * 2))
                    pool.tensor_copy(A[e][:, 2, :], row(qf, it * 2 + e)).then_inc(ls_q, 1)
                for e in range(2):
                    pool.wait_ge(ls_scores, it * 2 * LEVELS + (2 * 9 + e + 1))
                    pool.tensor_copy(QQ[e][:, 0, :].rearrange("p (b n) -> p b n", b=BLK),
                                     v_nat[:, :, bass.ds(it * 2 * HK + e * HK, HK)]).then_inc(ls_v, 1)

            walk(pool, 2, ls_copies)
            pool.wait_ge(rec_ready, past(HEADS))
            pool.memset(k_pad[:, 0:P], 0.0)
            pool.memset(k_pad[:, P + S:P + S + P], 0.0).then_inc(pad_ready, 1)
            pool.wait_ge(rot_step, 3 * 5)

            def wa_copies(it):
                for e in range(2):
                    pool.wait_ge(wa_scores, past(it * 4))
                    pool.tensor_copy(q_st[e][:, :], row(qa, it * 2 + e)).then_inc(wa_q, 1)

            walk(pool, 2, wa_copies)
            sums("mix_out")
            pool.wait_ge(acc_evac, T0["mem_q"])

            def ma_copies(it):
                for e in range(2):
                    pool.wait_ge(ma_o, past(it * 2))
                    pool.tensor_copy(v_st[e][:, :, :], vm[:, :, bass.ds(it * 2 * MEM_D + e * MEM_D, MEM_D)]).then_inc(ma_v, 1)

            walk(pool, 2, ma_copies)
            sums("mem_o")
            up("up0")
            sums("down0")
            sums("renorm")
            up("up1")
            sums("down1")

            pool.wait_ge(chunk_done, C0["a_in"])
            pool.memset(u_p[:, :, 0:PAD], 0.0)
            pool.memset(win_a[:, :, 0:PAD], 0.0).then_inc(u_pad, 1)
            pool.wait_ge(chunk_done, C0["mla"])
            pool.memset(win_b[:, :, 0:PAD], 0.0).then_inc(u_pad, 1)
            pool.wait_ge(u_pad, 2)
            pool.wait_ge(acc_evac, T0["a_in"] + 4)
            bufs = [u_p, win_a, win_b, win_a, win_b]
            for i in range(4):
                src, dst, shift = bufs[i], bufs[i + 1], 1 << i
                if i:
                    pool.wait_ge(pool_step, i)
                pool.tensor_tensor(dst[:, i:4, PAD:PAD + S], src[:, i:4, PAD:PAD + S], src[:, i:4, PAD - shift:PAD + S - shift],
                                   ALU.add).then_inc(pool_step, 1)
            pool.wait_ge(rope2_landed, 64)
            pool.wait_ge(pool_step, 4)
            for g in range(4):
                b = bufs[g + 1]
                pool.tensor_tensor(b[:, g, PAD:PAD + S], b[:, g, PAD:PAD + S], cnt[:, g, :], ALU.mult).then_inc(pool_step, 1)
            for g in range(4):
                b = bufs[g + 1]
                pool.wait_ge(pool_step, 4 + g + 1)
                pool.tensor_tensor(u_p[:, g, PAD:PAD + S], b[:, g, PAD:PAD + S], u_p[:, g, PAD:PAD + S], ALU.subtract).then_inc(pool_step, 1)
            pool.wait_ge(acc_evac, T0["a_in"] + 10)
            pool.wait_ge(pool_step, 12)
            pool.tensor_copy(k_h[MLA_NOPE:MLA_QK, :, :], free(lat[MLA_NOPE:MLA_QK, 5, :], 0, [[0, MLA_HEADS], [1, S]])).then_inc(kr_copied, 1)

            def mla_copies(it):
                for e in range(2):
                    u = it * 2 + e
                    pool.wait_ge(la_o, past(it * 2))
                    for i in range(2):
                        c = ident[0:16, bass.ds(it * 2 + e + 8 * i, 1)]
                        ins = pool.tensor_copy(sel_st[e][0:16, i, :], free(c, 0, [[0, MLA_QK]]))
                    ins.then_inc(la_sel, 1)
                    pool.tensor_copy(vl_st[e][:, :, :], v_mla[:, :, bass.ds(it * 2 * MLA_V + e * MLA_V, MLA_V)]).then_inc(la_v, 1)
                for e in range(2):
                    u = it * 2 + e
                    st = qk_st[e][0:MLA_QK, :, :]
                    pool.wait_ge(la_swap, u + 1)
                    pool.tensor_tensor(st, st, free(rope_c[0:MLA_QK, :], 0, [[0, 2], [1, S]]), ALU.mult).then_inc(la_cos, 1)

            pool.wait_ge(hd_stat, 1)
            walk(pool, MLA_HEADS // 2, mla_copies)
            sums("a_out")
            up("up2")
            sums("down2")
            up("up3")
            sums("down3")
            pool.wait_ge(chunk_done, C0["c_in"])
            pool.memset(cu[:, :, 0:2], 0.0).then_inc(cu_pad, 1)

            def conv_mix(it):
                for j in range(2):
                    for e in range(2):
                        pool.wait_ge(acc_evac, it * 12 + (T0["c_in"] + 6 * j + 4 + e + 1))
                        pool.tensor_tensor(cu[:, e, 2:2 + S], cu[:, e, 2:2 + S], ch[:, e, :], ALU.mult).then_inc(cu_ready, 1)
                    for e in range(2):
                        pool.wait_ge(cv_step, it * 12 + (6 * j + 3 * e + 3))
                        pool.tensor_tensor(cv[:, e, :], cv[:, e, :], cg[:, e, :], ALU.mult).then_inc(cz_ready, 1)

            walk(pool, 2, conv_mix)
            sums("c_out")
            up("up4")

        @block.tensor
        def _(pe):
            for at_start in (ls_o, ma_o, la_o, wa_scores):
                pe.sem_inc(at_start, 1)

            def products(out_ap, w, x, first, last):
                (wh, wl), (xh, xl) = w, x
                pe.matmul(out_ap, wh, xh, start=first, stop=False)
                pe.matmul(out_ap, wh, xl, start=False, stop=False)
                return pe.matmul(out_ap, wl, xh, start=False, stop=last)

            def w_at(c, a, n):
                return w_hi[c % 2][:, a:a + n], w_lo[c % 2][:, a:a + n]

            def begin(c, t, n, reg_c=0, reg_t=0):
                pe.wait_ge(lo_ready, reg_c + (c + 1))
                if t + n > 4:
                    pe.wait_ge(acc_evac, reg_t + (t + n - 4))

            def plain(c, t, x, ready=None, reg_c=0, reg_t=0, width=S):
                begin(c, t, 2, reg_c, reg_t)
                for k in range(KT):
                    if ready:
                        pe.wait_ge(ready[0], ready[1] + k + 1)
                    for m in range(2):
                        mm = products(ps[:, (t + m) % 4, 0:width], w_at(c, k * PAIR + m * P, P), (x[0][:, k, :], x[1][:, k, :]),
                                      k == 0, k == KT - 1)
                mm.then_inc(chunk_done, 1)

            def stat(n):
                pe.wait_ge(ss_ready, 9 * n)
                pe.matmul(ps[:, 4, :], ones, ssum[:, :], start=True, stop=True).then_inc(stat_done, 1)

            def linear(name, x, ready=None, n=None, before=None, width=S):
                c0, t0 = C0[name], T0[name]
                n = n or dict((a, b) for a, b, _ in PHASES)[name]
                plain(c0, t0, x, ready, width=width)
                if before is not None:
                    stat(before)
                plain(c0 + 1, t0 + 2, x, width=width)

                def step(it):
                    plain(c0, t0, x, None, it * 2, it * 4, width)
                    plain(c0 + 1, t0 + 2, x, None, it * 2, it * 4, width)

                if n > 2:
                    walk(pe, n // 2, step, 1)

            def down(name):
                c0, t0, f0 = C0[name], T0[name], FT * UPS["up" + name[4:]]

                def pair(j, it):
                    t = t0 + 2 * j
                    for i in range(3):
                        c = c0 + 3 * j + i
                        pe.wait_ge(lo_ready, it * 6 + (c + 1))
                        if i == 0:
                            pe.wait_ge(acc_evac, it * 4 + (t - 2))
                        for k in range(8 * i, min(8 * i + 8, FT)):
                            if j == 0:
                                pe.wait_ge(f_ready, past(f0 + k + 1))
                            for m in range(2):
                                mm = products(ps[:, (t + m) % 4, :], w_at(c, (k % 8) * PAIR + m * P, P),
                                              (f_hi[:, k, :], f_lo[:, k, :]), k == 0, k == FT - 1)
                        mm.then_inc(chunk_done, 1)

                def step(it):
                    pair(0, it)
                    pair(1, it)

                walk(pe, 2, step)

            x = (x_hi, x_lo)
            pe.wait_ge(par_landed, 32)
            for k in range(KT):
                pe.wait_ge(x_sq, k + 1)
                mm = pe.matmul(ps[:, 4, :], ones, sq8[:, k, :], start=(k == 0), stop=(k == KT - 1))
            mm.then_inc(stat_done, 1)

            linear("qf", x, (x_ready, 0))
            for j in range(2):
                c, t = C0["v"] + j, T0["v"] + 2 * j
                begin(c, t, 2)
                for b in range(BLK):
                    for k in range(KT):
                        mm = products(ps[:, (t + b // 2) % 4, (b % 2) * PAIR:(b % 2 + 1) * PAIR],
                                      (x_hi[:, k, b * P:(b + 1) * P], x_lo[:, k, b * P:(b + 1) * P]),
                                      w_at(c, k * PAIR, PAIR), k == 0, k == KT - 1)
                mm.then_inc(chunk_done, 1)
            linear("g", x)

            pe.wait_ge(acc_evac, T0["kv_a"])
            pe.wait_ge(f_ready1, 8)

            def ls_heads(it):
                for level in range(LEVELS):
                    w = 1 << (level - 1) if level else 0
                    for e in range(2):
                        bank = 4 + 2 * e + level % 2
                        if level < 2:
                            pe.wait_ge(ls_ops, it * 18 + (e + 1))
                            pe.wait_ge(rec_ready, past(it * 2))
                        else:
                            pe.wait_ge(ls_ops, it * 18 + (2 * (level - 1) + e + 1))
                            pe.wait_ge(ls_diag, it * 16 + (2 * (level - 2) + e + 1))
                        if level == 0:
                            pe.wait_ge(ls_q, it * 2 + e + 1)
                        if 1 <= level < 8:
                            pe.wait_ge(ls_kc, it * 28 + (4 * (level - 1) + 2 * (e + 1)))
                        qq = QQ[e][:, :, :]
                        if level < 8:
                            for b in range(BLK):
                                if level == 0:
                                    lhs, rhs = A[e][:, 3, b * P:(b + 1) * P], A[e][:, 2, b * P:(b + 1) * P]
                                else:
                                    dims = [[2 * w, P // (2 * w)], [S + w, 2], [1, w]]
                                    lhs, rhs = KC[e][:, b * P:(b + 1) * P], free(qq, b * P, dims)
                                mm = pe.matmul(ps[:, bank, b * P:(b + 1) * P], lhs, rhs, start=True, stop=True)
                        elif level == 8:
                            for b in range(BLK):
                                q = b + 1 if b % 2 == 0 else b - 1
                                mm = pe.matmul(ps[:, bank, b * P:(b + 1) * P], KK[e][:, 1 - b % 2, b * P:(b + 1) * P],
                                               QQ[e][:, 1 - b % 2, q * P:(q + 1) * P], start=True, stop=True)
                        else:
                            for b in range(BLK):
                                half = b // 2
                                mm = pe.matmul(ps[:, bank if half == 0 else e, (b % 2) * 256:(b % 2 + 1) * 256],
                                               KK[e][:, 1 - half, b * P:(b + 1) * P],
                                               QQ[e][:, 1 - half, (1 - half) * 256:(2 - half) * 256], start=True, stop=True)
                        mm.then_inc(ls_scores, 1)
                for e in range(2):
                    pe.wait_ge(ls_diag, it * 16 + (14 + e + 1))
                    pe.wait_ge(ls_cross, it * 6 + (2 + 2 * (e + 1)))
                    pe.wait_ge(ls_v, it * 2 + e + 1)
                    for b in range(BLK):
                        mm = pe.matmul(ps[:, 2 + e, :], QQ[e][:, 0, b * P:(b + 1) * P], A[e][:, b, :], start=(b == 0), stop=(b == BLK - 1))
                    mm.then_inc(ls_o, 1)
                for e in range(2):
                    pe.wait_ge(ls_sq, it * 2 + e + 1)
                    pe.matmul(ps[:, 4 + 2 * e, :], ones, KK[e][:, 0, :], start=True, stop=True).then_inc(ls_ss, 1)

            walk(pe, 2, ls_heads)

            c, t = C0["kv_a"], T0["kv_a"]
            begin(c, t, 2)
            for k in range(KT):
                products(ps[:, t % 4, :], w_at(c, k * PAIR, P), (x_hi[:, k, :], x_lo[:, k, :]), k == 0, k == KT - 1)
            for b in range(BLK):
                for k in range(KT):
                    mm = products(ps[:, (t + 1) % 4, b * P:(b + 1) * P], (x_hi[:, k, b * P:(b + 1) * P], x_lo[:, k, b * P:(b + 1) * P]),
                                  w_at(c, k * PAIR + P, P), k == 0, k == KT - 1)
            mm.then_inc(chunk_done, 1)

            def swap(i, tile, src):
                pe.wait_ge(acc_evac, tile + 1)
                pe.wait_ge(const_landed, 32)
                if i >= 2:
                    pe.wait_ge(rot_step, 3 * (i - 2) + 1)
                pe.matmul(ps[:, 4 + i % 2, :], perm1[:, :], src, start=True, stop=True).then_inc(perm_done, 1)

            pe.wait_ge(ls_norm, 16 - 2)
            plain(C0["q_a"], T0["q_a"], x)
            swap(0, T0["kv_a"], k_pad[:, P:P + S])
            plain(C0["q_a"] + 1, T0["q_a"] + 2, x)
            for i in range(WIN_TILES):
                swap(1 + i, T0["q_a"] + i, qa[:, i, :])
            pe.wait_ge(acc_evac, T0["merge"])
            pe.wait_ge(rot_step, 3 * 5)

            def wa_heads(it):
                def scores(e, p):
                    u = it * 4 + 2 * e + p
                    pe.wait_ge(wa_q, it * 2 + e + 1)
                    pe.wait_ge(wa_s, past(u))
                    for n in range(BLK):
                        mm = pe.matmul(ps[:, n, 0:384], q_st[e][64 * p:64 * p + 64, n * P:(n + 1) * P],
                                       k_pad[64 * p:64 * p + 64, n * P:n * P + 384], start=True, stop=True)
                    mm.then_inc(wa_scores, 1)

                def values(e, p):
                    u = it * 4 + 2 * e + p
                    pe.wait_ge(wa_p, u + 1)
                    pe.wait_ge(wa_pT, past(u))
                    for n in range(BLK):
                        for r in range(3):
                            i = 3 * n + r
                            mm = pe.transpose(ps[:, 4 + i // 4, (i % 4) * P:(i % 4 + 1) * P], w_s[p][:, n, r * P:(r + 1) * P], ident)
                    mm.then_inc(wa_turned, 1)
                    pe.wait_ge(wa_pT, past(u + 1))
                    if p == 0:
                        pe.wait_ge(att_ready, past(it * 2 + e))
                    for n in range(BLK):
                        kept = [r for r in range(3) if 0 <= n - 1 + r < BLK]
                        for r in kept:
                            mm = pe.matmul(ps[64 * p:64 * p + 64, 7, n * P:(n + 1) * P], va[:, n - 1 + r, 64 * p:64 * p + 64],
                                           w_pT[p][:, (3 * n + r) * P:(3 * n + r + 1) * P], start=(r == kept[0]), stop=(r == kept[-1]))
                    mm.then_inc(wa_o, 1)

                units = [(0, 0), (0, 1), (1, 0), (1, 1)]
                scores(0, 0)
                for i in range(4):
                    if i < 3:
                        scores(*units[i + 1])
                    values(*units[i])

            walk(pe, 2, wa_heads)

            for k in range(KT):
                pe.wait_ge(mem_sq_ready, k + 1)
                mm = pe.matmul(ps[:, 5, 0:MEM], ones, mem_sq[:, k, :], start=(k == 0), stop=(k == KT - 1))
            mm.then_inc(mem_stat, 1)

            c0, t0 = C0["merge"], T0["merge"]
            pe.wait_ge(rec_ready, past(HEADS))
            pe.wait_ge(att_ready, past(WIN_TILES))

            def merge(it):
                for j in range(2):
                    c, t = c0 + 3 * j, t0 + 8 * j
                    plain(c, t, x, None, it * 6, it * 16)
                    plain(c + 1, t + 2, x, None, it * 6, it * 16)
                    for half, src in enumerate(((rec_hi, rec_lo), (att_hi, att_lo))):
                        begin(c + 2, t + 4 + 2 * half, 2, it * 6, it * 16)
                        for k in range(4):
                            for m in range(2):
                                mm = products(ps[:, (t + 4 + 2 * half + m) % 4, :], w_at(c + 2, (4 * half + k) * PAIR + m * P, P),
                                              (src[0][:, k, :], src[1][:, k, :]), k == 0, k == 3)
                        if half == 1:
                            mm.then_inc(chunk_done, 1)

            walk(pe, 2, merge)
            linear("mix_out", (mrg_hi, mrg_lo), (mrg_ready, 1))

            linear("mem_k", (mem_hi, mem_lo), (mem_ready, 0), before=1, width=MEM)
            c1, t1 = C0["mem_v"], T0["mem_v"]

            def mem_values(it):
                for j in range(2):
                    c, t = c1 + j, t1 + 2 * j
                    begin(c, t, 2, it * 2, it * 4)
                    for e in range(2):
                        for k in range(KT):
                            mm = products(ps[:, (t + e) % 4, 0:PAIR], (mem_hi[:, k, e * P:(e + 1) * P], mem_lo[:, k, e * P:(e + 1) * P]),
                                          w_at(c, k * PAIR, PAIR), k == 0, k == KT - 1)
                    mm.then_inc(chunk_done, 1)

            walk(pe, 2, mem_values)
            c2, t2 = C0["mem_q"], T0["mem_q"]
            pe.wait_ge(x_ready, XR0["mix_out"] + KT)

            def mem_heads(it):
                for e in range(2):
                    plain(c2 + e, t2 + 2 * e, x, None, it * 2, it * 4)
                for e in range(2):
                    u = it * 2 + e
                    pe.wait_ge(acc_evac, it * 4 + (t2 + 2 * e + 2))
                    pe.wait_ge(mo_ready, past(it * 4 + 2 * e))
                    for n in range(BLK):
                        for d in range(2):
                            mm = pe.matmul(ps[:, 4 + n // 2, (n % 2) * MEM:(n % 2 + 1) * MEM], qm[e][:, d, n * P:(n + 1) * P],
                                           row(km, it * 4 + 2 * e + d), start=(d == 0), stop=(d == 1))
                    mm.then_inc(ma_scores, 1)
                    pe.wait_ge(ma_p, u + 1)
                    pe.wait_ge(ma_pT, past(u))
                    for mb in range(2):
                        for n in range(BLK):
                            mm = pe.transpose(ps[:, 6 + mb, n * P:(n + 1) * P], m_p[e][:, n, mb * P:(mb + 1) * P], ident)
                    mm.then_inc(ma_turned, 1)
                    pe.wait_ge(ma_pT, past(u + 1))
                    pe.wait_ge(ma_v, u + 1)
                    for d in range(2):
                        for mb in range(2):
                            mm = pe.matmul(ps[:, 4 + d, :], v_st[e][:, mb, d * P:(d + 1) * P], m_pT[e][:, mb, :], start=(mb == 0), stop=(mb == 1))
                    mm.then_inc(ma_o, 1)

            walk(pe, 2, mem_heads)
            linear("mem_o", (mo_hi, mo_lo), (mo_ready, 1))
            linear("up0", x, (x_ready, XR0["mem_o"]), before=2)
            down("down0")
            stat(3)
            linear("up1", x, (x_ready, XR0["renorm"]), before=4)
            down("down1")

            for j in range(5):
                plain(C0["a_in"] + j, T0["a_in"] + 2 * j, x, (x_ready, XR0["down1"]) if j == 0 else None)
                if j == 0:
                    stat(5)
            for i in range(5):
                pe.wait_ge(lat_sq, i + 1)
                mm = pe.matmul(ps[:, 5 if i < 3 else 6, :], ones, lat_q2[:, i, :], start=(i in (0, 3)), stop=(i in (2, 4)))
                if i in (2, 4):
                    mm.then_inc(lat_stat, 1)
            c, t = C0["mla"], T0["mla"]
            for i in range(24):
                chunk = c + sum(i > m for m in MLA_LAST)
                begin(chunk, t + i, 1)
                bank = (t + i) % 4
                if i < 8:
                    if i == 0:
                        pe.wait_ge(lat_ready, 5)
                    for k in range(3):
                        mm = products(ps[0:MLA_QK, bank, :], w_at(chunk, (i % 7) * 3 * MLA_QK + k * MLA_QK, MLA_QK),
                                      (lat_hi[:, k, :], lat_lo[:, k, :]), k == 0, k == 2)
                elif i < 12:
                    pe.wait_ge(pl_ready, i - 8 + 1)
                    mm = products(ps[:, bank, :], w_at(chunk, 3 * MLA_QK + (i - 8) * P, P), (pl_hi[:, i - 8, :], pl_lo[:, i - 8, :]), True, True)
                elif i < 16:
                    b = i - 12
                    for k in range(2):
                        mm = products(ps[:, bank, :], (lat_hi[:, 3 + k, b * P:(b + 1) * P], lat_lo[:, 3 + k, b * P:(b + 1) * P]),
                                      w_at(chunk, 3 * MLA_QK + 4 * P + k * S, S), k == 0, k == 1)
                else:
                    for k in range(2):
                        mm = products(ps[:, bank, :], w_at(chunk, k * S + (i - 16) * MLA_NOPE, P), (lat_hi[:, 3 + k, :], lat_lo[:, 3 + k, :]),
                                      k == 0, k == 1)
                mm.then_inc(chunk_done if i in MLA_LAST else mla_tile, 1)
            pe.wait_ge(rope2_landed, 64)
            for i in range(16):
                if i % 8 == 0:
                    pe.wait_ge(hd_sq, i // 8 + 1)
                src = qh_sq if i < 8 else kh_sq
                mm = pe.matmul(ps[0:16, 4, :], sel16[0:MLA_QK, 15 - i:31 - i], src[0:MLA_QK, i % 8, :], start=(i == 0), stop=(i == 15))
            mm.then_inc(hd_stat, 1)
            pe.wait_ge(hd_rstd, 1)
            pe.wait_ge(acc_evac, T0["a_out"])

            def mla_heads(it):
                def rotated(e):
                    u = it * 2 + e
                    pe.wait_ge(la_sel, u + 1)
                    pe.wait_ge(la_sin, past(u))
                    for i in range(2):
                        mm = pe.matmul(ps[0:MLA_QK, 4 + i, :], sel_st[e][0:16, i, :], sq[0:16, :], start=True, stop=True)
                    mm.then_inc(la_spread, 1)
                    pe.wait_ge(la_norm, u * 2 + 2)
                    for i in range(2):
                        mm = pe.matmul(ps[0:MLA_QK, 4 + i, :], perm2[0:MLA_QK, 0:MLA_QK], qk_st[e][0:MLA_QK, i, :], start=True, stop=True)
                    mm.then_inc(la_swap, 1)

                rotated(0)
                for e in range(2):
                    u = it * 2 + e
                    pe.wait_ge(la_rot, u + 1)
                    pe.wait_ge(la_pT, past(u))
                    for n in range(BLK):
                        mm = pe.matmul(ps[:, n, 0:(n + 1) * P], qk_st[e][0:MLA_QK, 0, n * P:(n + 1) * P], qk_st[e][0:MLA_QK, 1, 0:(n + 1) * P],
                                       start=True, stop=True)
                    mm.then_inc(la_scores, 1)
                    if e == 0:
                        rotated(1)
                    pe.wait_ge(la_p, u + 1)
                    for kb in range(BLK):
                        for n in range(kb, BLK):
                            mm = pe.transpose(ps[:, kb, n * P:(n + 1) * P], l_p[:, n, kb * P:(kb + 1) * P], ident)
                    mm.then_inc(la_turned, 1)
                    pe.wait_ge(la_pT, past(u + 1))
                    pe.wait_ge(la_v, u + 1)
                    if e == 0:
                        pe.wait_ge(cat1_ready, past(it))
                    for kb in range(BLK):
                        mm = pe.matmul(ps[64 * e:64 * e + 64, 7, kb * P:S], vl_st[e][:, kb, :], l_pT[:, kb, kb * P:S],
                                       start=(kb == 0), stop=(kb == BLK - 1))
                    mm.then_inc(la_o, 1)

            walk(pe, MLA_HEADS // 2, mla_heads)

            def cat(k):
                return cat_hi[k // 4][:, k % 4, :], cat_lo[k // 4][:, k % 4, :]

            def a_out(c, t, reg_c=0, reg_t=0):
                begin(c, t, 2, reg_c, reg_t)
                for k in range(KT):
                    for m in range(2):
                        mm = products(ps[:, (t + m) % 4, :], w_at(c, k * PAIR + m * P, P), cat(k), k == 0, k == KT - 1)
                mm.then_inc(chunk_done, 1)

            def a_out_step(it):
                a_out(C0["a_out"], T0["a_out"], it * 2, it * 4)
                a_out(C0["a_out"] + 1, T0["a_out"] + 2, it * 2, it * 4)

            pe.wait_ge(cat0_ready, 4)
            pe.wait_ge(cat1_ready, past(4))
            walk(pe, 2, a_out_step)
            linear("up2", x, (x_ready, XR0["a_out"]), before=6)
            down("down2")
            linear("up3", x, (x_ready, XR0["down2"]), before=7)
            down("down3")

            c3, t3 = C0["c_in"], T0["c_in"]

            def conv_mix(it):
                for k in range(6):
                    plain(c3 + k, t3 + 2 * k, x, (x_ready, XR0["down3"]) if k == 0 else None, it * 6, it * 12)

            for k in range(6):
                plain(c3 + k, t3 + 2 * k, x, (x_ready, XR0["down3"]) if k == 0 else None)
                if k == 0:
                    stat(8)
            walk(pe, 2, conv_mix, 1)
            linear("c_out", (cc_hi, cc_lo), (cc_ready, 0))
            linear("up4", x, (x_ready, XR0["c_out"]), before=9)
            down("down4")


def _cols(w, cols):
    w = w[:, cols]
    return w.reshape(w.shape[0] // P, P, w.shape[1]).transpose(1, 0, 2)


def _pairs(w):
    return [_cols(w, slice(PAIR * j, PAIR * (j + 1))).reshape(P, CW) for j in range(w.shape[1] // PAIR)]


def _up(w_gate, w_up):
    return [c for g, u in zip(_pairs(w_gate), _pairs(w_up)) for c in (g, u)]


def _padded(a):
    out = np.zeros((P, CW), np.float32)
    out[:, :a.shape[1]] = a
    return out


def _down(w):
    out = []
    for j in range(D // PAIR):
        t = _cols(w, slice(PAIR * j, PAIR * (j + 1)))
        out += [_padded(t[:, 8 * i:8 * i + 8].reshape(P, -1)) for i in range(3)]
    return out


def _columns(v):
    return v.reshape(-1, P).T


def _stream(a):
    w = a["w_in"][0]
    kw = HEADS * HK
    at = np.cumsum([0, kw, kw, kw, kw, kw, WIN_HEADS * WIN_D, WIN_KV * WIN_D, WIN_KV * WIN_D, D, D])
    q_r, fz_f, fz_b, i_r, g_r, q_a, k_a, v_a, gate_r, gate_a = [w[:, at[i]:at[i + 1]] for i in range(10)]
    order = np.concatenate([np.arange(WIN_D) + WIN_D * hd for j in range(WIN_TILES) for hd in (j, j + WIN_TILES)])
    f_heads = np.concatenate([x[:, HK * i:HK * (i + 1)] for i in range(HEADS) for x in (fz_b, fz_f)], axis=1)
    out = _pairs(q_r) + _pairs(f_heads) + _pairs(i_r) + _pairs(g_r)
    out += _pairs(np.concatenate([k_a, v_a], axis=1)) + _pairs(q_a[:, order])
    branches = _pairs(np.concatenate([a["w_br_rec"][0], a["w_br_att"][0][order]], axis=0))
    for c in zip(_pairs(gate_r), _pairs(gate_a), branches):
        out += c
    out += _pairs(a["w_mix_out"][0])
    out += _pairs(a["w_mem_kv"][0]) + _pairs(a["w_mem_q"][0]) + _pairs(a["w_mem_o"][0])
    out += _up(a["w_up"][0][:, FF:], a["w_up"][0][:, :FF]) + _down(a["w_down"][0])
    for layer in range(2):
        out += _up(a["ffn1_w_gate_2"][layer], a["ffn1_w_up_2"][layer]) + _down(a["ffn1_w_down_2"][layer])
        if layer == 0:
            wi = a["a_w_in_2"][0]
            cut = POOL + Q_LORA + KV_LORA
            rope = np.zeros((D, P), np.float32)
            rope[:, MLA_NOPE:MLA_QK] = wi[:, cut:]
            out += _pairs(np.concatenate([wi[:, :cut], rope], axis=1))
            wq = _cols(a["a_w_q_up_2"][0], slice(None)).reshape(P, 3, MLA_HEADS, MLA_QK).transpose(0, 2, 1, 3)
            wkv = _cols(a["a_w_kv_up_2"][0], slice(None)).reshape(P, 2, MLA_HEADS, MLA_NOPE + MLA_V)
            pool = a["a_w_pool_2"][0].transpose(1, 0, 2).reshape(P, POOL)
            out.append(_padded(wq[:, :7].reshape(P, -1)))
            out.append(_padded(np.concatenate([wq[:, 7].reshape(P, -1), pool, wkv[..., MLA_NOPE:].reshape(P, -1)], axis=1)))
            out.append(_padded(wkv[..., :MLA_NOPE].reshape(P, -1)))
            out += _pairs(a["a_w_out_2"][0])
        else:
            wi = a["c_w_in_2"][0]
            for c in zip(_pairs(wi[:, :D]), _pairs(wi[:, D:2 * D]), _pairs(wi[:, 2 * D:])):
                out += c
            out += _pairs(a["c_w_out_2"][0])
        out += _up(a["ffn2_w_gate_2"][layer], a["ffn2_w_up_2"][layer]) + _down(a["ffn2_w_down_2"][layer])
    assert len(out) == CHUNKS
    return np.stack(out)


def _params(a):
    par = np.zeros((P, NPAR), np.float32)

    def put(name, cols):
        par[:cols.shape[0], COL[name]:COL[name] + cols.shape[1]] = cols

    for name in ("norm_mix", "norm_mem", "norm_mem_kv", "norm_ffn", "hg_norm", "conv_b"):
        put(name, _columns(a[name][0]))
    put("final_norm", _columns(a["final_norm"]))
    for i in range(2):
        put(f"ffn1_{i}", _columns(a["ffn1_norm_2"][i]))
        put(f"mix_{i}", _columns(a["mix_norm_2"][i]))
        put(f"ffn2_{i}", _columns(a["ffn2_norm_2"][i]))
    for j in range(3):
        put(f"conv_w{j}", _columns(a["conv_w"][0, j]))
        put(f"cc_w{j}", _columns(a["c_conv_w_2"][0, j]))
    put("q_a_norm", _columns(a["a_q_a_norm_2"][0]))
    put("kv_a_norm", _columns(a["a_kv_a_norm_2"][0]))
    put("q_head", a["a_q_head_norm_2"][0][:, None])
    put("k_head", a["a_k_head_norm_2"][0][:, None])
    put("pool_scale", _columns(a["a_pool_scale_2"][0]))
    put("sink", np.broadcast_to(a["attn_sink"][0], (P, WIN_HEADS)))
    for j in range(2):
        lb = a["lower_bounds"][:, j].reshape(2, HEADS, HK)
        put(f"lb{j}", np.stack([lb[1], lb[0]], axis=1).reshape(2 * HEADS, HK).T)
    rot = WIN_D // 4
    freq = np.float32(1.0) / (np.float32(500000.0) ** (np.arange(0, rot, 2, dtype=np.float32) / np.float32(rot)))
    d = np.arange(P) % WIN_D
    put("inv_freq", np.where(d < rot, freq[d % (rot // 2)], 0.0).astype(np.float32)[:, None])
    put("rot_sign", np.where(d < rot // 2, -1.0, 1.0).astype(np.float32)[:, None])
    put("eps", np.full((P, 1), EPS, np.float32))
    return par


def _constants():
    c = np.zeros((P, NCONST), np.float32)
    i, j = np.arange(P)[:, None], np.arange(P)[None, :]

    def put(name, a):
        c[:a.shape[0], CCOL[name]:CCOL[name] + a.shape[1]] = a

    put("ident", np.eye(P))
    put("ones", np.ones((P, P)))
    band = np.zeros((P, BLK, 384))
    key = np.arange(384)[None, :] - P
    for n in range(BLK):
        ok = (np.abs(i - key) <= P) & (key + n * P >= 0) & (key + n * P < S)
        band[:, n] = np.where(ok, 0.0, NEG)
    put("band", band.reshape(P, -1))
    half = WIN_D // 8
    d = np.arange(P) % WIN_D
    partner = np.where(d < half, np.arange(P) + half, np.where(d < 2 * half, np.arange(P) - half, -1))
    put("perm1", (i == partner[None, :]).astype(np.float32))
    half2 = MLA_ROPE // 2
    f = np.arange(P)
    partner2 = np.where((f >= MLA_NOPE) & (f < MLA_NOPE + half2), f + half2,
                        np.where((f >= MLA_NOPE + half2) & (f < MLA_QK), f - half2, -1))
    put("perm2", (i == partner2[None, :]).astype(np.float32))
    put("causal", np.where(j <= i, 0.0, NEG))
    sel = np.zeros((P, 32))
    sel[:, 15] = 1.0
    put("sel", sel)
    freq = np.float32(10000.0) ** (-np.arange(0, MLA_ROPE, 2, dtype=np.float32) / np.float32(MLA_ROPE))
    ang = np.arange(S, dtype=np.float32)[:, None] * freq[None, :]
    cos, sin = np.cos(ang).T, np.sin(ang).T
    rope_c, rope_s = np.ones((P, S)), np.zeros((P, S))
    rope_c[MLA_NOPE:MLA_QK] = np.concatenate([cos, cos])
    rope_s[MLA_NOPE:MLA_QK] = np.concatenate([-sin, sin])
    put("rope_c", rope_c)
    put("rope_s", rope_s)
    count = np.stack([1.0 / np.minimum(np.arange(1, S + 1), 2 << g) for g in range(4)])
    put("levels", _level_masks().reshape(P, -1))
    put("count", np.broadcast_to(count.reshape(1, -1), (P, 4 * S)))
    return c


def _level_masks():
    s, t = np.arange(P)[:, None, None], np.arange(P)[None, None, :]
    lv = np.arange(7)[None, :, None]
    return (((s >> lv) != (t >> lv)) & ((s >> (lv + 1)) == (t >> (lv + 1)))).astype(np.float32)


def kernel(**inputs):
    from concourse import bacc
    from concourse.bass_utils import run_bass_kernel_spmd

    a = {k: np.asarray(v) for k, v in inputs.items()}
    arrays = {
        "stream": _stream(a),
        "x": np.ascontiguousarray(a["x"][0].T.reshape(KT, P, S).transpose(1, 0, 2)),
        "mem": np.ascontiguousarray(a["mem"][0].T.reshape(KT, P, MEM).transpose(1, 0, 2)),
        "positions": np.ascontiguousarray(np.broadcast_to(a["positions"].reshape(1, S), (P, S))),
        "params": _params(a),
        "constants": _constants(),
    }
    nc = bacc.Bacc("TRN2", target_bir_lowering=False, num_devices=1)
    args = [nc.dram_tensor(f"in_{k}", v.shape, mybir.dt.from_np(v.dtype), kind="ExternalInput").ap() for k, v in arrays.items()]
    out = nc.dram_tensor("out_x", (P, KT, S), F32, kind="ExternalOutput").ap()
    build(nc, *args, out)
    result = run_bass_kernel_spmd(nc, [{f"in_{k}": v for k, v in arrays.items()}], core_ids=[0])
    y = result.results[0]["out_x"]
    return np.ascontiguousarray(y.transpose(1, 0, 2).reshape(D, S).T).reshape(1, S, D)
```

```python
from contextlib import ExitStack

import numpy as np

import concourse.bass as bass
from concourse import mybir

F32 = mybir.dt.float32
F32R = mybir.dt.float32r
U8 = mybir.dt.uint8
I32 = mybir.dt.int32
ALU = mybir.AluOpType
ACT = mybir.ActivationFunctionType
AX = mybir.AxisListType

P = 128
S = 512
D = 1024
KT = D // P
MEM = 256
FF = 2816
FT = FF // P
HEADS = 4
HK = 128
BLK = S // P
WIN_HEADS, WIN_KV, WIN_D = 8, 2, 64
WIN_TILES = WIN_HEADS // 2
MEM_HEADS, MEM_D = 4, 256
MLA_HEADS, MLA_NOPE, MLA_ROPE, MLA_V = 8, 64, 32, 64
MLA_QK = MLA_NOPE + MLA_ROPE
Q_LORA, KV_LORA, POOL = 384, 256, 512
EPS = 1e-6
NEG = -1e30
CW = 2048
PAIR = 256

PHASES = [
    ("qf", 6, 12), ("v", 2, 4), ("gq", 4, 8), ("kv_a", 1, 2), ("merge", 12, 32), ("mix_out", 4, 8),
    ("mem_k", 4, 8), ("mem_v", 4, 8), ("mem_q", 4, 8), ("mem_o", 4, 8),
    ("up0", 22, 44), ("down0", 12, 8),
    ("up1", 22, 44), ("down1", 12, 8),
    ("a_in", 5, 10), ("mla", 3, 20), ("a_out", 4, 8),
    ("up2", 22, 44), ("down2", 12, 8),
    ("up3", 22, 44), ("down3", 12, 8),
    ("c_in", 12, 24), ("c_out", 4, 8),
    ("up4", 22, 44), ("down4", 12, 8),
]
C0, T0 = {}, {}
_c = _t = 0
for _name, _n, _m in PHASES:
    C0[_name], T0[_name] = _c, _t
    _c, _t = _c + _n, _t + _m
CHUNKS = _c
RESIDUALS = ["mix_out", "mem_o", "down0", "renorm", "down1", "a_out", "down2", "down3", "c_out", "down4"]
R0 = {name: KT * i for i, name in enumerate(RESIDUALS)}
N0 = {name: i for i, name in enumerate(RESIDUALS)}

COL = {}
_at = 0
for _name, _n in [("norm_mix", 8), ("norm_mem", 8), ("norm_mem_kv", 8), ("norm_ffn", 8), ("final_norm", 8),
                  ("ffn1_0", 8), ("ffn1_1", 8), ("mix_0", 8), ("mix_1", 8), ("ffn2_0", 8), ("ffn2_1", 8),
                  ("hg_norm", 4), ("conv_b", 22), ("conv_w0", 22), ("conv_w1", 22), ("conv_w2", 22),
                  ("q_a_norm", 3), ("kv_a_norm", 2), ("q_head", 1), ("k_head", 1), ("pool_scale", 4),
                  ("cc_w0", 8), ("cc_w1", 8), ("cc_w2", 8), ("sink", 8), ("lb0", 8), ("lb1", 8),
                  ("inv_freq", 1), ("rot_sign", 1), ("eps", 1)]:
    COL[_name] = _at
    _at += _n
NPAR = _at

CCOL = {}
_at = 0
for _name, _n in [("ident", P), ("ones", P), ("band", BLK * 384), ("perm1", P), ("perm2", P), ("causal", P), ("sel", 32),
                  ("rope_c", S), ("rope_s", S), ("count", 4 * S), ("levels", 7 * P)]:
    CCOL[_name] = _at
    _at += _n
NCONST = _at


def row(tensor, i):
    if isinstance(i, int):
        return tensor[:, i, :]
    return tensor[:, bass.ds(i, 1), :].rearrange("p a n -> p (a n)")


def rows(tensor, i, n):
    return tensor[:, bass.ds(i, n), :]


def past(n):
    return n + 1


def free(ap, offset, dims):
    return bass.AP(tensor=ap.tensor, offset=ap.offset + offset, ap=[ap.ap[0]] + dims)


def build(nc, stream, x_in, mem_in, pos_in, par_in, const_in, out):
    ctx = ExitStack()
    with ctx:
        TILE = 4 * S
        at = [16512]

        def take(nbytes):
            nbytes = -(-nbytes // 32) * 32
            at[0] += nbytes
            return at[0] - nbytes

        def place(name, offset, shape, dt=F32):
            return nc.alloc_sbuf_tensor_at(name, shape, dt, offset=offset)

        H_AT, XH_AT, XL_AT = take(KT * TILE), take(KT * TILE), take(KT * TILE)
        W_AT = [take(4 * CW) for _ in range(6)]
        HID = take(2 * FT * TILE)
        TMP = take(2 * 4 * (S + 8) + 2 * TILE)

        def hid(tile):
            return HID + TILE * tile

        h = place("h", H_AT, [P, KT, S])
        x_hi = place("x_hi", XH_AT, [P, KT, S], F32R)
        x_lo = place("x_lo", XL_AT, [P, KT, S], F32R)
        stage = [place(f"stage{i}", W_AT[i], [P, CW]) for i in range(2)]
        w_hi = [place(f"w_hi{i}", W_AT[2 + i], [P, CW], F32R) for i in range(2)]
        w_lo = [place(f"w_lo{i}", W_AT[4 + i], [P, CW], F32R) for i in range(2)]
        gate_b = place("gate_b", TMP, [P, 2, S + 8])
        up_b = place("up_b", TMP + 2 * 4 * (S + 8), [P, 2, S])
        rstd = place("rstd", take(TILE), [P, S])
        ssum = place("ssum", take(TILE), [P, S])
        sq = place("sq", take(TILE), [P, S])
        par = place("par", take(4 * NPAR), [P, NPAR])
        const2 = place("const2", take(4 * 2 * P), [P, 2 * P])
        ident, ones = const2[:, 0:P], const2[:, P:2 * P]
        small = place("small", take(4 * 64), [P, 64])
        ls_mask = place("ls_mask", take(7 * P), [P, 7, P], U8)
        ROPE = take(2 * TILE)
        rope_c = place("rope_c", ROPE, [P, S])
        rope_s = place("rope_s", ROPE + TILE, [P, S])
        assert at[0] <= 229344

        f_hi = place("f_hi", HID, [P, FT, S], F32R)
        f_lo = place("f_lo", hid(FT), [P, FT, S], F32R)
        qf = place("qf", hid(0), [P, 12, S])
        v_nat = place("v_nat", hid(12), [P, BLK, HEADS * HK])
        g_silu = place("g_silu", hid(16), [P, HEADS, S])
        rec_hi = place("rec_hi", hid(26), [P, HEADS, S], F32R)
        rec_lo = place("rec_lo", hid(30), [P, HEADS, S], F32R)
        att_hi = place("att_hi", hid(34), [P, WIN_TILES, S], F32R)
        att_lo = place("att_lo", hid(38), [P, WIN_TILES, S], F32R)
        mrg_hi = place("mrg_hi", hid(0), [P, KT, S], F32R)
        mrg_lo = place("mrg_lo", hid(8), [P, KT, S], F32R)
        QQ = [place(f"QQ{e}", hid(20 if e == 0 else 34), [P, 2, S]) for e in range(2)]
        KK = [place(f"KK{e}", hid(22 if e == 0 else 36), [P, 2, S]) for e in range(2)]
        TA = [place(f"TA{e}", hid(24 if e == 0 else 38), [P, 2, S // 2]) for e in range(2)]
        TB = [place(f"TB{e}", hid(25 if e == 0 else 39), [P, 2, S // 4]) for e in range(2)]
        KC = [sq, rstd]
        A = [place(f"A{e}", hid(40) if e == 0 else TMP, [P, BLK, S]) for e in range(2)]
        qa = place("qa", hid(0), [P, WIN_TILES, S])
        k_pad = place("k_pad", hid(4), [P, P + S + P])
        k_hi = place("k_hi", hid(4) + 6 * S, [P, P + S + P], F32R)
        k_lo = place("k_lo", hid(7), [P, P + S + P], F32R)
        w_s = [place(f"w_s{e}", hid(9 + 3 * e), [P, BLK, 384]) for e in range(2)]
        wT_hi = place("wT_hi", hid(15), [P, 3, S], F32R)
        wT_lo = place("wT_lo", hid(18), [P, 3, S], F32R)
        q_hi, q_lo = place("q_hi", hid(21), [P, S], F32R), place("q_lo", hid(22), [P, S], F32R)
        rot_t = place("rot_t", hid(23), [P, S])
        va_hi, va_lo = place("va_hi", hid(42), [P, BLK, P], F32R), place("va_lo", hid(43), [P, BLK, P], F32R)
        band = place("band", TMP, [P, BLK, 384])
        perm1 = place("perm1", hid(25), [P, P])
        pos_i = place("pos_i", hid(34), [P, S], I32)
        ang = place("ang", hid(35), [P, S])
        turns = place("turns", hid(36), [P, S])
        mask_f = place("mask_f", hid(38), [P, 7, P])
        sq8 = place("sq8", hid(0), [P, KT, S])
        sqx = place("sqx", XH_AT, [P, KT, S])
        xn = place("xn", hid(8), [P, 2, S])
        mem_raw = place("mem_raw", hid(16), [P, KT, MEM])
        mem_hi = place("mem_hi", hid(20), [P, KT, MEM], F32R)
        mem_lo2 = [place("mem_lo0", hid(24), [P, KT // 2, MEM], F32R), place("mem_lo1", hid(42), [P, KT // 2, MEM], F32R)]
        mem_r, mem_t = rope_c[:, 0:MEM], rope_s[:, :].rearrange("p (a n) -> p a n", a=2)

        def mem_lo(k):
            return mem_lo2[k // 4][:, k % 4]

        km_hi = place("km_hi", hid(0), [P, KT, MEM], F32R)
        km_lo = place("km_lo", hid(4), [P, KT, MEM], F32R)
        vm_hi = place("vm_hi", hid(8), [P, 2, D], F32R)
        vm_lo = place("vm_lo", hid(12), [P, 2, D], F32R)
        qm = place("qm", ROPE, [P, 2, S])
        qm_hi = [place(f"qm_hi{e}", hid(24 - 8 * e), [P, 2, S], F32R) for e in range(2)]
        qm_lo = [place(f"qm_lo{e}", hid(26 - 8 * e), [P, 2, S], F32R) for e in range(2)]
        m_p = [place(f"m_p{e}", hid(20 + 2 * e), [P, BLK, MEM]) for e in range(2)]
        pm_hi = place("pm_hi", TMP, [P, 2, S], F32R)
        pm_lo = place("pm_lo", TMP + 2 * TILE, [P, 2, S], F32R)
        mo_hi = place("mo_hi", hid(28), [P, KT, S], F32R)
        mo_lo = place("mo_lo", hid(36), [P, KT, S], F32R)
        PAD = 8
        u_p = place("u_p", hid(0), [P, 4, PAD + S])
        lat = place("lat", hid(5), [P, 6, S])
        lat_hi = place("lat_hi", hid(11), [P, 5, S], F32R)
        lat_lo = place("lat_lo", hid(16), [P, 5, S], F32R)
        lat_q2 = place("lat_q2", hid(21), [P, 5, S])
        lat_r = place("lat_r", hid(29), [P, 2, S])
        pl_hi = place("pl_hi", hid(21), [P, 4, S], F32R)
        pl_lo = place("pl_lo", hid(25), [P, 4, S], F32R)
        win = place("win", hid(36), [P, 7, PAD + S])
        cnt = place("cnt", TMP, [P, 4, S])
        v_mla = place("v_mla", hid(29), [P, BLK, MLA_HEADS * MLA_V])
        pc2 = place("pc2", hid(33), [P, 2 * P + 32])
        perm2, causal, sel16 = pc2[:, 0:P], pc2[:, P:2 * P], pc2[:, 2 * P:2 * P + 32]
        cat_hi = [place("cat_hi0", hid(36), [P, 4, S], F32R), place("cat_hi1", hid(0), [P, 4, S], F32R)]
        cat_lo = [place("cat_lo0", hid(40), [P, 4, S], F32R), place("cat_lo1", hid(4), [P, 4, S], F32R)]
        q_h = place("q_h", XH_AT, [P, MLA_HEADS, S])
        k_h = place("k_h", XL_AT, [P, MLA_HEADS, S])
        hd_t = [place(f"hd_t{e}", hid(8 + e), [P, S]) for e in range(2)]
        hd_q = [place(f"hd_q{e}", hid(34 + e), [P, S]) for e in range(2)]
        hd_r = [sq, rstd]
        hd_rhi, hd_rlo = place("hd_rhi", hid(5), [P, S], F32R), place("hd_rlo", hid(6), [P, S], F32R)
        sp_hi = [place(f"sp_hi{e}", hid(11 + e), [P, S], F32R) for e in range(2)]
        sp_lo = [place(f"sp_lo{e}", hid(13 + e), [P, S], F32R) for e in range(2)]
        ones_r = place("ones_r", hid(15), [P, MLA_QK], F32R)
        l_p = [place(f"l_p{e}", hid(8 + 3 * e), [P, 3, S]) for e in range(2)]
        l_pT = [place(f"l_pT{e}", hid(14 + 3 * e), [P, 3, S]) for e in range(2)]
        vl_st = [place(f"vl_st{e}", hid(24 + e), [P, BLK, MLA_V]) for e in range(2)]
        q_c = [place(f"q_c{e}", hid(26 + e), [P, S]) for e in range(2)]
        cc_hi = place("cc_hi", hid(0), [P, KT, S], F32R)
        cc_lo = place("cc_lo", hid(8), [P, KT, S], F32R)
        cg = place("cg", hid(16), [P, 2, S])
        cu = place("cu", hid(18), [P, 2, S + 2])
        cv = place("cv", hid(21), [P, 2, S])
        ch = place("ch", hid(23), [P, 2, S])

        ps = nc.alloc_psum_tensor("ps", [P, 8, S], F32)

        def sem(name):
            return ctx.enter_context(nc.semaphore(name))

        landed = [sem("landed0"), sem("landed1")]
        hi_ready, lo_ready = sem("hi_ready"), sem("lo_ready")
        chunk_done = sem("chunk_done")
        acc_evac = sem("acc_evac")
        x_landed = [sem("x_landed0"), sem("x_landed1")]
        par_landed, pos_landed, mask_landed = sem("par_landed"), sem("pos_landed"), sem("mask_landed")
        x_sq, x_ss, trig, rope1_ready, xn_ready = sem("x_sq"), sem("x_ss"), sem("trig"), sem("rope1_ready"), sem("xn_ready")
        lb_step, lb_exp = sem("lb_step"), sem("lb_exp")
        stat_done, std_ready, rstd_ready = sem("stat_done"), sem("std_ready"), sem("rstd_ready")
        sq_ready, ss_ready = sem("sq_ready"), sem("ss_ready")
        x_hi_ready, x_ready = sem("x_hi_ready"), sem("x_ready")
        renorm_ready = sem("renorm_ready")
        conv_step, silu_ready, prod_ready = sem("conv_step"), sem("silu_ready"), sem("prod_ready")
        f_hi_ready, f_ready = sem("f_hi_ready"), sem("f_ready")
        qf_act, f_ready1, g_ready = sem("qf_act"), sem("f_ready1"), sem("g_ready")
        ls_q, ls_init, ls_ops, ls_scores, ls_diag, ls_cross, ls_v, ls_kc, ls_qops = (sem("ls_q"), sem("ls_init"), sem("ls_ops"), sem("ls_scores"),
                                                                    sem("ls_diag"), sem("ls_cross"), sem("ls_v"), sem("ls_kc"), sem("ls_qops"))
        ls_o, ls_sq, ls_ss, ls_std, ls_norm, ls_hi, rec_ready = (sem("ls_o"), sem("ls_sq"), sem("ls_ss"), sem("ls_std"),
                                                                 sem("ls_norm"), sem("ls_hi"), sem("rec_ready"))
        const_landed, pad_ready, perm_done, rot_step = sem("const_landed"), sem("pad_ready"), sem("perm_done"), sem("rot_step")
        va_hi_ready, k_hi_ready, k_ready, wa_qhi, wT_hi_ready = (
            sem("va_hi_ready"), sem("k_hi_ready"), sem("k_ready"), sem("wa_qhi"), sem("wT_hi_ready"))
        wa_q, wa_scores, wa_s, wa_max, wa_exp, wa_den, wa_p, wa_turned, wa_pT, wa_o, wa_hi, att_ready = (
            sem("wa_q"), sem("wa_scores"), sem("wa_s"), sem("wa_max"), sem("wa_exp"), sem("wa_den"), sem("wa_p"),
            sem("wa_turned"), sem("wa_pT"), sem("wa_o"), sem("wa_hi"), sem("att_ready"))
        gate_sig, mrg_t, mrg_prod, mrg_sum, mrg_hi_ready, mrg_ready = (sem("gate_sig"), sem("mrg_t"), sem("mrg_prod"), sem("mrg_sum"),
                                                             sem("mrg_hi_ready"), sem("mrg_ready"))
        mem_landed, mem_sq_ready, mem_stat, mem_std, mem_n, mem_hi_ready, mem_ready = (
            sem("mem_landed"), sem("mem_sq_ready"), sem("mem_stat"), sem("mem_std"), sem("mem_n"), sem("mem_hi_ready"), sem("mem_ready"))
        mem_kv, qm_hi_ready, qm_ready, pm_hi_ready = (
            sem("mem_kv"), sem("qm_hi_ready"), sem("qm_ready"), sem("pm_hi_ready"))
        ma_scores, ma_max, ma_exp, ma_den, ma_p, ma_turned, ma_pT, ma_o, ma_hi, mo_ready = (
            sem("ma_scores"), sem("ma_max"), sem("ma_exp"), sem("ma_den"), sem("ma_p"), sem("ma_turned"), sem("ma_pT"),
            sem("ma_o"), sem("ma_hi"), sem("mo_ready"))
        rope2_landed, lat_sq, lat_stat, lat_std, lat_n, lat_hi_ready, lat_ready = (
            sem("rope2_landed"), sem("lat_sq"), sem("lat_stat"), sem("lat_std"), sem("lat_n"), sem("lat_hi_ready"), sem("lat_ready"))
        u_pad, pool_step, pl_hi_ready, pl_ready, mla_tile, cat0_hi, cat0_ready = (
            sem("u_pad"), sem("pool_step"), sem("pl_hi_ready"), sem("pl_ready"), sem("mla_tile"), sem("cat0_hi"), sem("cat0_ready"))
        kr_copied, hd_sq, hd_stat, hd_std, hd_rstd = sem("kr_copied"), sem("hd_sq"), sem("hd_stat"), sem("hd_std"), sem("hd_rstd")
        la_q, hd_rhi_ready, hd_rsplit, sp_ready = sem("la_q"), sem("hd_rhi_ready"), sem("hd_rsplit"), sem("sp_ready")
        la_spread, la_norm, la_swap, la_sin, la_cos, la_rot = (
            sem("la_spread"), sem("la_norm"), sem("la_swap"), sem("la_sin"), sem("la_cos"), sem("la_rot"))
        la_scores, la_mask, la_max, la_exp, la_den, la_p, la_turned, la_pT, la_v, la_o, la_hi, cat1_ready = (
            sem("la_scores"), sem("la_mask"), sem("la_max"), sem("la_exp"), sem("la_den"), sem("la_p"), sem("la_turned"),
            sem("la_pT"), sem("la_v"), sem("la_o"), sem("la_hi"), sem("cat1_ready"))
        cu_pad, cu_ready, cv_step, cz_ready, cc_hi_ready, cc_ready = (
            sem("cu_pad"), sem("cu_ready"), sem("cv_step"), sem("cz_ready"), sem("cc_hi_ready"), sem("cc_ready"))
        out_done = sem("out_done")

        def pc(name, i, n=1):
            k = COL[name] + i
            return par[:, k:k + n] if isinstance(k, int) else par[:, bass.ds(k, n)]

        def cc(name, n):
            return const_in[:, CCOL[name]:CCOL[name] + n]

        UPS = {f"up{i}": i for i in range(5)}
        FOLLOWED = {
            "mix_out": "norm_mem", "mem_o": "norm_ffn", "down0": None, "renorm": "ffn1_0", "down1": "mix_0",
            "a_out": "ffn2_0", "down2": "ffn1_1", "down3": "mix_1", "c_out": "ffn2_1", "down4": None}
        SCALE = {"mix_out": 1.0, "mem_o": 1.0, "down0": 1.0, "down1": 0.5, "a_out": 1.0, "down2": 0.5, "down3": 0.5,
                 "c_out": 1.0, "down4": 0.5}
        XR0, _n = {}, 0
        for name in RESIDUALS:
            XR0[name] = KT + _n
            _n += KT if FOLLOWED[name] else 0
        NS0 = {name: 1 + i for i, name in enumerate(n for n in RESIDUALS if n != "down4")}

        MLA_LAST = [6, 11, 19]
        CAUSAL_AT = {4: (0, 0), 3: (1, 0), 1: (1, 3 * P), 2: (2, 0)}
        TURNED_AT = {0: (2, 0), 1: (0, 0), 2: (1, 0), 3: (2, 2 * P)}
        TURNED_OF = {b: range(max(b - 1, 0), min(b + 2, BLK)) for b in range(BLK)}
        LEVELS = 10

        def ls_level(it, level, e):
            w = 1 << (level - 1)
            odd, even = (TA[e], S // 2), (TB[e], S // 4)
            new, old = (odd, even) if level % 2 else (even, odd)
            base, pitch = (rows(qf, it * 4 + (2 * e + 4), 2), S) if w == 1 else (old[0][:, :, :], old[1])
            return w, S // (2 * w), base, pitch, new

        def walk(engine, n, body, first=0):
            with engine.Fori(first, n) as it:
                body(it)

        block = ctx.enter_context(nc.Block())

        @block.sync
        def _(sp):
            for i in range(4):
                sp.dma_start(h[:, 2 * i:2 * i + 2, :], x_in[:, 2 * i:2 * i + 2, :]).then_inc(x_landed[i // 2], 16)

            def load(c, slot):
                src = stream[c] if isinstance(c, int) else stream[bass.ds(c, 1)].rearrange("a p n -> p (a n)")
                sp.dma_start(stage[slot][:, :], src).then_inc(landed[slot], 16)

            load(0, 0)
            load(1, 1)

            def two(i):
                for s in range(2):
                    sp.wait_ge(lo_ready, i * 2 + s - 1)
                    load(i * 2 + s, s)

            walk(sp, CHUNKS // 2, two, 1)
            if CHUNKS % 2:
                sp.wait_ge(lo_ready, CHUNKS - 2)
                load(CHUNKS - 1, (CHUNKS - 1) % 2)

            for m in range(KT):
                sp.wait_ge(acc_evac, T0["down4"] + m + 1)
                sp.dma_start(out[:, m, :], h[:, m, :]).then_inc(out_done, 16)
            sp.wait_ge(out_done, 16 * KT)

        @block.scalar
        def _(act):
            def split_hi(c):
                n, reg = c
                if isinstance(reg, int) and n + reg >= CHUNKS:
                    return
                slot = n % 2
                act.wait_ge(landed[slot], reg * 8 + 16 * (n // 2 + 1))
                if n >= 2:
                    act.wait_ge(chunk_done, reg + (n - 1))
                act.activation(w_hi[slot][:, :], stage[slot][:, :], ACT.Copy).then_inc(hi_ready, 1)

            def stat(n, bias_scale=1.0 / D):
                act.wait_ge(stat_done, n + 1)
                act.activation(ssum[:, :], ps[:, 4, :], ACT.Sqrt, bias=pc("eps", 0), scale=bias_scale).then_inc(std_ready, 1)

            def residual(name):
                r0, t0, c0 = XR0[name], T0[name], C0[name]
                gain = FOLLOWED[name]
                per = 6 if name.startswith("down") else 2

                def step(it):
                    for pair in range(2):
                        for k in range(per // 2):
                            split_hi((c0 + 2 + pair * (per // 2) + k, it * per))
                        for e in range(2):
                            m = 2 * pair + e
                            if gain:
                                act.wait_ge(acc_evac, it * 4 + t0 + m + 1)
                                act.activation(row(x_hi, it * 4 + m), row(h, it * 4 + m), ACT.Copy,
                                               scale=pc(gain, it * 4 + m)).then_inc(x_hi_ready, 1)
                            elif name == "down0":
                                act.wait_ge(acc_evac, it * 4 + t0 + m + 1)
                                act.activation(row(sqx, it * 4 + m), row(h, it * 4 + m), ACT.Square).then_inc(x_sq, 1)

                if name == "down4":
                    step(0)
                    step(1)
                else:
                    walk(act, 2, step)

            def up(name):
                c0, t0, f0, conv = C0[name], T0[name], FT * UPS[name], name == "up0"

                def step(it):
                    split_hi((c0 + 2, it * 2))
                    for e in range(2):
                        if conv:
                            act.wait_ge(conv_step, it * 6 + 3 * e + 3)
                            act.activation(gate_b[:, e, 1:1 + S], up_b[:, e, :], ACT.Silu).then_inc(silu_ready, 1)
                        else:
                            act.wait_ge(acc_evac, it * 4 + t0 + e + 1)
                            act.activation(gate_b[:, e, 1:1 + S], gate_b[:, e, 1:1 + S], ACT.Silu).then_inc(silu_ready, 1)
                    split_hi((c0 + 3, it * 2))
                    for e in range(2):
                        act.wait_ge(prod_ready, it * 2 + f0 + e + 1)
                        act.activation(row(f_hi, it * 2 + e), up_b[:, e, :], ACT.Copy).then_inc(f_hi_ready, 1)

                walk(act, FT // 2, step)

            act.dma_start(par[:, :], par_in).then_inc(par_landed, 16)
            act.dma_start(const2[:, :], const_in[:, 0:2 * P]).then_inc(par_landed, 16)
            act.dma_start(pos_i[:, :], pos_in).then_inc(pos_landed, 16)
            act.dma_start(mask_f[:, :, :], cc("levels", 7 * P).rearrange("p (a n) -> p a n", a=7)).then_inc(mask_landed, 16)
            for k in range(KT):
                if k % 4 == 0:
                    act.wait_ge(x_landed[k // 4], 32)
                act.activation(sq8[:, k, :], h[:, k, :], ACT.Square).then_inc(x_sq, 1)
            split_hi((0, 0))
            act.wait_ge(par_landed, 32)
            stat(0)
            split_hi((1, 0))
            for k in range(KT):
                act.wait_ge(xn_ready, k + 1)
                act.activation(x_hi[:, k, :], xn[:, k % 2, :], ACT.Copy).then_inc(x_hi_ready, 1)
            act.wait_ge(lb_step, 3)
            act.activation(small[:, 32:40], small[:, 32:40], ACT.Exp).then_inc(lb_exp, 1)
            act.activation(small[:, 40:48], small[:, 40:48], ACT.Exp).then_inc(lb_exp, 1)

            c0 = C0["qf"]

            def qf_step(it):
                split_hi((c0 + 2, it * 2))
                split_hi((c0 + 3, it * 2))

            walk(act, 3, qf_step)
            act.wait_ge(acc_evac, T0["qf"] + 4)
            act.activation(qf[:, 0:4, :], qf[:, 0:4, :], ACT.Silu).then_inc(qf_act, 1)
            act.wait_ge(acc_evac, T0["qf"] + 12)
            act.activation(qf[:, 4:12, :], qf[:, 4:12, :], ACT.Sigmoid).then_inc(qf_act, 1)
            for c in range(C0["v"], C0["gq"]):
                split_hi((c + 2, 0))
            act.wait_ge(trig, 2)
            act.activation(rope_s[:, :], ang[:, :], ACT.Sin).then_inc(rope1_ready, 1)
            act.activation(rope_c[:, :], turns[:, :], ACT.Sin).then_inc(rope1_ready, 1)

            def ls_tail(it):
                for level in range(1, 8):
                    w = 1 << (level - 1)
                    for e in range(2):
                        act.wait_ge(ls_ops, it * 18 + (max(2 * (level - 1), 0) + e + 1))
                        if level > 1:
                            act.wait_ge(ls_scores, it * 2 * LEVELS + (2 * (level - 1) + e + 1))
                        else:
                            act.wait_ge(ls_o, past(it * 2))
                        for half in range(2):
                            act.activation(free(KC[e][:, :], half * w, [[2 * w, S // (2 * w)], [1, w]]),
                                           free(KK[e][:, :, :], half * w + (1 - half) * S, [[2 * w, S // (2 * w)], [1, w]]),
                                           ACT.Copy).then_inc(ls_kc, 1)
                    if level == 2:
                        split_hi((C0["gq"] + 2, it * 2))
                        act.wait_ge(acc_evac, it * 4 + (T0["gq"] + 2))
                        act.activation(rows(g_silu, it * 2, 2), rows(g_silu, it * 2, 2), ACT.Silu).then_inc(g_ready, 1)
                for e in range(2):
                    a = A[e][:, :, :]
                    act.wait_ge(ls_scores, it * 2 * LEVELS + 2 * 8 + e + 1)
                    act.activation(free(a, P, [[1280, 2], [384, 2], [1, P]]),
                                   ps[:, 4 + 2 * e, :].rearrange("p (a b n) -> p a b n", a=2, b=2), ACT.Copy).then_inc(ls_cross, 1)
                for e in range(2):
                    act.wait_ge(ls_scores, it * 2 * LEVELS + 2 * 9 + e + 1)
                    act.activation(A[e][:, 0:2, 256:512], ps[:, 5 + 2 * e, :].rearrange("p (a n) -> p a n", a=2),
                                   ACT.Copy).then_inc(ls_cross, 1)
                    act.activation(A[e][:, 2:4, 0:256], ps[:, e, :].rearrange("p (a n) -> p a n", a=2),
                                   ACT.Copy).then_inc(ls_cross, 1)
                for e in range(2):
                    act.wait_ge(ls_o, past(it * 2 + e + 1))
                    act.activation(KK[e][:, 0, :], ps[:, 5 + 2 * e, :], ACT.Square).then_inc(ls_sq, 1)
                for e in range(2):
                    act.wait_ge(ls_ss, it * 2 + e + 1)
                    act.activation(KK[e][:, 1, :], ps[:, 4 + 2 * e, :], ACT.Sqrt, bias=pc("eps", 0), scale=1.0 / HK).then_inc(ls_std, 1)
                split_hi((C0["gq"] + 3, it * 2))
                for e in range(2):
                    act.wait_ge(ls_norm, it * 8 + 4 * e + 4)
                    act.activation(row(rec_hi, it * 2 + e), TA[e][:, :, :].rearrange("p a n -> p (a n)"), ACT.Copy).then_inc(ls_hi, 1)

            walk(act, 2, ls_tail)

            act.wait_ge(rec_ready, past(HEADS))
            act.dma_start(band[:, :, :], cc("band", 4 * 384).rearrange("p (a n) -> p a n", a=4)).then_inc(const_landed, 16)
            act.dma_start(perm1[:, :], cc("perm1", P)).then_inc(const_landed, 16)
            act.wait_ge(chunk_done, C0["kv_a"] + 1)
            act.activation(va_hi[:, :, :], ps[:, (T0["kv_a"] + 1) % 4, :].rearrange("p (a n) -> p a n", a=BLK), ACT.Copy).then_inc(va_hi_ready, 1)
            split_hi((C0["kv_a"] + 2, 0))

            def q_round(j):
                act.activation(q_hi[:, :], row(qa, j), ACT.Copy).then_inc(wa_qhi, 1)

            def exponentials(j, p):
                act.wait_ge(wa_max, j * 4 + (2 * p + 2))
                for n in range(BLK):
                    act.activation(w_s[p][:, n, :], w_s[p][:, n, :], ACT.Exp, bias=small[:, 4 * p + n:4 * p + n + 1],
                                   accum_out=small[:, 8 + 4 * p + n:9 + 4 * p + n])
                act.activation(small[:, 16 + 4 * p:20 + 4 * p], small[:, 4 * p:4 * p + 4], ACT.Exp,
                               bias=pc("sink", j + 4 * p)).then_inc(wa_exp, 1)

            def divided(j, p):
                act.wait_ge(wa_den, j * 4 + (2 * p + 2))
                act.wait_ge(wa_exp, j * 2 + (p + 1))
                for n in range(BLK):
                    ins = act.activation(w_s[p][:, n, :], w_s[p][:, n, :], ACT.Copy, scale=small[:, 24 + 4 * p + n:25 + 4 * p + n])
                ins.then_inc(wa_p, 1)

            def wa_tile(j, last=False):
                if not last:
                    act.wait_ge(wa_scores, past(j * 2 + 2))
                    q_round(j + 1)
                for p in range(2):
                    half = slice(64 * p, 64 * p + 64)
                    act.wait_ge(wa_turned, j * 2 + (p + 1))
                    act.activation(wT_hi[:, 0:2, 0:384], ps[:, 4:6, 0:384], ACT.Copy)
                    act.activation(wT_hi[:, 2, :], ps[:, 6, :], ACT.Copy).then_inc(wT_hi_ready, 1)
                    if not (last and p == 1):
                        exponentials(j + p, 1 - p)
                        divided(j + p, 1 - p)
                    act.wait_ge(wa_o, j * 2 + (p + 1))
                    act.activation(row(att_hi, j)[half], ps[half, 7, :], ACT.Copy).then_inc(wa_hi, 1)

            act.wait_ge(rot_step, 3)
            act.activation(k_hi[:, :], k_pad[:, :], ACT.Copy).then_inc(k_hi_ready, 1)
            act.wait_ge(rot_step, 3 * 2)
            q_round(0)
            exponentials(0, 0)
            divided(0, 0)
            act.wait_ge(rot_step, 3 * 5)
            walk(act, WIN_TILES - 1, wa_tile)
            wa_tile(WIN_TILES - 1, last=True)

            act.wait_ge(att_ready, past(2 * WIN_TILES))
            act.dma_start(mem_raw[:, :, :], mem_in).then_inc(mem_landed, 16)
            c0, t0 = C0["merge"], T0["merge"]

            def merge(it):
                for j in range(2):
                    t = it * 16 + (t0 + 8 * j)
                    n = it * 4 + 2 * j
                    split_hi((c0 + 2 + 3 * j, it * 6))
                    for e in range(2):
                        act.wait_ge(acc_evac, t + e + 1)
                        act.activation(gate_b[:, e, 0:S], gate_b[:, e, 0:S], ACT.Sigmoid).then_inc(gate_sig, 1)
                    split_hi((c0 + 3 + 3 * j, it * 6))
                    for e in range(2):
                        act.wait_ge(acc_evac, t + e + 3)
                        act.activation(up_b[:, e, :], up_b[:, e, :], ACT.Sigmoid).then_inc(gate_sig, 1)
                    split_hi((c0 + 4 + 3 * j, it * 6))
                    for e in range(2):
                        act.wait_ge(mrg_sum, n + e + 1)
                        act.activation(row(mrg_hi, n + e), up_b[:, e, :], ACT.Copy).then_inc(mrg_hi_ready, 1)

            walk(act, 2, merge)
            act.wait_ge(mem_stat, 1)
            act.activation(mem_r, ps[:, 5, 0:MEM], ACT.Sqrt, bias=pc("eps", 0), scale=1.0 / D).then_inc(mem_std, 1)
            for k in range(KT):
                act.wait_ge(mem_n, k + 1)
                act.activation(mem_hi[:, k, :], mem_t[:, k % 2, :], ACT.Copy).then_inc(mem_hi_ready, 1)

            residual("mix_out")

            def mem_chunks(name, to):
                c0, t0, n0 = C0[name], T0[name], 0 if name == "mem_k" else 4

                def step(it):
                    for j in range(2):
                        split_hi((c0 + j + 2, it * 2))
                        act.wait_ge(chunk_done, it * 2 + (c0 + j + 1))
                        b = (t0 + 2 * j) % 4
                        act.activation(to(it * 2 + j), ps[:, b:b + 2, 0:MEM], ACT.Copy).then_inc(mem_kv, 1)

                walk(act, 2, step)

            mem_chunks("mem_k", lambda i: rows(km_hi, i * 2, 2))
            mem_chunks("mem_v", lambda i: vm_hi[:, :, bass.ds(i * PAIR, PAIR)])

            stat(NS0["mix_out"])
            c0 = C0["mem_q"]

            def q_rounded(u):
                act.wait_ge(acc_evac, T0["mem_q"] + 2 * u + 2)
                if u >= 2:
                    act.wait_ge(ma_scores, u - 1)
                act.activation(qm_hi[u % 2][:, :, :], qm[:, :, :], ACT.Copy).then_inc(qm_hi_ready, 1)

            def exponentials(u):
                e = u % 2
                act.wait_ge(ma_max, u * 2 + 2)
                for n in range(BLK):
                    ins = act.activation(m_p[e][:, n, :], ps[:, 4 + n // 2, (n % 2) * MEM:(n % 2 + 1) * MEM], ACT.Exp,
                                         bias=small[:, 4 * e + n:4 * e + n + 1], scale=MEM_D ** -0.5,
                                         accum_out=small[:, 8 + 4 * e + n:9 + 4 * e + n])
                ins.then_inc(ma_exp, 1)

            def divided(u):
                e = u % 2
                act.wait_ge(ma_den, u + 1)
                act.wait_ge(ma_exp, u + 1)
                for n in range(BLK):
                    ins = act.activation(m_p[e][:, n, :], m_p[e][:, n, :], ACT.Copy, scale=small[:, 24 + 4 * e + n:25 + 4 * e + n])
                ins.then_inc(ma_p, 1)

            for u in range(2):
                q_rounded(u)
                split_hi((c0 + 2 + u, 0))
            exponentials(0)
            divided(0)
            for u in range(MEM_HEADS):
                more = u + 1 < MEM_HEADS
                act.wait_ge(ma_turned, u + 1)
                act.activation(pm_hi[:, :, :], ps[:, 6:8, :], ACT.Copy).then_inc(pm_hi_ready, 1)
                if u + 2 < MEM_HEADS:
                    q_rounded(u + 2)
                if more:
                    exponentials(u + 1)
                act.wait_ge(ma_o, u + 1)
                act.activation(mo_hi[:, 2 * u:2 * u + 2, :], ps[:, 6:8, :], ACT.Copy).then_inc(ma_hi, 1)
                if more:
                    divided(u + 1)
                if u + 2 < MEM_HEADS:
                    split_hi((c0 + 4 + u, 0))

            residual("mem_o")
            stat(NS0["mem_o"])
            up("up0")
            residual("down0")
            stat(NS0["down0"])
            for m in range(KT):
                act.wait_ge(renorm_ready, m + 1)
                act.activation(sq8[:, m, :], h[:, m, :], ACT.Square).then_inc(x_sq, 1)
                act.activation(x_hi[:, m, :], h[:, m, :], ACT.Copy, scale=pc("ffn1_0", m)).then_inc(x_hi_ready, 1)
            stat(NS0["renorm"])
            up("up1")
            residual("down1")

            act.wait_ge(chunk_done, C0["a_in"])
            act.dma_start(rope_c[:, :], cc("rope_c", S)).then_inc(rope2_landed, 16)
            act.dma_start(rope_s[:, :], cc("rope_s", S)).then_inc(rope2_landed, 16)
            act.dma_start(pc2[:, :], const_in[:, CCOL["perm2"]:CCOL["perm2"] + 2 * P + 32]).then_inc(rope2_landed, 16)
            act.dma_start(cnt[:, :, :], cc("count", 4 * S).rearrange("p (a n) -> p a n", a=4)).then_inc(rope2_landed, 16)
            stat(NS0["down1"])
            c0 = C0["a_in"]
            for j in range(3):
                split_hi((c0 + j + 2, 0))
            for i in range(5):
                act.wait_ge(acc_evac, T0["a_in"] + i + 1)
                act.activation(lat_q2[:, i, :], lat[:, i, :], ACT.Square).then_inc(lat_sq, 1)
            split_hi((c0 + 5, 0))
            for i in range(2):
                act.wait_ge(lat_stat, i + 1)
                act.activation(lat_r[:, i, :], ps[:, 5 + i, :], ACT.Sqrt, bias=pc("eps", 0),
                               scale=1.0 / (Q_LORA if i == 0 else KV_LORA)).then_inc(lat_std, 1)
            for i in range(5):
                act.wait_ge(lat_n, i + 1)
                act.activation(lat_hi[:, i, :], lat[:, i, :], ACT.Copy).then_inc(lat_hi_ready, 1)
            split_hi((c0 + 6, 0))
            act.wait_ge(chunk_done, C0["mla"])
            act.wait_ge(acc_evac, T0["a_in"] + 6)
            act.activation(k_h[MLA_NOPE:MLA_QK, :, :], free(lat[MLA_NOPE:MLA_QK, 5, :], 0, [[0, MLA_HEADS], [1, S]]),
                           ACT.Copy).then_inc(kr_copied, 1)
            split_hi((c0 + 7, 0))

            def head_rows(w):
                act.wait_ge(hd_rstd, w + 1)
                if w:
                    act.wait_ge(sp_ready, 8)
                act.activation(hd_rhi[0:8, :], hd_r[w][0:8, :], ACT.Copy).then_inc(hd_rhi_ready, 1)
                act.wait_ge(hd_rsplit, w + 1)

                def heads(it):
                    for e in range(2):
                        own = ident[0:8, bass.ds(it * 2 + e, 1)]
                        act.wait_ge(la_spread, past(it * 2 + 8 * w))
                        act.activation(sp_hi[e][0:8, :], hd_rhi[0:8, :].bitcast(F32), ACT.Copy, scale=own)
                        act.activation(sp_lo[e][0:8, :], hd_rlo[0:8, :].bitcast(F32), ACT.Copy, scale=own).then_inc(sp_ready, 1)

                walk(act, MLA_HEADS // 2, heads)

            for w, src in enumerate((q_h, k_h)):
                for i in range(MLA_HEADS):
                    act.wait_ge(acc_evac, T0["mla"] + (i + 1 if w == 0 else 12 + i // 2 + 1))
                    if w == 1:
                        act.wait_ge(kr_copied, 1)
                    if 8 * w + i >= 2:
                        act.wait_ge(hd_stat, 8 * w + i - 1)
                    act.activation(hd_q[i % 2][0:MLA_QK, :], src[0:MLA_QK, i, :], ACT.Square).then_inc(hd_sq, 1)
                act.wait_ge(hd_stat, 8 * w + 8)
                act.activation(hd_r[w][0:8, :], ps[0:8, 4 + w, :], ACT.Sqrt, bias=par[0:8, COL["eps"]:COL["eps"] + 1],
                               scale=1.0 / MLA_QK).then_inc(hd_std, 1)
                if w == 0:
                    for g in range(4):
                        act.wait_ge(pool_step, 8 + g + 1)
                        act.activation(pl_hi[:, g, :], u_p[:, g, PAD:PAD + S], ACT.Copy).then_inc(pl_hi_ready, 1)
            act.wait_ge(acc_evac, T0["mla"] + 16)
            act.activation(ones_r[0:8, :], ones[0:8, 0:MLA_QK], ACT.Copy)
            head_rows(0)
            head_rows(1)
            split_hi((c0 + 8, 0))
            split_hi((c0 + 9, 0))
            for g in range(4):
                act.wait_ge(acc_evac, T0["mla"] + 16 + g + 1)
                act.activation(cat_hi[0][:, g, :], u_p[:, g, PAD:PAD + S], ACT.Copy).then_inc(cat0_hi, 1)

            def exponentials(v, e):
                act.wait_ge(la_max, 2 * v + 2)
                for n in range(BLK):
                    b, c = CAUSAL_AT[n + 1]
                    w = (n + 1) * P
                    ins = act.activation(l_p[e][:, b, c:c + w], ps[:, 3 * e + b, c:c + w], ACT.Exp, bias=small[:, 4 * e + n:4 * e + n + 1],
                                         scale=MLA_QK ** -0.5, accum_out=small[:, 8 + 4 * e + n:9 + 4 * e + n])
                ins.then_inc(la_exp, 1)

            def divided(v, e):
                act.wait_ge(la_den, v + 1)
                act.wait_ge(la_exp, v + 1)
                for n in range(BLK):
                    b, c = CAUSAL_AT[n + 1]
                    w = (n + 1) * P
                    ins = act.activation(l_p[e][:, b, c:c + w], l_p[e][:, b, c:c + w], ACT.Copy, scale=small[:, 24 + 4 * e + n:25 + 4 * e + n])
                ins.then_inc(la_p, 1)

            def out_hi(it, e):
                act.wait_ge(la_o, it * 2 + (e + 1))
                act.activation(row(cat_hi[1], it)[64 * e:64 * e + 64], ps[64 * e:64 * e + 64, 6 + e, :], ACT.Copy).then_inc(la_hi, 1)

            def mla_heads(it, first=False, last=False):
                for e in range(2):
                    if not (first and e == 0):
                        out_hi(it - 1 if e == 0 else it, 1 - e)
                    if not (last and e == 1):
                        divided(it * 2 + (e + 1), 1 - e)
                    if not last:
                        exponentials(it * 2 + (e + 2), e)

            exponentials(0, 0)
            divided(0, 0)
            exponentials(1, 1)
            mla_heads(0, first=True)
            walk(act, MLA_HEADS // 2 - 1, mla_heads, 1)
            mla_heads(MLA_HEADS // 2 - 1, last=True)
            out_hi(MLA_HEADS // 2 - 1, 1)
            residual("a_out")
            stat(NS0["a_out"])
            up("up2")
            residual("down2")
            stat(NS0["down2"])
            up("up3")
            residual("down3")

            stat(NS0["down3"])
            c0 = C0["c_in"]

            def conv_mix(it):
                for j in range(2):
                    for k in range(3):
                        split_hi((c0 + 2 + 3 * j + k, it * 6))
                    for e in range(2):
                        act.wait_ge(cz_ready, it * 4 + 2 * j + e + 1)
                        act.activation(row(cc_hi, it * 4 + 2 * j + e), cv[:, e, :], ACT.Copy).then_inc(cc_hi_ready, 1)

            walk(act, 2, conv_mix)
            residual("c_out")
            stat(NS0["c_out"])
            up("up4")
            residual("down4")

        @block.vector
        def _(dve):
            for at_start in (rec_ready, wa_s, wa_pT, att_ready, mo_ready, la_sin, cat1_ready, mrg_ready, f_ready):
                dve.sem_inc(at_start, 1)

            def split_lo(c):
                n, reg = c
                if isinstance(reg, int) and n + reg >= CHUNKS:
                    return
                slot = n % 2
                dve.wait_ge(hi_ready, reg + (n + 1))
                dve.tensor_tensor(w_lo[slot][:, :], stage[slot][:, :], w_hi[slot][:, :].bitcast(F32),
                                  ALU.subtract).then_inc(lo_ready, 1)

            def norm_rstd(n):
                dve.wait_ge(std_ready, n + 1)
                dve.reciprocal(rstd[:, :], ssum[:, :]).then_inc(rstd_ready, 1)
                dve.wait_ge(rstd_ready, n + 1)

            def residual(name):
                r0, t0, c0, n0 = XR0[name], T0[name], C0[name], N0[name]
                gain, scale = FOLLOWED[name], SCALE[name]
                per = 6 if name.startswith("down") else 2

                def step(it):
                    for pair in range(2):
                        last = c0 + (pair + 1) * (per // 2) - 1
                        for k in range(per // 2 - 1):
                            dve.wait_ge(chunk_done, it * per + (c0 + pair * (per // 2) + k + 1))
                            split_lo((c0 + 2 + pair * (per // 2) + k, it * per))
                        dve.wait_ge(chunk_done, it * per + (last + 1))
                        for e in range(2):
                            m = 2 * pair + e
                            hm = row(h, it * 4 + m)
                            dve.scalar_tensor_tensor(hm, ps[:, (t0 + m) % 4, :], scale, hm, ALU.mult, ALU.add).then_inc(acc_evac, 1)
                        split_lo((last + 2, it * per))
                        for e in range(2):
                            m = 2 * pair + e
                            if gain:
                                dve.wait_ge(x_hi_ready, it * 4 + (r0 + m + 1))
                                dve.scalar_tensor_tensor(row(x_lo, it * 4 + m), row(h, it * 4 + m), pc(gain, it * 4 + m),
                                                         row(x_hi, it * 4 + m).bitcast(F32), ALU.mult, ALU.subtract).then_inc(x_ready, 1)

                if name == "down4":
                    step(0)
                    step(1)
                else:
                    walk(dve, 2, step)

            def up(name):
                c0, t0, f0, conv = C0[name], T0[name], FT * UPS[name], name == "up0"

                def step(it):
                    dve.wait_ge(chunk_done, it * 2 + (c0 + 1))
                    for e in range(2):
                        dve.tensor_tensor(gate_b[:, e, 1:1 + S], ps[:, (t0 + e) % 4, :], rstd[:, :], ALU.mult).then_inc(acc_evac, 1)
                    split_lo((c0 + 2, it * 2))
                    dve.wait_ge(f_ready, past(it * 2 + f0))
                    if conv:
                        for e in range(2):
                            f = it * 2 + e
                            g = gate_b[:, e, :]
                            dve.wait_ge(acc_evac, it * 4 + (t0 + e + 1))
                            dve.tensor_scalar(up_b[:, e, :], g[:, 1:1 + S], pc("conv_w1", f), pc("conv_b", f), ALU.mult, ALU.add).then_inc(conv_step, 1)
                            dve.wait_ge(conv_step, it * 6 + 3 * e + 1)
                            dve.scalar_tensor_tensor(up_b[:, e, :], g[:, 0:S], pc("conv_w0", f), up_b[:, e, :], ALU.mult, ALU.add).then_inc(conv_step, 1)
                            dve.wait_ge(conv_step, it * 6 + 3 * e + 2)
                            dve.scalar_tensor_tensor(up_b[:, e, :], g[:, 2:2 + S], pc("conv_w2", f), up_b[:, e, :], ALU.mult, ALU.add).then_inc(conv_step, 1)
                    dve.wait_ge(chunk_done, it * 2 + (c0 + 2))
                    for e in range(2):
                        if conv:
                            dve.wait_ge(silu_ready, it * 2 + (f0 + e + 1))
                        dve.tensor_tensor(up_b[:, e, :], ps[:, (t0 + 2 + e) % 4, :], rstd[:, :], ALU.mult).then_inc(acc_evac, 1)
                    split_lo((c0 + 3, it * 2))
                    for e in range(2):
                        dve.wait_ge(f_hi_ready, it * 2 + (f0 + e + 1))
                        dve.tensor_tensor(row(f_lo, it * 2 + e), up_b[:, e, :], row(f_hi, it * 2 + e).bitcast(F32), ALU.subtract).then_inc(f_ready, 1)

                walk(dve, FT // 2, step)

            for k in range(1, KT):
                dve.wait_ge(x_sq, k + 1)
                if k > 1:
                    dve.wait_ge(x_ss, k - 1)
                dve.tensor_tensor(ssum[:, :], sq8[:, 0, :] if k == 1 else ssum[:, :], sq8[:, k, :], ALU.add).then_inc(x_ss, 1)
            split_lo((0, 0))
            norm_rstd(0)
            for k in range(KT):
                if k >= 2:
                    dve.wait_ge(x_ready, k - 1)
                dve.scalar_tensor_tensor(xn[:, k % 2, :], h[:, k, :], pc("norm_mix", k), rstd[:, :], ALU.mult, ALU.mult).then_inc(xn_ready, 1)
                if k >= 1:
                    dve.wait_ge(x_hi_ready, k)
                    dve.tensor_tensor(x_lo[:, k - 1, :], xn[:, (k - 1) % 2, :], x_hi[:, k - 1, :].bitcast(F32), ALU.subtract).then_inc(x_ready, 1)
            dve.wait_ge(x_hi_ready, KT)
            dve.tensor_tensor(x_lo[:, KT - 1, :], xn[:, (KT - 1) % 2, :], x_hi[:, KT - 1, :].bitcast(F32), ALU.subtract).then_inc(x_ready, 1)

            split_lo((1, 0))
            dve.wait_ge(par_landed, 32)
            lb, om, t8 = small[:, 32:40], small[:, 40:48], small[:, 48:56]
            a0, a1 = pc("lb0", 0, 8), pc("lb1", 0, 8)
            step = [0]

            def link(ins, s):
                step[0] += 1
                ins.then_inc(s, 1)
                dve.wait_ge(s, step[0])

            link(dve.tensor_tensor(t8, a0, a1, ALU.max), lb_step)
            link(dve.tensor_tensor(lb, a0, t8, ALU.subtract), lb_step)
            dve.tensor_tensor(om, a1, t8, ALU.subtract).then_inc(lb_step, 1)
            step[0] += 1
            dve.wait_ge(lb_exp, 2)
            link(dve.tensor_tensor(t8, lb, om, ALU.add), lb_step)
            link(dve.reciprocal(t8, t8), lb_step)
            link(dve.tensor_tensor(lb, lb, t8, ALU.mult), lb_step)
            link(dve.tensor_scalar(om, lb, -1.0, 1.0, ALU.mult, ALU.add), lb_step)
            c0, t0 = C0["qf"], T0["qf"]

            def qf_step(it):
                for j in range(2):
                    dve.wait_ge(chunk_done, it * 2 + (c0 + j + 1))
                    for e in range(2):
                        dve.tensor_copy(row(qf, it * 4 + 2 * j + e), ps[:, (t0 + 2 * j + e) % 4, :]).then_inc(acc_evac, 1)
                    split_lo((c0 + j + 2, it * 2))

            walk(dve, 3, qf_step)
            two_pi = 2.0 * np.pi
            p1 = 6.28125
            p2 = float(np.float32(np.round((two_pi - p1) * 2.0 ** 22) / 2.0 ** 22))
            p3 = float(np.float32(two_pi - p1 - p2))
            big = 1.5 * 2.0 ** 23
            top = 3.1415925
            dve.wait_ge(mask_landed, 16)
            link(dve.tensor_copy(ls_mask[:, :, :], mask_f[:, :, :]), lb_step)
            dve.wait_ge(pos_landed, 16)
            link(dve.tensor_copy(ang[:, :], pos_i[:, :]), lb_step)
            link(dve.tensor_scalar(ang[:, :], ang[:, :], pc("inv_freq", 0), None, ALU.mult), lb_step)
            link(dve.tensor_scalar(turns[:, :], ang[:, :], 1.0 / two_pi, None, ALU.mult), lb_step)
            link(dve.tensor_scalar(turns[:, :], turns[:, :], big, None, ALU.add), lb_step)
            link(dve.tensor_scalar(turns[:, :], turns[:, :], -big, None, ALU.add), lb_step)
            for part in (p1, p2, p3):
                link(dve.scalar_tensor_tensor(ang[:, :], turns[:, :], -part, ang[:, :], ALU.mult, ALU.add), lb_step)
            link(dve.tensor_scalar(turns[:, :], ang[:, :], float(np.pi / 2), -two_pi, ALU.is_gt, ALU.mult), lb_step)
            link(dve.scalar_tensor_tensor(turns[:, :], ang[:, :], float(np.pi / 2), turns[:, :], ALU.add, ALU.add), lb_step)
            dve.tensor_scalar(ang[:, :], ang[:, :], top, -top, ALU.min, ALU.max).then_inc(trig, 1)
            dve.tensor_scalar(turns[:, :], turns[:, :], top, -top, ALU.min, ALU.max).then_inc(trig, 1)

            for j in range(2):
                dve.wait_ge(chunk_done, C0["v"] + j + 1)
                for e in range(2):
                    dve.tensor_scalar(v_nat[:, 2 * e:2 * e + 2, j * PAIR:(j + 1) * PAIR],
                                      ps[:, (T0["v"] + 2 * j + e) % 4, :].rearrange("p (a n) -> p a n", a=2),
                                      HK ** -0.5, None, ALU.mult).then_inc(acc_evac, 1)
                split_lo((C0["v"] + j + 2, 0))
                if j == 0:
                    dve.wait_ge(qf_act, 2)
                    for i in range(8):
                        dve.tensor_scalar(qf[:, 4 + i, :], qf[:, 4 + i, :], om[:, i:i + 1], lb[:, i:i + 1], ALU.mult, ALU.add).then_inc(f_ready1, 1)
            dve.wait_ge(rope1_ready, 2)
            dve.tensor_scalar(rope_s[:, :], rope_s[:, :], pc("rot_sign", 0), None, ALU.mult).then_inc(rope1_ready, 1)
            dve.wait_ge(f_ready1, 8)

            def ls_heads(it):
                def init(e):
                    f = 2 * e + 4
                    dve.wait_ge(ls_o, past(it * 2))
                    fb, ff = row(qf, it * 4 + f), row(qf, it * 4 + f + 1)
                    q = row(qf, it * 2 + e)
                    dve.tensor_tensor(QQ[e][:, 0, :], q, fb, ALU.mult)
                    dve.tensor_tensor(QQ[e][:, 1, :], q, ff, ALU.mult)
                    dve.tensor_scalar(KK[e][:, 1, :], ff, -1.0, 1.0, ALU.mult, ALU.add).then_inc(ls_init, 1)
                    dve.tensor_scalar(KK[e][:, 0, :], fb, -1.0, 1.0, ALU.mult, ALU.add).then_inc(ls_init, 1)
                    dve.wait_ge(ls_init, it * 4 + 2 * e + 2)
                    dve.tensor_tensor(A[e][:, 3, :], KK[e][:, 0, :], KK[e][:, 1, :], ALU.add).then_inc(ls_ops, 1)

                def update(level, e):
                    w, nb, base, pitch, (new, npitch) = ls_level(it, level, e)
                    k4 = free(KK[e][:, :, :], w, [[2 * w, nb], [S - w, 2], [1, w]])
                    tk = free(base, 0, [[2, nb], [pitch + 1, 2], [0, w]])
                    dve.wait_ge(ls_scores, it * 2 * LEVELS + (2 * level + e + 1))
                    dve.wait_ge(ls_diag, it * 16 + (min(2 * (level - 1), 14) + e + 1))
                    ins = dve.tensor_tensor(k4, k4, tk, ALU.mult)
                    if w < S // 4:
                        a = free(base, 0, [[pitch, 2], [2, nb]])
                        b = free(base, 1, [[pitch, 2], [2, nb]])
                        ins = dve.tensor_tensor(free(new[:, :, :], 0, [[npitch, 2], [1, nb]]), a, b, ALU.mult)
                    ins.then_inc(ls_ops, 1)

                for e in range(2):
                    init(e)
                dve.wait_ge(chunk_done, it * 2 + (C0["gq"] + 1))
                for e in range(2):
                    dve.tensor_scalar(row(g_silu, it * 2 + e), ps[:, (T0["gq"] + e) % 4, :], 1.0, None, ALU.mult).then_inc(acc_evac, 1)
                for level in range(9):
                    for e in range(2):
                        a_diag = free(A[e][:, :, :], 0, [[S + P, BLK], [1, P]])
                        bank = 4 + 2 * e + level % 2
                        s4 = ps[:, bank, :].rearrange("p (a n) -> p a n", a=BLK)
                        if level == 0:
                            dve.wait_ge(ls_scores, it * 2 * LEVELS + (e + 1))
                            dve.tensor_tensor(a_diag, s4, free(ident, 0, [[0, BLK], [1, P]]), ALU.mult).then_inc(ls_diag, 1)
                            continue
                        update(level, e)
                        if level < 8:
                            dve.copy_predicated(a_diag, free(ls_mask[:, level - 1, :], 0, [[0, BLK], [1, P]]), s4).then_inc(ls_diag, 1)
                    if level == 3:
                        split_lo((C0["gq"] + 2, it * 2))
                for e in range(2):
                    o = TA[e][:, :, :].rearrange("p a n -> p (a n)")
                    r = KK[e][:, 1, :]
                    dve.wait_ge(ls_std, it * 2 + e + 1)
                    dve.reciprocal(r, r).then_inc(ls_norm, 1)
                    dve.wait_ge(ls_norm, it * 8 + 4 * e + 1)
                    dve.tensor_tensor(o, ps[:, 5 + 2 * e, :], r, ALU.mult).then_inc(ls_norm, 1)
                    dve.wait_ge(ls_norm, it * 8 + 4 * e + 2)
                    dve.tensor_scalar(o, o, pc("hg_norm", it * 2 + e), None, ALU.mult).then_inc(ls_norm, 1)
                    dve.wait_ge(ls_norm, it * 8 + 4 * e + 3)
                    dve.wait_ge(g_ready, it + 1)
                    dve.tensor_tensor(o, o, row(g_silu, it * 2 + e), ALU.mult).then_inc(ls_norm, 1)
                dve.wait_ge(chunk_done, it * 2 + (C0["gq"] + 2))
                for e in range(2):
                    dve.tensor_scalar(row(qa, it * 2 + e), ps[:, (T0["gq"] + 2 + e) % 4, :], 1.0, None, ALU.mult).then_inc(acc_evac, 1)
                split_lo((C0["gq"] + 3, it * 2))
                for e in range(2):
                    dve.wait_ge(ls_hi, it * 2 + e + 1)
                    dve.tensor_tensor(row(rec_lo, it * 2 + e), TA[e][:, :, :].rearrange("p a n -> p (a n)"),
                                      row(rec_hi, it * 2 + e).bitcast(F32), ALU.subtract).then_inc(rec_ready, 1)

            walk(dve, 2, ls_heads)

            rot = [0]

            def rotate(target):
                i = rot[0]
                rot[0] += 1
                dve.wait_ge(perm_done, i + 1)
                dve.wait_ge(rope1_ready, 3)
                if i:
                    dve.wait_ge(rot_step, 3 * i)
                dve.tensor_tensor(rot_t[:, :], ps[:, 4 + i % 4, :], rope_s[:, :], ALU.mult).then_inc(rot_step, 1)
                dve.tensor_tensor(target, target, rope_c[:, :], ALU.mult).then_inc(rot_step, 1)
                dve.wait_ge(rot_step, 3 * i + 2)
                dve.tensor_tensor(target, target, rot_t[:, :], ALU.add).then_inc(rot_step, 1)

            t0 = T0["kv_a"]
            dve.wait_ge(chunk_done, C0["kv_a"] + 1)
            dve.wait_ge(pad_ready, 1)
            dve.tensor_copy(k_pad[:, P:P + S], ps[:, t0 % 4, :]).then_inc(acc_evac, 1)
            dve.wait_ge(va_hi_ready, 1)
            dve.tensor_tensor(va_lo[:, :, :], ps[:, (t0 + 1) % 4, :].rearrange("p (a n) -> p a n", a=BLK), va_hi[:, :, :].bitcast(F32),
                              ALU.subtract).then_inc(acc_evac, 1)
            rotate(k_pad[:, P:P + S])
            rotate(qa[:, 0, :])
            dve.wait_ge(k_hi_ready, 1)
            dve.tensor_tensor(k_lo[:, :], k_pad[:, :], k_hi[:, :].bitcast(F32), ALU.subtract).then_inc(k_ready, 1)
            dve.wait_ge(const_landed, 32)

            def maxima(j, p):
                mx, nm = small[:, 56 + 4 * p:60 + 4 * p], small[:, 4 * p:4 * p + 4]
                u1 = j * 2 + (p + 1)
                dve.wait_ge(wa_scores, past(u1))
                dve.scalar_tensor_tensor(w_s[p][:, :, :], ps[:, 0:4, 0:384], WIN_D ** -0.5, band[:, :, :], ALU.mult, ALU.add).then_inc(wa_s, 1)
                dve.wait_ge(wa_s, past(u1))
                dve.tensor_reduce(mx, w_s[p][:, :, :], AX.X, ALU.max).then_inc(wa_max, 1)
                dve.wait_ge(wa_max, j * 4 + (2 * p + 1))
                dve.tensor_scalar(nm, mx, pc("sink", j + 4 * p), -1.0, ALU.max, ALU.mult).then_inc(wa_max, 1)

            def denominators(j, p):
                d, es, rd = small[:, 8 + 4 * p:12 + 4 * p], small[:, 16 + 4 * p:20 + 4 * p], small[:, 24 + 4 * p:28 + 4 * p]
                dve.wait_ge(wa_exp, j * 2 + (p + 1))
                dve.tensor_tensor(rd, d, es, ALU.add).then_inc(wa_den, 1)
                dve.wait_ge(wa_den, j * 4 + (2 * p + 1))
                dve.reciprocal(rd, rd).then_inc(wa_den, 1)

            def wa_tile(j, last=False):
                for p in range(2):
                    half = slice(64 * p, 64 * p + 64)
                    dve.wait_ge(wT_hi_ready, j * 2 + (p + 1))
                    dve.tensor_tensor(wT_lo[:, 0:2, 0:384], ps[:, 4:6, 0:384], wT_hi[:, 0:2, 0:384].bitcast(F32), ALU.subtract)
                    dve.tensor_tensor(wT_lo[:, 2, :], ps[:, 6, :], wT_hi[:, 2, :].bitcast(F32), ALU.subtract).then_inc(wa_pT, 1)
                    if not (last and p == 1):
                        denominators(j + p, 1 - p)
                    if not last:
                        maxima(j + 1, p)
                    dve.wait_ge(wa_hi, j * 2 + (p + 1))
                    dve.tensor_tensor(row(att_lo, j)[half], ps[half, 7, :], row(att_hi, j)[half].bitcast(F32), ALU.subtract).then_inc(att_ready, 1)

            rotate(qa[:, 1, :])
            maxima(0, 0)
            for i in range(2, WIN_TILES):
                rotate(qa[:, i, :])
            denominators(0, 0)
            maxima(0, 1)
            split_lo((C0["kv_a"] + 2, 0))
            walk(dve, WIN_TILES - 1, wa_tile)
            wa_tile(WIN_TILES - 1, last=True)

            c0, t0 = C0["merge"], T0["merge"]

            def merge(it):
                for j in range(2):
                    t = t0 + 8 * j
                    n = it * 4 + 2 * j
                    c = c0 + 3 * j
                    dve.wait_ge(chunk_done, it * 6 + (c + 1))
                    for e in range(2):
                        dve.tensor_copy(gate_b[:, e, 0:S], ps[:, (t + e) % 4, :]).then_inc(acc_evac, 1)
                    split_lo((c + 2, it * 6))
                    dve.wait_ge(chunk_done, it * 6 + (c + 2))
                    dve.wait_ge(mrg_ready, past(n))
                    for e in range(2):
                        dve.tensor_copy(up_b[:, e, :], ps[:, (t + 2 + e) % 4, :]).then_inc(acc_evac, 1)
                    split_lo((c + 3, it * 6))
                    dve.wait_ge(chunk_done, it * 6 + (c + 3))
                    for e in range(2):
                        dve.wait_ge(gate_sig, it * 8 + (4 * j + e + 1))
                        dve.tensor_tensor(gate_b[:, e, 0:S], gate_b[:, e, 0:S], ps[:, (t + 4 + e) % 4, :], ALU.mult).then_inc(acc_evac, 1)
                    for e in range(2):
                        dve.wait_ge(gate_sig, it * 8 + (4 * j + 2 + e + 1))
                        dve.tensor_tensor(up_b[:, e, :], up_b[:, e, :], ps[:, (t + 6 + e) % 4, :], ALU.mult).then_inc(acc_evac, 1)
                    split_lo((c + 4, it * 6))
                    for e in range(2):
                        dve.wait_ge(acc_evac, it * 16 + (t + 6 + e + 1))
                        dve.tensor_tensor(up_b[:, e, :], up_b[:, e, :], gate_b[:, e, 0:S], ALU.add).then_inc(mrg_sum, 1)
                    for e in range(2):
                        dve.wait_ge(mrg_hi_ready, n + e + 1)
                        dve.tensor_tensor(row(mrg_lo, n + e), up_b[:, e, :], row(mrg_hi, n + e).bitcast(F32), ALU.subtract).then_inc(mrg_ready, 1)

            walk(dve, 2, merge)

            dve.wait_ge(mem_std, 1)
            dve.reciprocal(mem_r, mem_r).then_inc(mem_std, 1)
            dve.wait_ge(mem_std, 2)
            for k in range(KT):
                if k >= 2:
                    dve.wait_ge(mem_ready, k - 1)
                dve.scalar_tensor_tensor(mem_t[:, k % 2, :], mem_raw[:, k, :], pc("norm_mem_kv", k), mem_r, ALU.mult, ALU.mult).then_inc(mem_n, 1)
                dve.wait_ge(mem_hi_ready, k + 1)
                dve.tensor_tensor(mem_lo(k), mem_t[:, k % 2, :], mem_hi[:, k, :].bitcast(F32), ALU.subtract).then_inc(mem_ready, 1)

            residual("mix_out")

            def mem_chunks(name, to, hi):
                c0, t0, n0 = C0[name], T0[name], 0 if name == "mem_k" else 4

                def step(it):
                    for j in range(2):
                        b = (t0 + 2 * j) % 4
                        i = it * 2 + j
                        dve.wait_ge(mem_kv, i + n0 + 1)
                        dve.wait_ge(chunk_done, i + (c0 + 1))
                        dve.tensor_tensor(to(i), ps[:, b:b + 2, 0:MEM], hi(i).bitcast(F32), ALU.subtract).then_inc(acc_evac, 2)
                        split_lo((c0 + j + 2, it * 2))

                walk(dve, 2, step)

            mem_chunks("mem_k", lambda i: rows(km_lo, i * 2, 2), lambda i: rows(km_hi, i * 2, 2))
            mem_chunks("mem_v", lambda i: vm_lo[:, :, bass.ds(i * PAIR, PAIR)], lambda i: vm_hi[:, :, bass.ds(i * PAIR, PAIR)])

            norm_rstd(NS0["mix_out"])
            c2, t2 = C0["mem_q"], T0["mem_q"]

            def q_normed(u):
                dve.wait_ge(chunk_done, c2 + u + 1)
                if u:
                    dve.wait_ge(qm_ready, u)
                b = (t2 + 2 * u) % 4
                dve.tensor_tensor(qm[:, :, :], ps[:, b:b + 2, :], free(rstd[:, :], 0, [[0, 2], [1, S]]), ALU.mult).then_inc(acc_evac, 2)

            def q_rest(u):
                dve.wait_ge(acc_evac, t2 + 2 * u + 2)
                dve.wait_ge(qm_hi_ready, u + 1)
                dve.tensor_tensor(qm_lo[u % 2][:, :, :], qm[:, :, :], qm_hi[u % 2][:, :, :].bitcast(F32), ALU.subtract).then_inc(qm_ready, 1)

            def maxima(u):
                e = u % 2
                mx, nm = small[:, 56 + 4 * e:60 + 4 * e], small[:, 4 * e:4 * e + 4]
                dve.wait_ge(ma_scores, u + 1)
                dve.tensor_reduce(mx, ps[:, 4:6, :].rearrange("p a (b n) -> p (a b) n", b=2), AX.X, ALU.max).then_inc(ma_max, 1)
                dve.wait_ge(ma_max, u * 2 + 1)
                dve.tensor_scalar(nm, mx, -(MEM_D ** -0.5), None, ALU.mult).then_inc(ma_max, 1)

            def denominators(u):
                e = u % 2
                dve.wait_ge(ma_exp, u + 1)
                dve.reciprocal(small[:, 24 + 4 * e:28 + 4 * e], small[:, 8 + 4 * e:12 + 4 * e]).then_inc(ma_den, 1)

            for u in range(2):
                q_normed(u)
                q_rest(u)
                split_lo((c2 + u + 2, 0))
            maxima(0)
            denominators(0)
            for u in range(MEM_HEADS):
                more = u + 1 < MEM_HEADS
                if u + 2 < MEM_HEADS:
                    q_normed(u + 2)
                dve.wait_ge(pm_hi_ready, u + 1)
                dve.tensor_tensor(pm_lo[:, :, :], ps[:, 6:8, :], pm_hi[:, :, :].bitcast(F32), ALU.subtract).then_inc(ma_pT, 1)
                if more:
                    maxima(u + 1)
                if u + 2 < MEM_HEADS:
                    q_rest(u + 2)
                dve.wait_ge(ma_hi, u + 1)
                for d in range(2):
                    dve.tensor_tensor(mo_lo[:, 2 * u + d, :], ps[:, 6 + d, :], mo_hi[:, 2 * u + d, :].bitcast(F32),
                                      ALU.subtract).then_inc(mo_ready, 1)
                if more:
                    denominators(u + 1)
                if u + 2 < MEM_HEADS:
                    split_lo((c2 + u + 4, 0))

            residual("mem_o")
            dve.memset(gate_b[:, :, 0:1], 0.0)
            dve.memset(gate_b[:, :, S + 1:S + 2], 0.0)
            norm_rstd(NS0["mem_o"])
            up("up0")
            residual("down0")
            norm_rstd(NS0["down0"])
            for m in range(KT):
                dve.scalar_tensor_tensor(h[:, m, :], h[:, m, :], pc("final_norm", m), rstd[:, :], ALU.mult, ALU.mult).then_inc(renorm_ready, 1)
                if m >= 1:
                    dve.wait_ge(x_hi_ready, XR0["renorm"] + m)
                    dve.scalar_tensor_tensor(x_lo[:, m - 1, :], h[:, m - 1, :], pc("ffn1_0", m - 1), x_hi[:, m - 1, :].bitcast(F32),
                                             ALU.mult, ALU.subtract).then_inc(x_ready, 1)
            dve.wait_ge(x_hi_ready, XR0["renorm"] + KT)
            dve.scalar_tensor_tensor(x_lo[:, KT - 1, :], h[:, KT - 1, :], pc("ffn1_0", KT - 1), x_hi[:, KT - 1, :].bitcast(F32),
                                     ALU.mult, ALU.subtract).then_inc(x_ready, 1)
            norm_rstd(NS0["renorm"])
            up("up1")
            residual("down1")

            norm_rstd(NS0["down1"])
            c0, t0 = C0["a_in"], T0["a_in"]

            def a_in(j):
                dve.wait_ge(chunk_done, c0 + j + 1)
                for e in range(2):
                    i = 2 * j + e
                    target = lat[:, i, :] if i < 6 else u_p[:, i - 6, PAD:PAD + S]
                    dve.tensor_tensor(target, ps[:, (t0 + i) % 4, :], rstd[:, :], ALU.mult).then_inc(acc_evac, 1)
                split_lo((c0 + j + 2, 0))

            for j in range(4):
                a_in(j)
            dve.wait_ge(lat_std, 2)
            dve.reciprocal(lat_r[:, :, :], lat_r[:, :, :]).then_inc(lat_std, 1)
            dve.wait_ge(lat_std, 3)
            for i in range(5):
                gain = pc("q_a_norm", i) if i < 3 else pc("kv_a_norm", i - 3)
                dve.scalar_tensor_tensor(lat[:, i, :], lat[:, i, :], gain, lat_r[:, 0 if i < 3 else 1, :], ALU.mult, ALU.mult).then_inc(lat_n, 1)
            for i in range(5):
                dve.wait_ge(lat_hi_ready, i + 1)
                dve.tensor_tensor(lat_lo[:, i, :], lat[:, i, :], lat_hi[:, i, :].bitcast(F32), ALU.subtract).then_inc(lat_ready, 1)
            a_in(4)
            t0 = T0["mla"]

            def mla_evac(i):
                if i in MLA_LAST:
                    dve.wait_ge(chunk_done, C0["mla"] + MLA_LAST.index(i) + 1)
                else:
                    dve.wait_ge(mla_tile, i + 1 - sum(m < i for m in MLA_LAST))
                src = ps[:, (t0 + i) % 4, :]
                if i < 8:
                    ins = dve.tensor_copy(q_h[0:MLA_QK, i, :], src[0:MLA_QK])
                elif i < 12:
                    ins = dve.tensor_copy(v_mla[:, i - 8, :], src)
                elif i < 16:
                    dve.tensor_copy(k_h[0:MLA_NOPE, 2 * (i - 12), :], src[0:MLA_NOPE])
                    ins = dve.tensor_copy(k_h[0:MLA_NOPE, 2 * (i - 12) + 1, :], src[MLA_NOPE:2 * MLA_NOPE])
                else:
                    ins = dve.tensor_scalar(u_p[:, i - 16, PAD:PAD + S], src, pc("pool_scale", i - 16), None, ALU.mult)
                ins.then_inc(acc_evac, 1)

            def head_norms(w, src, gain):

                def added(it):
                    for e in range(2):
                        n = it * 2 + (8 * w + e + 1)
                        tile = row(src, it * 2 + e)[0:MLA_QK]
                        dve.wait_ge(la_sin, past(n))
                        dve.wait_ge(la_cos, n)
                        dve.tensor_tensor(tile, tile, hd_t[e][0:MLA_QK, :], ALU.add).then_inc(la_rot, 1)

                def heads(it, first=False):
                    for e in range(2):
                        tile = row(src, it * 2 + e)[0:MLA_QK]
                        dve.wait_ge(la_spread, past(it * 2 + (8 * w + e + 1)))
                        dve.scalar_tensor_tensor(tile, tile, par[0:MLA_QK, COL[gain]:COL[gain] + 1], ps[0:MLA_QK, 4 + e, :],
                                                 ALU.mult, ALU.mult).then_inc(la_norm, 1)
                    if not first:
                        added(it - 1)
                        dve.wait_ge(la_rot, it * 2 + 8 * w)
                    for e in range(2):
                        dve.wait_ge(la_swap, it * 2 + (8 * w + e + 1))
                        dve.tensor_tensor(hd_t[e][0:MLA_QK, :], ps[0:MLA_QK, 6 + e, :], rope_s[0:MLA_QK, :], ALU.mult).then_inc(la_sin, 1)

                heads(0, first=True)
                walk(dve, MLA_HEADS // 2, heads, 1)
                added(MLA_HEADS // 2 - 1)
                dve.wait_ge(la_rot, 8 * (w + 1))

            def head_rstd(w):
                dve.wait_ge(hd_std, w + 1)
                dve.reciprocal(hd_r[w][0:8, :], hd_r[w][0:8, :]).then_inc(hd_rstd, 1)

            def head_rsplit(w):
                dve.wait_ge(hd_rstd, w + 1)
                dve.wait_ge(hd_rhi_ready, w + 1)
                dve.tensor_tensor(hd_rlo[0:8, :], hd_r[w][0:8, :], hd_rhi[0:8, :].bitcast(F32), ALU.subtract).then_inc(hd_rsplit, 1)

            for i in range(8):
                mla_evac(i)
            split_lo((C0["mla"] + 2, 0))
            for i in range(8, 16):
                mla_evac(i)
            head_rstd(0)
            for g in range(4):
                dve.wait_ge(pl_hi_ready, g + 1)
                dve.tensor_tensor(pl_lo[:, g, :], u_p[:, g, PAD:PAD + S], pl_hi[:, g, :].bitcast(F32), ALU.subtract).then_inc(pl_ready, 1)
            head_rstd(1)
            head_rsplit(0)
            for i in range(16, 20):
                mla_evac(i)
            dve.wait_ge(rope2_landed, 64)
            head_norms(0, q_h, "q_head")
            head_rsplit(1)
            head_norms(1, k_h, "k_head")
            split_lo((C0["mla"] + 3, 0))
            split_lo((C0["mla"] + 4, 0))
            for g in range(4):
                dve.wait_ge(cat0_hi, g + 1)
                dve.tensor_tensor(cat_lo[0][:, g, :], u_p[:, g, PAD:PAD + S], cat_hi[0][:, g, :].bitcast(F32), ALU.subtract).then_inc(cat0_ready, 1)

            def cols(e):
                return (small[:, 56 + 4 * e:60 + 4 * e], small[:, 4 * e:4 * e + 4], small[:, 8 + 4 * e:12 + 4 * e],
                        small[:, 24 + 4 * e:28 + 4 * e])

            def maxima(v, e):
                mx, nm, _, _ = cols(e)
                dve.wait_ge(la_scores, v + 1)
                wide = free(ps[:, 3 * e, :], 3 * P, [[3 * P, 3], [1, P]])
                dve.tensor_tensor(wide, wide, free(causal, 0, [[0, 3], [1, P]]), ALU.add)
                one = ps[:, 3 * e + 1, 3 * P:4 * P]
                dve.tensor_tensor(one, one, causal, ALU.add).then_inc(la_mask, 1)
                dve.wait_ge(la_mask, v + 1)
                for n in range(BLK):
                    b, c = CAUSAL_AT[n + 1]
                    ins = dve.tensor_reduce(mx[:, n:n + 1], ps[:, 3 * e + b, c:c + (n + 1) * P], AX.X, ALU.max)
                ins.then_inc(la_max, 1)
                dve.wait_ge(la_max, 2 * v + 1)
                dve.tensor_scalar(nm, mx, -(MLA_QK ** -0.5), None, ALU.mult).then_inc(la_max, 1)

            def denominators(v, e):
                _, _, d4, rd = cols(e)
                dve.wait_ge(la_exp, v + 1)
                dve.reciprocal(rd, d4).then_inc(la_den, 1)

            def turned(v, e):
                dve.wait_ge(la_turned, v + 1)
                dve.tensor_copy(l_pT[e][:, 0:2, :], ps[:, 3 * e:3 * e + 2, :])
                dve.tensor_copy(l_pT[e][:, 2, 0:2 * P], ps[:, 3 * e + 2, 0:2 * P]).then_inc(la_pT, 1)

            def out_lo(it, e):
                half = slice(64 * e, 64 * e + 64)
                dve.wait_ge(la_hi, it * 2 + (e + 1))
                dve.tensor_tensor(row(cat_lo[1], it)[half], ps[half, 6 + e, :], row(cat_hi[1], it)[half].bitcast(F32), ALU.subtract).then_inc(cat1_ready, 1)

            def mla_heads(it, first=False, last=False):
                for e in range(2):
                    turned(it * 2 + e, e)
                    if not (last and e == 1):
                        denominators(it * 2 + (e + 1), 1 - e)
                    if not (first and e == 0):
                        out_lo(it - 1 if e == 0 else it, 1 - e)
                    if not last:
                        maxima(it * 2 + (e + 2), e)

            maxima(0, 0)
            denominators(0, 0)
            maxima(1, 1)
            mla_heads(0, first=True)
            walk(dve, MLA_HEADS // 2 - 1, mla_heads, 1)
            mla_heads(MLA_HEADS // 2 - 1, last=True)
            out_lo(MLA_HEADS // 2 - 1, 1)
            residual("a_out")
            norm_rstd(NS0["a_out"])
            up("up2")
            residual("down2")
            norm_rstd(NS0["down2"])
            up("up3")
            residual("down3")

            norm_rstd(NS0["down3"])
            c3, t3 = C0["c_in"], T0["c_in"]
            dve.wait_ge(cu_pad, 1)

            def conv_mix(it):
                for j in range(2):
                    for k, target in enumerate((cg, cu, ch)):
                        dve.wait_ge(chunk_done, it * 6 + (c3 + 3 * j + k + 1))
                        for e in range(2):
                            o = target[:, e, 2:2 + S] if target is cu else target[:, e, :]
                            dve.tensor_tensor(o, ps[:, (t3 + 6 * j + 2 * k + e) % 4, :], rstd[:, :], ALU.mult).then_inc(acc_evac, 1)
                        split_lo((c3 + 3 * j + k + 2, it * 6))
                    for e in range(2):
                        f = it * 4 + 2 * j + e
                        dve.wait_ge(cu_ready, it * 4 + 2 * j + e + 1)
                        u, y = cu[:, e, :], cv[:, e, :]
                        dve.tensor_scalar(y, u[:, 2:2 + S], pc("cc_w2", f), None, ALU.mult).then_inc(cv_step, 1)
                        dve.wait_ge(cv_step, it * 12 + (6 * j + 3 * e + 1))
                        dve.scalar_tensor_tensor(y, u[:, 1:1 + S], pc("cc_w1", f), y, ALU.mult, ALU.add).then_inc(cv_step, 1)
                        dve.wait_ge(cv_step, it * 12 + (6 * j + 3 * e + 2))
                        dve.scalar_tensor_tensor(y, u[:, 0:S], pc("cc_w0", f), y, ALU.mult, ALU.add).then_inc(cv_step, 1)
                    for e in range(2):
                        f = it * 4 + 2 * j + e
                        dve.wait_ge(cc_hi_ready, it * 4 + 2 * j + e + 1)
                        dve.tensor_tensor(row(cc_lo, f), cv[:, e, :], row(cc_hi, f).bitcast(F32), ALU.subtract).then_inc(cc_ready, 1)

            walk(dve, 2, conv_mix)
            residual("c_out")
            norm_rstd(NS0["c_out"])
            up("up4")
            residual("down4")

        @block.gpsimd
        def _(pool):
            def sums(name):
                i = N0[name]
                base = 9 * i
                pool.wait_ge(rstd_ready, i + 1)
                pool.memset(ssum[:, :], 0.0).then_inc(ss_ready, 1)

                by_act = {"down0": sqx, "renorm": sq8}
                n_act = 8 * (1 + list(by_act).index(name)) if name in by_act else 0
                n_own = 8 * sum(other not in by_act for other in RESIDUALS[:i])

                def step(m):
                    if name in by_act:
                        pool.wait_ge(x_sq, m + (n_act + 1))
                        square = row(by_act[name], m)
                    else:
                        square = sq[:, :]
                        pool.wait_ge(acc_evac, m + (T0[name] + 1))
                        pool.wait_ge(ss_ready, m + (base + 1))
                        pool.tensor_tensor(square, row(h, m), row(h, m), ALU.mult).then_inc(sq_ready, 1)
                        pool.wait_ge(sq_ready, m + (n_own + 1))
                    pool.wait_ge(ss_ready, m + (base + 1))
                    pool.tensor_tensor(ssum[:, :], ssum[:, :], square, ALU.add).then_inc(ss_ready, 1)

                walk(pool, KT, step)

            def up(name):
                t0, f0 = T0[name], FT * UPS[name]

                def step(it):
                    for e in range(2):
                        pool.wait_ge(silu_ready, it * 2 + (f0 + e + 1))
                        pool.wait_ge(acc_evac, it * 4 + (t0 + 2 + e + 1))
                        pool.tensor_tensor(up_b[:, e, :], up_b[:, e, :], gate_b[:, e, 1:1 + S], ALU.mult).then_inc(prod_ready, 1)

                walk(pool, FT // 2, step)

            pool.wait_ge(f_ready1, 8)

            def ls_copies(it):
                for e in range(2):
                    pool.wait_ge(ls_o, past(it * 2))
                    pool.tensor_copy(A[e][:, 2, :], row(qf, it * 2 + e)).then_inc(ls_q, 1)
                for level in range(1, 9):
                    for e in range(2):
                        w, nb, base, pitch, _ = ls_level(it, level, e)
                        q4 = free(QQ[e][:, :, :], 0, [[2 * w, nb], [S + w, 2], [1, w]])
                        tq = free(base, 1, [[2, nb], [pitch - 1, 2], [0, w]])
                        pool.wait_ge(ls_scores, it * 2 * LEVELS + (2 * level + e + 1))
                        pool.wait_ge(ls_ops, it * 18 + (2 * (level - 1) + e + 1))
                        pool.tensor_tensor(q4, q4, tq, ALU.mult).then_inc(ls_qops, 1)
                for e in range(2):
                    pool.wait_ge(ls_scores, it * 2 * LEVELS + (2 * 9 + e + 1))
                    pool.tensor_copy(QQ[e][:, 0, :].rearrange("p (b n) -> p b n", b=BLK),
                                     v_nat[:, :, bass.ds(it * 2 * HK + e * HK, HK)]).then_inc(ls_v, 1)

            walk(pool, 2, ls_copies)
            pool.wait_ge(rec_ready, past(HEADS))
            pool.memset(k_pad[:, 0:P], 0.0)
            pool.memset(k_pad[:, P + S:P + S + P], 0.0).then_inc(pad_ready, 1)

            def q_rest(j):
                pool.wait_ge(wa_qhi, j + 1)
                pool.tensor_tensor(q_lo[:, :], row(qa, j), q_hi[:, :].bitcast(F32), ALU.subtract).then_inc(wa_q, 1)

            walk(pool, WIN_TILES, q_rest)
            acc, square = ssum[:, 0:MEM], sq[:, 0:MEM]
            pool.wait_ge(mem_landed, 16)
            pool.tensor_tensor(acc, mem_raw[:, 0, :], mem_raw[:, 0, :], ALU.mult).then_inc(mem_sq_ready, 1)
            for k in range(1, KT):
                pool.wait_ge(mem_sq_ready, 2 * k - 1)
                pool.tensor_tensor(square, mem_raw[:, k, :], mem_raw[:, k, :], ALU.mult).then_inc(mem_sq_ready, 1)
                pool.wait_ge(mem_sq_ready, 2 * k)
                pool.tensor_tensor(acc, acc, square, ALU.add).then_inc(mem_sq_ready, 1)
            pool.wait_ge(mem_stat, 1)
            sums("mix_out")
            sums("mem_o")
            up("up0")
            sums("down0")
            sums("renorm")
            up("up1")
            sums("down1")

            pool.wait_ge(chunk_done, C0["a_in"])
            pool.memset(u_p[:, :, 0:PAD], 0.0)
            pool.memset(win[:, :, 0:PAD], 0.0).then_inc(u_pad, 1)
            pool.wait_ge(u_pad, 1)
            pool.wait_ge(acc_evac, T0["a_in"] + 10)

            def window(i, g, shift=0):
                cut = slice(PAD - shift, PAD + S - shift)
                if i == 0:
                    return u_p[:, g, cut]
                n = slice(g.start, g.stop) if i % 2 else slice(g.start + 3, g.stop + 3)
                return win[:, n, cut]

            for i in range(4):
                if i:
                    pool.wait_ge(pool_step, i)
                g = slice(i, 4)
                pool.tensor_tensor(window(i + 1, g), window(i, g), window(i, g, 1 << i), ALU.add).then_inc(pool_step, 1)
            pool.wait_ge(rope2_landed, 64)
            pool.wait_ge(pool_step, 4)
            for g in range(4):
                b = window(g + 1, slice(g, g + 1))
                pool.tensor_tensor(b, b, cnt[:, g:g + 1, :], ALU.mult).then_inc(pool_step, 1)
            for g in range(4):
                b = window(g + 1, slice(g, g + 1))
                pool.wait_ge(pool_step, 4 + g + 1)
                u = u_p[:, g:g + 1, PAD:PAD + S]
                pool.tensor_tensor(u, b, u, ALU.subtract).then_inc(pool_step, 1)

            def head_norms(w, src):
                pool.wait_ge(pool_step, 12)

                def heads(it):
                    for e in range(2):
                        n = it * 2 + (8 * w + e + 1)
                        tile = row(src, it * 2 + e)[0:MLA_QK]
                        pool.wait_ge(la_swap, n)
                        pool.tensor_tensor(tile, tile, rope_c[0:MLA_QK, :], ALU.mult).then_inc(la_cos, 1)

                walk(pool, MLA_HEADS // 2, heads)

            head_norms(0, q_h)
            head_norms(1, k_h)
            pool.wait_ge(la_rot, 16)
            pool.wait_ge(acc_evac, T0["a_out"])

            def q_copy(v, e, reused=True):
                if reused:
                    pool.wait_ge(la_scores, v - 1)
                pool.tensor_copy(q_c[e][0:MLA_QK, :], row(q_h, v)[0:MLA_QK]).then_inc(la_q, 1)

            def v_copy(it, e, reused=True):
                if reused:
                    pool.wait_ge(la_o, it * 2 + (e - 1))
                src = v_mla[:, :, e * MLA_V + it * 2 * MLA_V:e * MLA_V + it * 2 * MLA_V + MLA_V] if isinstance(it, int) else \
                    v_mla[:, :, bass.ds(it * 2 * MLA_V + e * MLA_V, MLA_V)]
                pool.tensor_copy(vl_st[e][:, :, :], src).then_inc(la_v, 1)

            def mla_copies(it, first=False, last=False):
                for e in range(2):
                    if not last:
                        q_copy(it * 2 + (e + 2), e)
                for e in range(2):
                    v_copy(it, e, not first)

            q_copy(0, 0, False)
            q_copy(1, 1, False)
            mla_copies(0, first=True)
            walk(pool, MLA_HEADS // 2 - 1, mla_copies, 1)
            mla_copies(MLA_HEADS // 2 - 1, last=True)
            sums("a_out")
            up("up2")
            sums("down2")
            up("up3")
            sums("down3")
            pool.wait_ge(chunk_done, C0["c_in"])
            pool.memset(cu[:, :, 0:2], 0.0).then_inc(cu_pad, 1)

            def conv_mix(it):
                for j in range(2):
                    for e in range(2):
                        pool.wait_ge(acc_evac, it * 12 + (T0["c_in"] + 6 * j + 4 + e + 1))
                        pool.tensor_tensor(cu[:, e, 2:2 + S], cu[:, e, 2:2 + S], ch[:, e, :], ALU.mult).then_inc(cu_ready, 1)
                    for e in range(2):
                        pool.wait_ge(cv_step, it * 12 + (6 * j + 3 * e + 3))
                        pool.tensor_tensor(cv[:, e, :], cv[:, e, :], cg[:, e, :], ALU.mult).then_inc(cz_ready, 1)

            walk(pool, 2, conv_mix)
            sums("c_out")
            up("up4")

        @block.tensor
        def _(pe):
            for at_start in (ls_o, la_spread, wa_scores):
                pe.sem_inc(at_start, 1)

            def products(out_ap, w, x, first, last):
                (wh, wl), (xh, xl) = w, x
                pe.matmul(out_ap, wh, xh, start=first, stop=False)
                pe.matmul(out_ap, wh, xl, start=False, stop=False)
                return pe.matmul(out_ap, wl, xh, start=False, stop=last)

            def w_at(c, a, n):
                return w_hi[c % 2][:, a:a + n], w_lo[c % 2][:, a:a + n]

            def begin(c, t, n, reg_c=0, reg_t=0):
                pe.wait_ge(lo_ready, reg_c + (c + 1))
                if t + n > 4:
                    pe.wait_ge(acc_evac, reg_t + (t + n - 4))

            def plain(c, t, x, ready=None, reg_c=0, reg_t=0, width=S):
                begin(c, t, 2, reg_c, reg_t)
                for k in range(KT):
                    if ready:
                        pe.wait_ge(ready[0], ready[1] + k + 1)
                    for m in range(2):
                        mm = products(ps[:, (t + m) % 4, 0:width], w_at(c, k * PAIR + m * P, P), (x[0][:, k, :], x[1](k) if callable(x[1]) else x[1][:, k, :]),
                                      k == 0, k == KT - 1)
                mm.then_inc(chunk_done, 1)

            def some(c, t, tiles, operand, ready=None):
                begin(c, t, 2)
                for k in tiles:
                    if ready:
                        pe.wait_ge(ready[0], ready[1] + k + 1)
                    for m in range(2):
                        mm = products(ps[:, (t + m) % 4, :], w_at(c, k * PAIR + m * P, P), operand(k), k == 0, k == KT - 1)
                if tiles[-1] == KT - 1:
                    mm.then_inc(chunk_done, 1)

            def stat(n):
                pe.wait_ge(ss_ready, 9 * n)
                pe.matmul(ps[:, 4, :], ones, ssum[:, :], start=True, stop=True).then_inc(stat_done, 1)

            def linear(name, x, ready=None, n=None, before=None, width=S):
                c0, t0 = C0[name], T0[name]
                n = n or dict((a, b) for a, b, _ in PHASES)[name]
                plain(c0, t0, x, ready, width=width)
                if before is not None:
                    stat(before)
                plain(c0 + 1, t0 + 2, x, width=width)

                def step(it):
                    plain(c0, t0, x, None, it * 2, it * 4, width)
                    plain(c0 + 1, t0 + 2, x, None, it * 2, it * 4, width)

                if n > 2:
                    walk(pe, n // 2, step, 1)

            def down(name):
                c0, t0, f0 = C0[name], T0[name], FT * UPS["up" + name[4:]]

                def pair(j, it):
                    t = t0 + 2 * j
                    for i in range(3):
                        c = c0 + 3 * j + i
                        pe.wait_ge(lo_ready, it * 6 + (c + 1))
                        if i == 0:
                            pe.wait_ge(acc_evac, it * 4 + (t - 2))
                        for k in range(8 * i, min(8 * i + 8, FT)):
                            if j == 0:
                                pe.wait_ge(f_ready, past(f0 + k + 1))
                            for m in range(2):
                                mm = products(ps[:, (t + m) % 4, :], w_at(c, (k % 8) * PAIR + m * P, P),
                                              (f_hi[:, k, :], f_lo[:, k, :]), k == 0, k == FT - 1)
                        mm.then_inc(chunk_done, 1)

                def step(it):
                    pair(0, it)
                    pair(1, it)

                walk(pe, 2, step)

            x = (x_hi, x_lo)
            pe.wait_ge(par_landed, 32)
            pe.wait_ge(x_ss, KT - 1)
            pe.matmul(ps[:, 4, :], ones, ssum[:, :], start=True, stop=True).then_inc(stat_done, 1)

            linear("qf", x, (x_ready, 0))
            for j in range(2):
                c, t = C0["v"] + j, T0["v"] + 2 * j
                begin(c, t, 2)
                for b in range(BLK):
                    for k in range(KT):
                        mm = products(ps[:, (t + b // 2) % 4, (b % 2) * PAIR:(b % 2 + 1) * PAIR],
                                      (x_hi[:, k, b * P:(b + 1) * P], x_lo[:, k, b * P:(b + 1) * P]),
                                      w_at(c, k * PAIR, PAIR), k == 0, k == KT - 1)
                mm.then_inc(chunk_done, 1)

            def ls_heads(it):
                plain(C0["gq"], T0["gq"], x, None, it * 2, it * 4)
                pe.wait_ge(acc_evac, it * 4 + (T0["gq"] + 2))
                for level in range(LEVELS):
                    w = 1 << (level - 1) if level else 0
                    for e in range(2):
                        bank = 4 + 2 * e + level % 2
                        if level < 2:
                            pe.wait_ge(ls_ops, it * 18 + (e + 1))
                        else:
                            pe.wait_ge(ls_ops, it * 18 + (2 * (level - 1) + e + 1))
                            pe.wait_ge(ls_qops, it * 16 + (2 * (level - 2) + e + 1))
                            pe.wait_ge(ls_diag, it * 16 + (2 * (level - 2) + e + 1))
                        if level == 0:
                            pe.wait_ge(ls_q, it * 2 + e + 1)
                        if 1 <= level < 8:
                            pe.wait_ge(ls_kc, it * 28 + (4 * (level - 1) + 2 * (e + 1)))
                        qq = QQ[e][:, :, :]
                        if level < 8:
                            for b in range(BLK):
                                if level == 0:
                                    lhs, rhs = A[e][:, 3, b * P:(b + 1) * P], A[e][:, 2, b * P:(b + 1) * P]
                                else:
                                    dims = [[2 * w, P // (2 * w)], [S + w, 2], [1, w]]
                                    lhs, rhs = KC[e][:, b * P:(b + 1) * P], free(qq, b * P, dims)
                                mm = pe.matmul(ps[:, bank, b * P:(b + 1) * P], lhs, rhs, start=True, stop=True)
                        elif level == 8:
                            for b in range(BLK):
                                q = b + 1 if b % 2 == 0 else b - 1
                                mm = pe.matmul(ps[:, bank, b * P:(b + 1) * P], KK[e][:, 1 - b % 2, b * P:(b + 1) * P],
                                               QQ[e][:, 1 - b % 2, q * P:(q + 1) * P], start=True, stop=True)
                        else:
                            for b in range(BLK):
                                half = b // 2
                                mm = pe.matmul(ps[:, bank if half == 0 else e, (b % 2) * 256:(b % 2 + 1) * 256],
                                               KK[e][:, 1 - half, b * P:(b + 1) * P],
                                               QQ[e][:, 1 - half, (1 - half) * 256:(2 - half) * 256], start=True, stop=True)
                        mm.then_inc(ls_scores, 1)
                for e in range(2):
                    pe.wait_ge(ls_diag, it * 16 + (14 + e + 1))
                    pe.wait_ge(ls_cross, it * 6 + (2 + 2 * (e + 1)))
                    pe.wait_ge(ls_v, it * 2 + e + 1)
                    for b in range(BLK):
                        mm = pe.matmul(ps[:, 5 + 2 * e, :], QQ[e][:, 0, b * P:(b + 1) * P], A[e][:, b, :], start=(b == 0), stop=(b == BLK - 1))
                    mm.then_inc(ls_o, 1)
                for e in range(2):
                    pe.wait_ge(ls_sq, it * 2 + e + 1)
                    pe.matmul(ps[:, 4 + 2 * e, :], ones, KK[e][:, 0, :], start=True, stop=True).then_inc(ls_ss, 1)
                plain(C0["gq"] + 1, T0["gq"] + 2, x, None, it * 2, it * 4)

            walk(pe, 2, ls_heads)

            c, t = C0["kv_a"], T0["kv_a"]
            begin(c, t, 2)
            for k in range(KT):
                products(ps[:, t % 4, :], w_at(c, k * PAIR, P), (x_hi[:, k, :], x_lo[:, k, :]), k == 0, k == KT - 1)
            for b in range(BLK):
                for k in range(KT):
                    mm = products(ps[:, (t + 1) % 4, b * P:(b + 1) * P], (x_hi[:, k, b * P:(b + 1) * P], x_lo[:, k, b * P:(b + 1) * P]),
                                  w_at(c, k * PAIR + P, P), k == 0, k == KT - 1)
            mm.then_inc(chunk_done, 1)

            def swap(i, tile, src):
                pe.wait_ge(acc_evac, tile + 1)
                pe.wait_ge(const_landed, 32)
                if i >= 4:
                    pe.wait_ge(rot_step, 3 * (i - 4) + 1)
                pe.matmul(ps[:, 4 + i % 4, :], perm1[:, :], src, start=True, stop=True).then_inc(perm_done, 1)

            swap(0, T0["kv_a"], k_pad[:, P:P + S])
            for i in range(WIN_TILES):
                swap(1 + i, T0["gq"] + 4 * (i // 2) + 2 + i % 2, qa[:, i, :])
            pe.wait_ge(acc_evac, T0["merge"])
            pe.wait_ge(k_ready, 1)

            def scores(j, p, first=False):
                half = slice(64 * p, 64 * p + 64)
                pe.wait_ge(wa_q, j + 1)
                if not first:
                    pe.wait_ge(wa_s, past(j * 2 + p))
                for n in range(BLK):
                    mm = products(ps[:, n, 0:384], (q_hi[half, n * P:(n + 1) * P], q_lo[half, n * P:(n + 1) * P]),
                                  (k_hi[half, n * P:n * P + 384], k_lo[half, n * P:n * P + 384]), True, True)
                mm.then_inc(wa_scores, 1)

            def turn(j, p):
                pe.wait_ge(wa_p, j * 2 + (p + 1))
                for b in range(BLK):
                    to, to_col = TURNED_AT[b]
                    for i, n in enumerate(TURNED_OF[b]):
                        r = b - n + 1
                        mm = pe.transpose(ps[:, 4 + to, to_col + i * P:to_col + (i + 1) * P], w_s[p][:, n, r * P:(r + 1) * P], ident)
                mm.then_inc(wa_turned, 1)

            def values(j, p):
                pe.wait_ge(wa_pT, past(j * 2 + (p + 1)))
                pe.wait_ge(att_ready, past(j * 2 + p))
                for b in (0, 3, 1, 2):
                    at_bank, at_col = TURNED_AT[b]
                    n0, width = TURNED_OF[b][0] * P, len(TURNED_OF[b]) * P
                    cols = slice(at_col, at_col + width)
                    mm = products(ps[:, 7, n0:n0 + width], (va_hi[:, b, :], va_lo[:, b, :]),
                                  (wT_hi[:, at_bank, cols], wT_lo[:, at_bank, cols]), b == 0, b == 2)
                mm.then_inc(wa_o, 1)

            def wa_tile(j, last=False):
                for p in range(2):
                    turn(j, p)
                    if not last:
                        scores(j + 1, p)
                    else:
                        pe.wait_ge(wa_s, past(2 * WIN_TILES))
                        some(C0["merge"], T0["merge"], range(3 * p, 3 * p + 3), lambda k: (x[0][:, k, :], x[1][:, k, :]))
                    values(j, p)

            scores(0, 0, first=True)
            scores(0, 1)
            pe.wait_ge(rot_step, 3 * 5)
            walk(pe, WIN_TILES - 1, wa_tile)
            wa_tile(WIN_TILES - 1, last=True)

            c0, t0 = C0["merge"], T0["merge"]
            some(c0, t0, range(6, KT), lambda k: (x[0][:, k, :], x[1][:, k, :]))

            def merge(it, first=False):
                for j in range(2):
                    c, t = c0 + 3 * j, t0 + 8 * j
                    if not (first and j == 0):
                        plain(c, t, x, None, it * 6, it * 16)
                    plain(c + 1, t + 2, x, None, it * 6, it * 16)
                    for half, src in enumerate(((rec_hi, rec_lo), (att_hi, att_lo))):
                        begin(c + 2, t + 4 + 2 * half, 2, it * 6, it * 16)
                        if first and j == 0:
                            pe.wait_ge(*((rec_ready, past(HEADS)), (att_ready, past(2 * WIN_TILES)))[half])
                        for k in range(4):
                            for m in range(2):
                                mm = products(ps[:, (t + 4 + 2 * half + m) % 4, :], w_at(c + 2, (4 * half + k) * PAIR + m * P, P),
                                              (src[0][:, k, :], src[1][:, k, :]), k == 0, k == 3)
                        if half == 1:
                            mm.then_inc(chunk_done, 1)

            merge(0, first=True)
            merge(1)
            pe.wait_ge(mem_sq_ready, 2 * KT - 1)
            pe.matmul(ps[:, 5, 0:MEM], ones, ssum[:, 0:MEM], start=True, stop=True).then_inc(mem_stat, 1)
            linear("mix_out", (mrg_hi, mrg_lo), (mrg_ready, 1))

            linear("mem_k", (mem_hi, mem_lo), (mem_ready, 0), before=1, width=MEM)
            c1, t1 = C0["mem_v"], T0["mem_v"]

            def mem_values(it):
                for j in range(2):
                    c, t = c1 + j, t1 + 2 * j
                    begin(c, t, 2, it * 2, it * 4)
                    for e in range(2):
                        for k in range(KT):
                            mm = products(ps[:, (t + e) % 4, 0:PAIR], (mem_hi[:, k, e * P:(e + 1) * P], mem_lo(k)[:, e * P:(e + 1) * P]),
                                          w_at(c, k * PAIR, PAIR), k == 0, k == KT - 1)
                    mm.then_inc(chunk_done, 1)

            walk(pe, 2, mem_values)
            c2, t2 = C0["mem_q"], T0["mem_q"]
            pe.wait_ge(x_ready, XR0["mix_out"] + KT)

            def queries(u):
                plain(c2 + u, t2 + 2 * u, x)

            def scores(u):
                pe.wait_ge(qm_ready, u + 1)
                if u:
                    pe.wait_ge(ma_exp, u)
                for n in range(BLK):
                    for d in range(2):
                        q = qm_hi[u % 2][:, d, n * P:(n + 1) * P], qm_lo[u % 2][:, d, n * P:(n + 1) * P]
                        mm = products(ps[:, 4 + n // 2, (n % 2) * MEM:(n % 2 + 1) * MEM], q, (km_hi[:, 2 * u + d, :], km_lo[:, 2 * u + d, :]),
                                      d == 0, d == 1)
                mm.then_inc(ma_scores, 1)

            def turn(u):
                pe.wait_ge(ma_p, u + 1)
                if u:
                    pe.wait_ge(mo_ready, past(2 * u))
                for mb in range(2):
                    for n in range(BLK):
                        mm = pe.transpose(ps[:, 6 + mb, n * P:(n + 1) * P], m_p[u % 2][:, n, mb * P:(mb + 1) * P], ident)
                mm.then_inc(ma_turned, 1)

            def values(u):
                pe.wait_ge(ma_pT, u + 1)
                for d in range(2):
                    at_col = u * MEM_D + d * P
                    for mb in range(2):
                        mm = products(ps[:, 6 + d, :], (vm_hi[:, mb, at_col:at_col + P], vm_lo[:, mb, at_col:at_col + P]),
                                      (pm_hi[:, mb, :], pm_lo[:, mb, :]), mb == 0, mb == 1)
                mm.then_inc(ma_o, 1)

            c3, t3 = C0["mem_o"], T0["mem_o"]

            def first_out(i, tiles):
                some(c3 + i, t3 + 2 * i, tiles, lambda k: (mo_hi[:, k, :], mo_lo[:, k, :]), (mo_ready, past(0)))

            def out_step(it):
                plain(c3, t3, (mo_hi, mo_lo), None, it * 2, it * 4)
                plain(c3 + 1, t3 + 2, (mo_hi, mo_lo), None, it * 2, it * 4)

            queries(0)
            queries(1)
            scores(0)
            for u in range(MEM_HEADS):
                if u + 2 < MEM_HEADS:
                    queries(u + 2)
                else:
                    first_out(u + 2 - MEM_HEADS, range(0, 4))
                turn(u)
                if u + 1 < MEM_HEADS:
                    scores(u + 1)
                else:
                    first_out(0, range(4, 6))
                values(u)
            first_out(1, range(4, 6))
            first_out(0, range(6, KT))
            first_out(1, range(6, KT))
            walk(pe, 2, out_step, 1)
            linear("up0", x, (x_ready, XR0["mem_o"]), before=2)
            down("down0")
            stat(3)
            linear("up1", x, (x_ready, XR0["renorm"]), before=4)
            down("down1")

            for j in range(5):
                plain(C0["a_in"] + j, T0["a_in"] + 2 * j, x, (x_ready, XR0["down1"]) if j == 0 else None)
                if j == 0:
                    stat(5)
                if j == 3:
                    for i in range(5):
                        pe.wait_ge(lat_sq, i + 1)
                        mm = pe.matmul(ps[:, 5 if i < 3 else 6, :], ones, lat_q2[:, i, :], start=(i in (0, 3)), stop=(i in (2, 4)))
                        if i in (2, 4):
                            mm.then_inc(lat_stat, 1)
            c, t = C0["mla"], T0["mla"]

            def mla_out(i):
                chunk = c + sum(i > m for m in MLA_LAST)
                begin(chunk, t + i, 1)
                bank = (t + i) % 4
                if i < 8:
                    if i == 0:
                        pe.wait_ge(lat_ready, 5)
                    for k in range(3):
                        mm = products(ps[0:MLA_QK, bank, :], w_at(chunk, (i % 7) * 3 * MLA_QK + k * MLA_QK, MLA_QK),
                                      (lat_hi[:, k, :], lat_lo[:, k, :]), k == 0, k == 2)
                elif i < 12:
                    b = i - 8
                    for k in range(2):
                        mm = products(ps[:, bank, :], (lat_hi[:, 3 + k, b * P:(b + 1) * P], lat_lo[:, 3 + k, b * P:(b + 1) * P]),
                                      w_at(chunk, 3 * MLA_QK + k * S, S), k == 0, k == 1)
                elif i < 16:
                    for k in range(2):
                        mm = products(ps[:, bank, :], w_at(chunk, k * S + (i - 12) * P, P), (lat_hi[:, 3 + k, :], lat_lo[:, 3 + k, :]),
                                      k == 0, k == 1)
                else:
                    pe.wait_ge(pl_ready, 4)
                    mm = products(ps[:, bank, :], w_at(chunk, 2 * S + (i - 16) * P, P), (pl_hi[:, i - 16, :], pl_lo[:, i - 16, :]), True, True)
                mm.then_inc(chunk_done if i in MLA_LAST else mla_tile, 1)

            def head_sums(w):
                for i in range(MLA_HEADS):
                    pe.wait_ge(hd_sq, 8 * w + i + 1)
                    pe.matmul(ps[0:8, 4 + w, :], sel16[0:MLA_QK, 15 - i:23 - i], hd_q[i % 2][0:MLA_QK, :],
                              start=(i == 0), stop=(i == MLA_HEADS - 1)).then_inc(hd_stat, 1)

            def head_norms(w, src):
                def heads(it):
                    for e in range(2):
                        n = it * 2 + (8 * w + e + 1)
                        pe.wait_ge(sp_ready, n)
                        out_ap = ps[0:MLA_QK, 4 + e, :]
                        pe.matmul(out_ap, ones_r[0:8, :], sp_hi[e][0:8, :], start=True, stop=False)
                        pe.matmul(out_ap, ones_r[0:8, :], sp_lo[e][0:8, :], start=False, stop=True).then_inc(la_spread, 1)
                    for e in range(2):
                        n = it * 2 + (8 * w + e + 1)
                        pe.wait_ge(la_norm, n)
                        pe.wait_ge(la_sin, past(it * 2 + 8 * w))
                        pe.matmul(ps[0:MLA_QK, 6 + e, :], perm2[0:MLA_QK, 0:MLA_QK], row(src, it * 2 + e)[0:MLA_QK],
                                  start=True, stop=True).then_inc(la_swap, 1)

                walk(pe, MLA_HEADS // 2, heads)

            for i in range(16):
                mla_out(i)
            pe.wait_ge(rope2_landed, 64)
            head_sums(0)
            head_sums(1)
            for i in range(16, 20):
                mla_out(i)
            head_norms(0, q_h)
            head_norms(1, k_h)
            pe.wait_ge(la_rot, 16)
            pe.wait_ge(acc_evac, T0["a_out"])

            def scores(v, e, reused=True):
                pe.wait_ge(la_q, v + 1)
                if reused:
                    pe.wait_ge(la_pT, v - 1)
                for n in range(BLK):
                    b, at_col = CAUSAL_AT[n + 1]
                    w = (n + 1) * P
                    mm = pe.matmul(ps[:, 3 * e + b, at_col:at_col + w], q_c[e][0:MLA_QK, n * P:(n + 1) * P], row(k_h, v)[0:MLA_QK, 0:w],
                                   start=True, stop=True)
                mm.then_inc(la_scores, 1)

            def turn(v, e):
                pe.wait_ge(la_p, v + 1)
                for kb in range(BLK):
                    to, to_col = CAUSAL_AT[BLK - kb]
                    for n in range(kb, BLK):
                        b, at_col = CAUSAL_AT[n + 1]
                        mm = pe.transpose(ps[:, 3 * e + to, to_col + (n - kb) * P:to_col + (n - kb + 1) * P],
                                          l_p[e][:, b, at_col + kb * P:at_col + (kb + 1) * P], ident)
                mm.then_inc(la_turned, 1)

            def values(v, e, reused=True):
                pe.wait_ge(la_pT, v + 1)
                pe.wait_ge(la_v, v + 1)
                if reused:
                    pe.wait_ge(cat1_ready, past(v - 1))
                for kb in range(BLK):
                    b, at_col = CAUSAL_AT[BLK - kb]
                    mm = pe.matmul(ps[64 * e:64 * e + 64, 6 + e, kb * P:S], vl_st[e][:, kb, :], l_pT[e][:, b, at_col:at_col + (BLK - kb) * P],
                                   start=(kb == 0), stop=(kb == BLK - 1))
                mm.then_inc(la_o, 1)

            def mla_heads(it, first=False):
                for e in range(2):
                    turn(it * 2 + e, e)
                    if not (first and e == 0):
                        values(it * 2 + (e - 1), 1 - e, not first)
                    scores(it * 2 + (e + 2), e)

            scores(0, 0, False)
            scores(1, 1, False)
            mla_heads(0, first=True)
            walk(pe, MLA_HEADS // 2 - 1, mla_heads, 1)

            def cat(k):
                return cat_hi[k // 4][:, k % 4, :], cat_lo[k // 4][:, k % 4, :]

            c, t, v = C0["a_out"], T0["a_out"], MLA_HEADS - 2
            turn(v, 0)
            values(v - 1, 1)
            pe.wait_ge(cat0_ready, 4)
            pe.wait_ge(la_pT, v + 1)
            some(c, t, range(0, 4), cat)
            turn(v + 1, 1)
            values(v, 0)
            pe.wait_ge(cat1_ready, past(v))
            some(c, t, range(4, 7), cat)
            values(v + 1, 1)
            some(c + 1, t + 2, range(0, 2), cat)
            pe.wait_ge(cat1_ready, past(MLA_HEADS))
            some(c, t, range(7, KT), cat)
            some(c + 1, t + 2, range(2, KT), cat)
            for i in range(2, 4):
                some(c + i, t + 2 * i, range(KT), cat)
            linear("up2", x, (x_ready, XR0["a_out"]), before=6)
            down("down2")
            linear("up3", x, (x_ready, XR0["down2"]), before=7)
            down("down3")

            c3, t3 = C0["c_in"], T0["c_in"]

            def conv_mix(it):
                for k in range(6):
                    plain(c3 + k, t3 + 2 * k, x, (x_ready, XR0["down3"]) if k == 0 else None, it * 6, it * 12)

            for k in range(6):
                plain(c3 + k, t3 + 2 * k, x, (x_ready, XR0["down3"]) if k == 0 else None)
                if k == 0:
                    stat(8)
            walk(pe, 2, conv_mix, 1)
            linear("c_out", (cc_hi, cc_lo), (cc_ready, 0))
            linear("up4", x, (x_ready, XR0["c_out"]), before=9)
            down("down4")


def _cols(w, cols):
    w = w[:, cols]
    return w.reshape(w.shape[0] // P, P, w.shape[1]).transpose(1, 0, 2)


def _pairs(w):
    return [_cols(w, slice(PAIR * j, PAIR * (j + 1))).reshape(P, CW) for j in range(w.shape[1] // PAIR)]


def _up(w_gate, w_up):
    return [c for g, u in zip(_pairs(w_gate), _pairs(w_up)) for c in (g, u)]


def _padded(a):
    out = np.zeros((P, CW), np.float32)
    out[:, :a.shape[1]] = a
    return out


def _down(w):
    out = []
    for j in range(D // PAIR):
        t = _cols(w, slice(PAIR * j, PAIR * (j + 1)))
        out += [_padded(t[:, 8 * i:8 * i + 8].reshape(P, -1)) for i in range(3)]
    return out


def _columns(v):
    return v.reshape(-1, P).T


def _stream(a):
    w = a["w_in"][0]
    kw = HEADS * HK
    at = np.cumsum([0, kw, kw, kw, kw, kw, WIN_HEADS * WIN_D, WIN_KV * WIN_D, WIN_KV * WIN_D, D, D])
    q_r, fz_f, fz_b, i_r, g_r, q_a, k_a, v_a, gate_r, gate_a = [w[:, at[i]:at[i + 1]] for i in range(10)]
    order = np.concatenate([np.arange(WIN_D) + WIN_D * hd for j in range(WIN_TILES) for hd in (j, j + WIN_TILES)])
    f_heads = np.concatenate([x[:, HK * i:HK * (i + 1)] for i in range(HEADS) for x in (fz_b, fz_f)], axis=1)
    out = _pairs(q_r) + _pairs(f_heads) + _pairs(i_r)
    for c in zip(_pairs(g_r), _pairs(q_a[:, order])):
        out += c
    out += _pairs(np.concatenate([k_a, v_a], axis=1))
    branches = _pairs(np.concatenate([a["w_br_rec"][0], a["w_br_att"][0][order]], axis=0))
    for c in zip(_pairs(gate_r), _pairs(gate_a), branches):
        out += c
    out += _pairs(a["w_mix_out"][0])
    out += _pairs(a["w_mem_kv"][0]) + _pairs(a["w_mem_q"][0]) + _pairs(a["w_mem_o"][0])
    out += _up(a["w_up"][0][:, FF:], a["w_up"][0][:, :FF]) + _down(a["w_down"][0])
    for layer in range(2):
        out += _up(a["ffn1_w_gate_2"][layer], a["ffn1_w_up_2"][layer]) + _down(a["ffn1_w_down_2"][layer])
        if layer == 0:
            wi = a["a_w_in_2"][0]
            cut = POOL + Q_LORA + KV_LORA
            rope = np.zeros((D, P), np.float32)
            rope[:, MLA_NOPE:MLA_QK] = wi[:, cut:]
            out += _pairs(np.concatenate([wi[:, POOL:cut], rope, wi[:, :POOL]], axis=1))
            wq = _cols(a["a_w_q_up_2"][0], slice(None)).reshape(P, 3, MLA_HEADS, MLA_QK).transpose(0, 2, 1, 3)
            wkv = _cols(a["a_w_kv_up_2"][0], slice(None)).reshape(P, 2, MLA_HEADS, MLA_NOPE + MLA_V)
            pool = a["a_w_pool_2"][0].transpose(1, 0, 2).reshape(P, POOL)
            out.append(_padded(wq[:, :7].reshape(P, -1)))
            out.append(_padded(np.concatenate([wq[:, 7].reshape(P, -1), wkv[..., MLA_NOPE:].reshape(P, -1)], axis=1)))
            out.append(_padded(np.concatenate([wkv[..., :MLA_NOPE].reshape(P, -1), pool], axis=1)))
            out += _pairs(a["a_w_out_2"][0])
        else:
            wi = a["c_w_in_2"][0]
            for c in zip(_pairs(wi[:, :D]), _pairs(wi[:, D:2 * D]), _pairs(wi[:, 2 * D:])):
                out += c
            out += _pairs(a["c_w_out_2"][0])
        out += _up(a["ffn2_w_gate_2"][layer], a["ffn2_w_up_2"][layer]) + _down(a["ffn2_w_down_2"][layer])
    assert len(out) == CHUNKS
    return np.stack(out)


def _params(a):
    par = np.zeros((P, NPAR), np.float32)

    def put(name, cols):
        par[:cols.shape[0], COL[name]:COL[name] + cols.shape[1]] = cols

    for name in ("norm_mix", "norm_mem", "norm_mem_kv", "norm_ffn", "hg_norm", "conv_b"):
        put(name, _columns(a[name][0]))
    put("final_norm", _columns(a["final_norm"]))
    for i in range(2):
        put(f"ffn1_{i}", _columns(a["ffn1_norm_2"][i]))
        put(f"mix_{i}", _columns(a["mix_norm_2"][i]))
        put(f"ffn2_{i}", _columns(a["ffn2_norm_2"][i]))
    for j in range(3):
        put(f"conv_w{j}", _columns(a["conv_w"][0, j]))
        put(f"cc_w{j}", _columns(a["c_conv_w_2"][0, j]))
    put("q_a_norm", _columns(a["a_q_a_norm_2"][0]))
    put("kv_a_norm", _columns(a["a_kv_a_norm_2"][0]))
    put("q_head", a["a_q_head_norm_2"][0][:, None])
    put("k_head", a["a_k_head_norm_2"][0][:, None])
    put("pool_scale", _columns(a["a_pool_scale_2"][0]))
    put("sink", np.broadcast_to(a["attn_sink"][0], (P, WIN_HEADS)))
    for j in range(2):
        lb = a["lower_bounds"][:, j].reshape(2, HEADS, HK)
        put(f"lb{j}", np.stack([lb[1], lb[0]], axis=1).reshape(2 * HEADS, HK).T)
    rot = WIN_D // 4
    freq = np.float32(1.0) / (np.float32(500000.0) ** (np.arange(0, rot, 2, dtype=np.float32) / np.float32(rot)))
    d = np.arange(P) % WIN_D
    put("inv_freq", np.where(d < rot, freq[d % (rot // 2)], 0.0).astype(np.float32)[:, None])
    put("rot_sign", np.where(d < rot // 2, -1.0, 1.0).astype(np.float32)[:, None])
    put("eps", np.full((P, 1), EPS, np.float32))
    return par


def _constants():
    c = np.zeros((P, NCONST), np.float32)
    i, j = np.arange(P)[:, None], np.arange(P)[None, :]

    def put(name, a):
        c[:a.shape[0], CCOL[name]:CCOL[name] + a.shape[1]] = a

    put("ident", np.eye(P))
    put("ones", np.ones((P, P)))
    band = np.zeros((P, BLK, 384))
    key = np.arange(384)[None, :] - P
    for n in range(BLK):
        ok = (np.abs(i - key) <= P) & (key + n * P >= 0) & (key + n * P < S)
        band[:, n] = np.where(ok, 0.0, NEG)
    put("band", band.reshape(P, -1))
    half = WIN_D // 8
    d = np.arange(P) % WIN_D
    partner = np.where(d < half, np.arange(P) + half, np.where(d < 2 * half, np.arange(P) - half, -1))
    put("perm1", (i == partner[None, :]).astype(np.float32))
    half2 = MLA_ROPE // 2
    f = np.arange(P)
    partner2 = np.where((f >= MLA_NOPE) & (f < MLA_NOPE + half2), f + half2,
                        np.where((f >= MLA_NOPE + half2) & (f < MLA_QK), f - half2, -1))
    put("perm2", (i == partner2[None, :]).astype(np.float32))
    put("causal", np.where(j <= i, 0.0, NEG))
    sel = np.zeros((P, 32))
    sel[:, 15] = 1.0
    put("sel", sel)
    freq = np.float32(10000.0) ** (-np.arange(0, MLA_ROPE, 2, dtype=np.float32) / np.float32(MLA_ROPE))
    ang = np.arange(S, dtype=np.float32)[:, None] * freq[None, :]
    cos, sin = np.cos(ang).T, np.sin(ang).T
    rope_c, rope_s = np.ones((P, S)), np.zeros((P, S))
    rope_c[MLA_NOPE:MLA_QK] = np.concatenate([cos, cos])
    rope_s[MLA_NOPE:MLA_QK] = np.concatenate([-sin, sin])
    put("rope_c", rope_c)
    put("rope_s", rope_s)
    count = np.stack([1.0 / np.minimum(np.arange(1, S + 1), 2 << g) for g in range(4)])
    put("levels", _level_masks().reshape(P, -1))
    put("count", np.broadcast_to(count.reshape(1, -1), (P, 4 * S)))
    return c


def _level_masks():
    s, t = np.arange(P)[:, None, None], np.arange(P)[None, None, :]
    lv = np.arange(7)[None, :, None]
    return (((s >> lv) != (t >> lv)) & ((s >> (lv + 1)) == (t >> (lv + 1)))).astype(np.float32)


def kernel(**inputs):
    from concourse import bacc
    from concourse.bass_utils import run_bass_kernel_spmd

    a = {k: np.asarray(v) for k, v in inputs.items()}
    arrays = {
        "stream": _stream(a),
        "x": np.ascontiguousarray(a["x"][0].T.reshape(KT, P, S).transpose(1, 0, 2)),
        "mem": np.ascontiguousarray(a["mem"][0].T.reshape(KT, P, MEM).transpose(1, 0, 2)),
        "positions": np.ascontiguousarray(np.broadcast_to(a["positions"].reshape(1, S), (P, S))),
        "params": _params(a),
        "constants": _constants(),
    }
    nc = bacc.Bacc("TRN2", target_bir_lowering=False, num_devices=1)
    args = [nc.dram_tensor(f"in_{k}", v.shape, mybir.dt.from_np(v.dtype), kind="ExternalInput").ap() for k, v in arrays.items()]
    out = nc.dram_tensor("out_x", (P, KT, S), F32, kind="ExternalOutput").ap()
    build(nc, *args, out)
    result = run_bass_kernel_spmd(nc, [{f"in_{k}": v for k, v in arrays.items()}], core_ids=[0])
    y = result.results[0]["out_x"]
    return np.ascontiguousarray(y.transpose(1, 0, 2).reshape(D, S).T).reshape(1, S, D)
```
